# Optimizing a Trainium2 kernel written in Bass

```python
import math
import jax, jax.numpy as jnp
from jax import lax
import numpy as np
import jax
import jax.numpy as jnp

D_MODEL = 2048
BATCH = 1
SEQ = 256
DEPTH = 1

CHUNK = 64
N_MIXERS = 2
EPS = 1e-6

GLA_HEADS = 4
GLA_KEY_WIDTH = D_MODEL // 2
GLA_VAL_WIDTH = D_MODEL
GLA_DK = GLA_KEY_WIDTH // GLA_HEADS
GLA_DV = GLA_VAL_WIDTH // GLA_HEADS
GLA_GATE_RANK = 16
GLA_GATE_TEMP = 16.0
GLA_IN_WIDTH = 2 * GLA_KEY_WIDTH + 2 * GLA_VAL_WIDTH + GLA_GATE_RANK

S5_WIDTH = D_MODEL // 2
S5_GROUP = 16
S5_GROUPS = S5_WIDTH // S5_GROUP
S5_STATE = 64
S5_DT_MIN = 1e-3
S5_DT_MAX = 1e-1
S5_EIG_CLIP = -1e-4

MLP_HIDDEN = 4 * D_MODEL


def _rmsnorm(x, g):
    xf = x.astype(jnp.float32)
    y = xf * lax.rsqrt(jnp.mean(xf * xf, axis=-1, keepdims=True) + EPS)
    return (y * g.astype(jnp.float32)).astype(x.dtype)

def _gla_mixer(h, w_in, w_gate_up, b_gate, o_norm, w_out):
    bsz, seq, _ = h.shape
    nc = seq // CHUNK
    proj = h @ w_in
    q, k, v, r, g_low = jnp.split(
        proj,
        [GLA_KEY_WIDTH, 2 * GLA_KEY_WIDTH, 2 * GLA_KEY_WIDTH + GLA_VAL_WIDTH,
         2 * GLA_KEY_WIDTH + 2 * GLA_VAL_WIDTH], axis=-1)
    log_a = jax.nn.log_sigmoid((g_low @ w_gate_up + b_gate).astype(jnp.float32)) / GLA_GATE_TEMP

    def to_chunks(t, dh):
        return t.reshape(bsz, nc, CHUNK, GLA_HEADS, dh).transpose(1, 0, 3, 2, 4).astype(jnp.float32)

    qc = to_chunks(q, GLA_DK) * (GLA_DK ** -0.5)
    kc = to_chunks(k, GLA_DK)
    vc = to_chunks(v, GLA_DV)
    ac = to_chunks(log_a, GLA_DK)
    cum = jnp.cumsum(ac, axis=3)
    total = cum[:, :, :, -1:, :]
    k_dec = kc * jnp.exp(total - cum)
    chunk_decay = jnp.exp(total[:, :, :, 0, :])

    def step(state, xs):
        q_c, k_c, v_c, d_c = xs
        state = d_c[..., None] * state + jnp.einsum('bhck,bhcv->bhkv', k_c, v_c)
        return state, jnp.einsum('bhck,bhkv->bhcv', q_c, state)

    s0 = jnp.zeros((bsz, GLA_HEADS, GLA_DK, GLA_DV), jnp.float32)
    _, o = lax.scan(step, s0, (qc, k_dec, vc, chunk_decay))
    o = o * lax.rsqrt(jnp.mean(o * o, axis=-1, keepdims=True) + EPS) * o_norm.astype(jnp.float32)
    o = o.transpose(1, 0, 3, 2, 4).reshape(bsz, seq, GLA_VAL_WIDTH).astype(h.dtype)
    return (o * jax.nn.silu(r)) @ w_out

def _s5_mixer(h, w_in, lam_re, lam_im, log_dt, b_re, b_im, c_re, c_im, d_skip, w_out):
    bsz, seq, _ = h.shape
    u = (h @ w_in).astype(jnp.float32)
    ug = u.reshape(bsz, seq, S5_GROUPS, S5_GROUP)
    lr = jnp.minimum(lam_re.astype(jnp.float32), S5_EIG_CLIP)
    li = lam_im.astype(jnp.float32)
    dt = jnp.exp(log_dt.astype(jnp.float32))[:, None]
    mag = jnp.exp(lr * dt)
    ang = li * dt
    ab_re = mag * jnp.cos(ang)
    ab_im = mag * jnp.sin(ang)
    den = lr * lr + li * li
    nr = ab_re - 1.0
    f_re = (nr * lr + ab_im * li) / den
    f_im = (ab_im * lr - nr * li) / den
    br = b_re.astype(jnp.float32)
    bi = b_im.astype(jnp.float32)
    bb_re = f_re[..., None] * br - f_im[..., None] * bi
    bb_im = f_re[..., None] * bi + f_im[..., None] * br
    bu_re = jnp.einsum('gnc,blgc->blgn', bb_re, ug)
    bu_im = jnp.einsum('gnc,blgc->blgn', bb_im, ug)
    a_re = jnp.broadcast_to(ab_re, bu_re.shape)
    a_im = jnp.broadcast_to(ab_im, bu_im.shape)

    def combine(e1, e2):
        a1r, a1i, b1r, b1i = e1
        a2r, a2i, b2r, b2i = e2
        return (a2r * a1r - a2i * a1i,
                a2r * a1i + a2i * a1r,
                a2r * b1r - a2i * b1i + b2r,
                a2r * b1i + a2i * b1r + b2i)

    _, _, x_re, x_im = lax.associative_scan(combine, (a_re, a_im, bu_re, bu_im), axis=1)
    y = (jnp.einsum('gcn,blgn->blgc', c_re.astype(jnp.float32), x_re)
         - jnp.einsum('gcn,blgn->blgc', c_im.astype(jnp.float32), x_im))
    y = y.reshape(bsz, seq, S5_WIDTH) + d_skip.astype(jnp.float32) * u
    y = jax.nn.gelu(y).astype(h.dtype)
    val, gate = jnp.split(y @ w_out, 2, axis=-1)
    return val * jax.nn.sigmoid(gate)

def _sq_relu_mlp(h, w_up, w_down):
    a = jax.nn.relu(h @ w_up)
    return (a * a) @ w_down

def first_inputs(seed: int = 0) -> dict:
    key = jax.random.key(seed)
    ks = jax.random.split(key, 24)
    n_gla = len(range(0, DEPTH, N_MIXERS))
    n_s5 = len(range(1, DEPTH, N_MIXERS))
    res_scale = (2 * DEPTH) ** -0.5

    def nrm(k, shape, scale):
        return jax.random.normal(k, shape, jnp.float32) * scale

    def gain(k, shape):
        return 1.0 + 0.02 * jax.random.normal(k, shape, jnp.float32)

    lam_im0 = math.pi * jnp.arange(S5_STATE, dtype=jnp.float32)
    return {
        'x': jax.random.normal(ks[0], (BATCH, SEQ, D_MODEL), jnp.float32),
        'gla_norm': gain(ks[1], (n_gla, D_MODEL)),
        'gla_w_in': nrm(ks[2], (n_gla, D_MODEL, GLA_IN_WIDTH), D_MODEL ** -0.5),
        'gla_w_gate_up': nrm(ks[3], (n_gla, GLA_GATE_RANK, GLA_KEY_WIDTH), GLA_GATE_RANK ** -0.5),
        'gla_b_gate': 1.0 + 0.1 * jax.random.normal(ks[4], (n_gla, GLA_KEY_WIDTH), jnp.float32),
        'gla_o_norm': gain(ks[5], (n_gla, GLA_DV)),
        'gla_w_out': nrm(ks[6], (n_gla, GLA_VAL_WIDTH, D_MODEL), GLA_VAL_WIDTH ** -0.5 * res_scale),
        's5_norm': gain(ks[7], (n_s5, D_MODEL)),
        's5_w_in': nrm(ks[8], (n_s5, D_MODEL, S5_WIDTH), D_MODEL ** -0.5),
        's5_lam_re': -0.5 + 0.01 * jax.random.normal(ks[9], (n_s5, S5_GROUPS, S5_STATE), jnp.float32),
        's5_lam_im': lam_im0 + 0.01 * jax.random.normal(ks[10], (n_s5, S5_GROUPS, S5_STATE), jnp.float32),
        's5_log_dt': jax.random.uniform(ks[11], (n_s5, S5_GROUPS), jnp.float32,
                                        minval=math.log(S5_DT_MIN), maxval=math.log(S5_DT_MAX)),
        's5_b_re': nrm(ks[12], (n_s5, S5_GROUPS, S5_STATE, S5_GROUP), (2 * S5_GROUP) ** -0.5),
        's5_b_im': nrm(ks[13], (n_s5, S5_GROUPS, S5_STATE, S5_GROUP), (2 * S5_GROUP) ** -0.5),
        's5_c_re': nrm(ks[14], (n_s5, S5_GROUPS, S5_GROUP, S5_STATE), (2 * S5_STATE) ** -0.5),
        's5_c_im': nrm(ks[15], (n_s5, S5_GROUPS, S5_GROUP, S5_STATE), (2 * S5_STATE) ** -0.5),
        's5_d': jax.random.normal(ks[16], (n_s5, S5_WIDTH), jnp.float32),
        's5_w_out': nrm(ks[17], (n_s5, S5_WIDTH, 2 * D_MODEL), S5_WIDTH ** -0.5 * res_scale),
        'mlp_norm': gain(ks[18], (DEPTH, D_MODEL)),
        'mlp_w_up': nrm(ks[19], (DEPTH, D_MODEL, MLP_HIDDEN), D_MODEL ** -0.5),
        'mlp_w_down': nrm(ks[20], (DEPTH, MLP_HIDDEN, D_MODEL), MLP_HIDDEN ** -0.5 * res_scale),
        'final_norm': gain(ks[21], (D_MODEL,)),
    }

def first_block(x, gla_norm, gla_w_in, gla_w_gate_up, gla_b_gate, gla_o_norm, gla_w_out,
              s5_norm, s5_w_in, s5_lam_re, s5_lam_im, s5_log_dt, s5_b_re, s5_b_im,
              s5_c_re, s5_c_im, s5_d, s5_w_out, mlp_norm, mlp_w_up, mlp_w_down, final_norm):
    h = x
    for i in range(DEPTH):
        j = i // N_MIXERS
        if i % N_MIXERS == 0:
            h = h + _gla_mixer(_rmsnorm(h, gla_norm[j]), gla_w_in[j], gla_w_gate_up[j],
                               gla_b_gate[j], gla_o_norm[j], gla_w_out[j])
        else:
            h = h + _s5_mixer(_rmsnorm(h, s5_norm[j]), s5_w_in[j], s5_lam_re[j], s5_lam_im[j],
                              s5_log_dt[j], s5_b_re[j], s5_b_im[j], s5_c_re[j], s5_c_im[j],
                              s5_d[j], s5_w_out[j])
        h = h + _sq_relu_mlp(_rmsnorm(h, mlp_norm[i]), mlp_w_up[i], mlp_w_down[i])
    return _rmsnorm(h, final_norm)


MEM_LEN = 256
DN_HEADS = 8
DN_DK = 128
DN_DV = 128
DN_CONV = 4
DN_CHUNK = 64
SWA_HEADS = 8
SWA_KV_HEADS = 2
SWA_DH = 64
WINDOW = 128
SB_HEADS = 4
SB_DH = 128
SB_BLOCK = 128
X_HEADS = 4
X_DH = 128
D_FF = 4096
FFN_CONV = 3
N_BRANCH = 3

DN_QK_WIDTH = DN_HEADS * DN_DK
DN_WIDTH = DN_HEADS * DN_DV
SWA_WIDTH = SWA_HEADS * SWA_DH
SWA_KV_WIDTH = SWA_KV_HEADS * SWA_DH
SB_WIDTH = SB_HEADS * SB_DH
X_WIDTH = X_HEADS * X_DH
IN_SIZES = (2 * DN_QK_WIDTH + DN_WIDTH, DN_WIDTH, DN_HEADS, DN_HEADS, SWA_WIDTH, 2 * SWA_KV_WIDTH, 3 * SB_WIDTH, N_BRANCH * D_MODEL)
IN_COLS = sum(IN_SIZES)


def rmsnorm(x, g):
    xf = x.astype(jnp.float32)
    y = xf * lax.rsqrt(jnp.mean(xf * xf, axis=-1, keepdims=True) + EPS)
    return (y * g.astype(jnp.float32)).astype(x.dtype)

def l2norm(x):
    xf = x.astype(jnp.float32)
    return xf * lax.rsqrt(jnp.sum(xf * xf, axis=-1, keepdims=True) + EPS)

def causal_dwconv(x, w):
    width = w.shape[0]
    seq = x.shape[1]
    xp = jnp.pad(x, ((0, 0), (width - 1, 0), (0, 0)))
    out = xp[:, 0:seq] * w[0]
    for i in range(1, width):
        out = out + xp[:, i:i + seq] * w[i]
    return out

def split_cols(t, sizes):
    offsets = [int(o) for o in np.cumsum(sizes)[:-1]]
    return jnp.split(t, offsets, axis=-1)

def alibi_slopes(n):
    return jnp.exp2(-8.0 * (jnp.arange(n, dtype=jnp.float32) + 1.0) / n)

def gated_delta_rule(q, k, v, g, beta):
    bsz, seq, heads, dk = q.shape
    dv = v.shape[-1]
    c = DN_CHUNK
    n = seq // c
    f32 = jnp.float32

    def chunks(t):
        return t.astype(f32).reshape(bsz, n, c, heads, -1).transpose(0, 1, 3, 2, 4)

    qc = chunks(q) * (dk ** -0.5)
    kc = chunks(k)
    vc = chunks(v)
    gc = jnp.cumsum(g.astype(f32).reshape(bsz, n, c, heads).transpose(0, 1, 3, 2), axis=-1)
    bc = beta.astype(f32).reshape(bsz, n, c, heads).transpose(0, 1, 3, 2)[..., None]
    causal = jnp.tril(jnp.ones((c, c), dtype=bool))
    strict = jnp.tril(jnp.ones((c, c), dtype=bool), -1)
    diff = gc[..., :, None] - gc[..., None, :]
    decay = jnp.where(causal, jnp.exp(jnp.where(causal, diff, 0.0)), 0.0)
    kb = kc * bc
    kk = jnp.einsum('bnhid,bnhjd->bnhij', kb, kc) * decay
    t_mat = jnp.eye(c, dtype=f32) + jnp.where(strict, kk, 0.0)
    u = lax.linalg.triangular_solve(t_mat, vc * bc, left_side=True, lower=True, unit_diagonal=True)
    w = lax.linalg.triangular_solve(t_mat, kb * jnp.exp(gc)[..., None], left_side=True, lower=True, unit_diagonal=True)
    qk = jnp.einsum('bnhid,bnhjd->bnhij', qc, kc) * decay
    q_dec = qc * jnp.exp(gc)[..., None]
    k_dec = kc * jnp.exp(gc[..., -1:] - gc)[..., None]
    g_last = jnp.exp(gc[..., -1])

    def step(state, xs):
        qk_n, qd_n, kd_n, u_n, w_n, gl_n = xs
        v_new = u_n - jnp.einsum('bhcd,bhde->bhce', w_n, state)
        o = jnp.einsum('bhcd,bhde->bhce', qd_n, state) + jnp.einsum('bhij,bhje->bhie', qk_n, v_new)
        state = state * gl_n[..., None, None] + jnp.einsum('bhcd,bhce->bhde', kd_n, v_new)
        return state, o

    xs = tuple(jnp.moveaxis(t, 1, 0) for t in (qk, q_dec, k_dec, u, w, g_last))
    state0 = jnp.zeros((bsz, heads, dk, dv), f32)
    _, o = lax.scan(step, state0, xs)
    return o.transpose(1, 0, 3, 2, 4).reshape(bsz, seq, heads, dv)

def sliding_window_gqa(q, k, v, sinks):
    bsz, seq = q.shape[:2]
    n = seq // WINDOW
    grp = SWA_HEADS // SWA_KV_HEADS
    qb = q.reshape(bsz, n, WINDOW, SWA_KV_HEADS, grp, SWA_DH)

    def band(t):
        tb = t.reshape(bsz, n, WINDOW, SWA_KV_HEADS, SWA_DH)
        prev = jnp.pad(tb, ((0, 0), (1, 0), (0, 0), (0, 0), (0, 0)))[:, :-1]
        return jnp.concatenate([prev, tb], axis=2)

    kb = band(k)
    vb = band(v)
    s = jnp.einsum('bnqhgd,bnkhd->bnhgqk', qb, kb).astype(jnp.float32) * (SWA_DH ** -0.5)
    qi = jnp.arange(WINDOW)[:, None]
    kj = jnp.arange(2 * WINDOW)[None, :]
    dist = qi + WINDOW - kj
    blk = jnp.arange(n)[:, None, None]
    valid = (dist >= 0) & (dist < WINDOW) & (blk * WINDOW + kj - WINDOW >= 0)
    slopes = alibi_slopes(SWA_HEADS).reshape(SWA_KV_HEADS, grp)[:, :, None, None]
    s = s - slopes * dist.astype(jnp.float32)
    s = jnp.where(valid[None, :, None, None], s, -jnp.inf)
    sink = sinks.astype(jnp.float32).reshape(SWA_KV_HEADS, grp)[:, :, None, None]
    m = jnp.maximum(jnp.max(s, axis=-1, keepdims=True), sink)
    p = jnp.exp(s - m)
    p = p / (jnp.sum(p, axis=-1, keepdims=True) + jnp.exp(sink - m))
    o = jnp.einsum('bnhgqk,bnkhd->bnqhgd', p.astype(vb.dtype), vb)
    return o.reshape(bsz, seq, SWA_WIDTH)

def stick_breaking_attention(q, k, v):
    bsz, seq, heads, dh = q.shape
    n = seq // SB_BLOCK
    f32 = jnp.float32
    tri_incl = jnp.tril(jnp.ones((SB_BLOCK, SB_BLOCK), f32))
    tri_blocks = jnp.tril(jnp.ones((n, n), f32), -1)
    scale = dh ** -0.5
    outs = []
    for i in range(n):
        nk = i + 1
        length = nk * SB_BLOCK
        q_blk = q[:, i * SB_BLOCK:(i + 1) * SB_BLOCK]
        k_blk = k[:, :length]
        v_blk = v[:, :length]
        z = jnp.einsum('bqhd,bshd->bhqs', q_blk, k_blk).astype(f32) * scale
        qpos = i * SB_BLOCK + jnp.arange(SB_BLOCK)
        valid = jnp.arange(length)[None, :] < qpos[:, None]
        zm = jnp.where(valid, z, -jnp.inf)
        l = jax.nn.log_sigmoid(-zm).reshape(bsz, heads, SB_BLOCK, nk, SB_BLOCK)
        rev_in = jnp.einsum('bhqnj,js->bhqns', l, tri_incl)
        after = jnp.einsum('bhqm,mn->bhqn', jnp.sum(l, axis=-1), tri_blocks[:nk, :nk])
        rev = (rev_in + after[..., None]).reshape(bsz, heads, SB_BLOCK, length)
        a = jnp.exp(zm + rev)
        outs.append(jnp.einsum('bhqs,bshd->bqhd', a.astype(v.dtype), v_blk))
    o = jnp.concatenate(outs, axis=1)
    return o.reshape(bsz, seq, heads * dh)

def hybrid_mixer(xn, w_in, dn_conv, dn_a_log, dn_dt_bias, dn_norm, swa_sinks, w_br_dn, w_br_swa, w_br_sb, w_o):
    bsz, seq, _ = xn.shape
    proj = xn @ w_in
    dn_qkv, dn_z, dn_a, dn_b, swa_q, swa_kv, sb_qkv, gates = split_cols(proj, IN_SIZES)
    dn_qkv = jax.nn.silu(causal_dwconv(dn_qkv, dn_conv))
    q, k, v = split_cols(dn_qkv, (DN_QK_WIDTH, DN_QK_WIDTH, DN_WIDTH))
    q = l2norm(q.reshape(bsz, seq, DN_HEADS, DN_DK))
    k = l2norm(k.reshape(bsz, seq, DN_HEADS, DN_DK))
    v = v.reshape(bsz, seq, DN_HEADS, DN_DV)
    g = -jnp.exp(dn_a_log.astype(jnp.float32)) * jax.nn.softplus(dn_a.astype(jnp.float32) + dn_dt_bias.astype(jnp.float32))
    beta = jax.nn.sigmoid(dn_b.astype(jnp.float32))
    o_dn = gated_delta_rule(q, k, v, g, beta)
    o_dn = rmsnorm(o_dn, dn_norm) * jax.nn.silu(dn_z.reshape(bsz, seq, DN_HEADS, DN_DV).astype(jnp.float32))
    y_dn = o_dn.reshape(bsz, seq, DN_WIDTH).astype(xn.dtype)
    swa_k, swa_v = split_cols(swa_kv, (SWA_KV_WIDTH, SWA_KV_WIDTH))
    y_swa = sliding_window_gqa(swa_q.reshape(bsz, seq, SWA_HEADS, SWA_DH), swa_k.reshape(bsz, seq, SWA_KV_HEADS, SWA_DH), swa_v.reshape(bsz, seq, SWA_KV_HEADS, SWA_DH), swa_sinks)
    sb_q, sb_k, sb_v = split_cols(sb_qkv, (SB_WIDTH, SB_WIDTH, SB_WIDTH))
    y_sb = stick_breaking_attention(sb_q.reshape(bsz, seq, SB_HEADS, SB_DH), sb_k.reshape(bsz, seq, SB_HEADS, SB_DH), sb_v.reshape(bsz, seq, SB_HEADS, SB_DH))
    gate = jax.nn.sigmoid(gates).reshape(bsz, seq, N_BRANCH, D_MODEL)
    merged = gate[:, :, 0] * (y_dn @ w_br_dn) + gate[:, :, 1] * (y_swa @ w_br_swa) + gate[:, :, 2] * (y_sb @ w_br_sb)
    return merged @ w_o

def memory_cross_attention(hn, mem_n, w_xq, w_xkv, w_xo):
    bsz, seq, _ = hn.shape
    q = (hn @ w_xq).reshape(bsz, seq, X_HEADS, X_DH)
    kv = (mem_n @ w_xkv).reshape(bsz, mem_n.shape[1], 2, X_HEADS, X_DH)
    s = jnp.einsum('bqhd,bmhd->bhqm', q, kv[:, :, 0]).astype(jnp.float32) * (X_DH ** -0.5)
    p = jax.nn.softmax(s, axis=-1)
    o = jnp.einsum('bhqm,bmhd->bqhd', p.astype(kv.dtype), kv[:, :, 1])
    return o.reshape(bsz, seq, X_WIDTH) @ w_xo

def conv_ffn(hn, w_up, ffn_conv, w_down):
    up = causal_dwconv(hn @ w_up, ffn_conv)
    gate, val = jnp.split(up, 2, axis=-1)
    return (jax.nn.silu(gate) * val) @ w_down

def second_inputs(seed: int = 0) -> dict:
    key = jax.random.key(seed)
    ks = jax.random.split(key, 24)
    f32 = jnp.float32

    def dense(k, shape, fan_in):
        return jax.random.normal(k, shape, f32) * (fan_in ** -0.5)

    def gain(k, shape):
        return 1.0 + 0.02 * jax.random.normal(k, shape, f32)

    dt = jnp.exp(jax.random.uniform(ks[6], (DEPTH, DN_HEADS), f32, minval=math.log(1e-3), maxval=math.log(0.1)))
    return {
        'x': jax.random.normal(ks[0], (BATCH, SEQ, D_MODEL), f32),
        'mem': jax.random.normal(ks[1], (BATCH, MEM_LEN, D_MODEL), f32),
        'norm_mix': gain(ks[2], (DEPTH, D_MODEL)),
        'w_in': dense(ks[3], (DEPTH, D_MODEL, IN_COLS), D_MODEL),
        'dn_conv': dense(ks[4], (DEPTH, DN_CONV, 2 * DN_QK_WIDTH + DN_WIDTH), DN_CONV),
        'dn_a_log': jnp.log(jax.random.uniform(ks[5], (DEPTH, DN_HEADS), f32, minval=1.0, maxval=16.0)),
        'dn_dt_bias': dt + jnp.log(-jnp.expm1(-dt)),
        'dn_norm': gain(ks[7], (DEPTH, DN_DV)),
        'swa_sinks': 0.5 * jax.random.normal(ks[8], (DEPTH, SWA_HEADS), f32),
        'w_br_dn': dense(ks[9], (DEPTH, DN_WIDTH, D_MODEL), DN_WIDTH),
        'w_br_swa': dense(ks[10], (DEPTH, SWA_WIDTH, D_MODEL), SWA_WIDTH),
        'w_br_sb': dense(ks[11], (DEPTH, SB_WIDTH, D_MODEL), SB_WIDTH),
        'w_o': dense(ks[12], (DEPTH, D_MODEL, D_MODEL), D_MODEL),
        'norm_xattn': gain(ks[13], (DEPTH, D_MODEL)),
        'norm_mem': gain(ks[14], (DEPTH, D_MODEL)),
        'w_xq': dense(ks[15], (DEPTH, D_MODEL, X_WIDTH), D_MODEL),
        'w_xkv': dense(ks[16], (DEPTH, D_MODEL, 2 * X_WIDTH), D_MODEL),
        'w_xo': dense(ks[17], (DEPTH, X_WIDTH, D_MODEL), X_WIDTH),
        'norm_ffn': gain(ks[18], (DEPTH, D_MODEL)),
        'w_up': dense(ks[19], (DEPTH, D_MODEL, 2 * D_FF), D_MODEL),
        'ffn_conv': dense(ks[20], (DEPTH, FFN_CONV, 2 * D_FF), FFN_CONV),
        'w_down': dense(ks[21], (DEPTH, D_FF, D_MODEL), D_FF),
        'norm_final': gain(ks[22], (D_MODEL,)),
    }

def second_block(x, mem, norm_mix, w_in, dn_conv, dn_a_log, dn_dt_bias, dn_norm, swa_sinks, w_br_dn, w_br_swa, w_br_sb, w_o, norm_xattn, norm_mem, w_xq, w_xkv, w_xo, norm_ffn, w_up, ffn_conv, w_down, norm_final):
    h = x
    for l in range(DEPTH):
        h = h + hybrid_mixer(rmsnorm(h, norm_mix[l]), w_in[l], dn_conv[l], dn_a_log[l], dn_dt_bias[l], dn_norm[l], swa_sinks[l], w_br_dn[l], w_br_swa[l], w_br_sb[l], w_o[l])
        h = h + memory_cross_attention(rmsnorm(h, norm_xattn[l]), rmsnorm(mem, norm_mem[l]), w_xq[l], w_xkv[l], w_xo[l])
        h = h + conv_ffn(rmsnorm(h, norm_ffn[l]), w_up[l], ffn_conv[l], w_down[l])
    return rmsnorm(h, norm_final)


def setup_inputs(seed=0):
    out = dict(first_inputs(seed))
    for name, value in second_inputs(seed + 1).items():
        if name != "x":
            out[name + "_2"] = value
    return out


def reference(
    x, gla_norm, gla_w_in, gla_w_gate_up, gla_b_gate, gla_o_norm, gla_w_out, s5_norm, s5_w_in,
    s5_lam_re, s5_lam_im, s5_log_dt, s5_b_re, s5_b_im, s5_c_re, s5_c_im, s5_d, s5_w_out,
    mlp_norm, mlp_w_up, mlp_w_down, final_norm, mem_2, norm_mix_2, w_in_2, dn_conv_2,
    dn_a_log_2, dn_dt_bias_2, dn_norm_2, swa_sinks_2, w_br_dn_2, w_br_swa_2, w_br_sb_2, w_o_2,
    norm_xattn_2, norm_mem_2, w_xq_2, w_xkv_2, w_xo_2, norm_ffn_2, w_up_2, ffn_conv_2, w_down_2,
    norm_final_2,
):
    x = first_block(
        x, gla_norm, gla_w_in, gla_w_gate_up, gla_b_gate, gla_o_norm, gla_w_out, s5_norm,
        s5_w_in, s5_lam_re, s5_lam_im, s5_log_dt, s5_b_re, s5_b_im, s5_c_re, s5_c_im, s5_d,
        s5_w_out, mlp_norm, mlp_w_up, mlp_w_down, final_norm,
    )
    return second_block(
        x, mem_2, norm_mix_2, w_in_2, dn_conv_2, dn_a_log_2, dn_dt_bias_2, dn_norm_2,
        swa_sinks_2, w_br_dn_2, w_br_swa_2, w_br_sb_2, w_o_2, norm_xattn_2, norm_mem_2, w_xq_2,
        w_xkv_2, w_xo_2, norm_ffn_2, w_up_2, ffn_conv_2, w_down_2, norm_final_2,
    )


_drawn_inputs = setup_inputs


def setup_inputs(seed=0):
    import zlib

    import numpy as np

    out = dict(_drawn_inputs(seed))
    spreads = {}
    factors = {'gla_o_norm': 5.388,
     'mlp_norm': 3.193,
     'norm_mix_2': 3.84,
     'dn_norm_2': 8.0,
     'swa_sinks_2': 5.103,
     'norm_xattn_2': 8.0,
     'norm_mem_2': 8.0,
     'norm_ffn_2': 13.389,
     'norm_final_2': 7.975}
    for name, (base, spread) in spreads.items():
        noise = np.random.default_rng([zlib.crc32(name.encode()), seed]).standard_normal(out[name].shape)
        drawn = base * np.exp(spread * noise) if base else spread * noise
        out[name] = jnp.asarray(drawn.astype(out[name].dtype))
    for name, factor in factors.items():
        out[name] = (out[name] * factor).astype(out[name].dtype)
    return out
```

```python
import numpy as np

P = 128
SEQ = 256
M = SEQ // P
D = 2048
CH = 2048
EPS = 1e-6
COLS = {"gla_norm": 0, "mlp_norm": 16, "b_gate": 32, "norm_mix": 40, "norm_xattn": 56, "norm_mem": 72, "norm_ffn": 88,
        "dn_conv": 104}
N_COLS = 104 + 24 * 4
BRANCH = [("sb", 0, 12)] * 5 + [("swa", 5, 8)] * 5 + [("dn", 10, 0)] * 6


def build(nc, x, mem, stream, cols, rows, wglow, wab, wgu, shapes, masks, out):
    import concourse.bass as bass
    from concourse import mybir
    from contextlib import ExitStack

    F32, F32R, BF16 = mybir.dt.float32, mybir.dt.float32r, mybir.dt.bfloat16
    ACT, ALU, AX = mybir.ActivationFunctionType, mybir.AluOpType, mybir.AxisListType
    N = 512
    NB = D // N
    SLOTS = 4
    AHEAD = 3
    NCHUNK = stream.shape[0]

    def at(n, i=None, step=0):
        return n if i is None else i * step + n

    with ExitStack() as ctx:
        def sem(name):
            return ctx.enter_context(nc.semaphore(name))

        cursor = [(nc.sbuf_base + 31) // 32 * 32]

        def take(nbytes):
            a = cursor[0]
            cursor[0] += (nbytes + 31) // 32 * 32
            return a

        def sb(name, shape, dt=F32, offset=None):
            nbytes = (2 if dt == BF16 else 4) * int(np.prod(shape[1:]))
            return nc.alloc_sbuf_tensor_at(name, shape, dt, offset=take(nbytes) if offset is None else offset)

        K = 1024
        h = sb("h", [P, M, D])
        a_raw = take(SLOTS * CH * 4)
        w_raw = sb("w_raw", [P, SLOTS, CH], F32, a_raw)
        w_lo = sb("w_lo", [P, SLOTS, CH], F32R, a_raw)
        w_hi = sb("w_hi", [P, SLOTS, CH], F32R)
        x_hi = sb("x_hi", [P, 16, SEQ], F32R)
        x_lo = sb("x_lo", [P, 16, SEQ], F32R)
        a_a = take(32 * K)
        a_hi = sb("a_hi", [P, 16, SEQ], F32R, a_a)
        a_lo = sb("a_lo", [P, 16, SEQ], F32R, a_a + 16 * K)
        nat = sb("nat", [P, 2, M, N])
        col = sb("col", [P, N_COLS])
        consts = sb("consts", [P, 2 * P])
        junk = sb("junk", [P, N], BF16)
        ss = [sb(f"ss{k}", [P, M, NB]) for k in range(2)]
        ms = [sb(f"ms{k}", [P, M]) for k in range(2)]
        var = [sb(f"var{k}", [P, M]) for k in range(2)]
        rstd = [sb(f"rstd{k}", [P, M]) for k in range(2)]
        mhalf = sb("mhalf", [P, M * 8])
        a_s = take(48 * K)
        a_z = take(9 * K // 2)
        assert cursor[0] <= nc.sbuf_usable_end, (cursor[0], nc.sbuf_usable_end)
        ident, ones = consts[:, 0:P], consts[:, P:2 * P]

        small_used = [0]

        def small(name, shape, dt=F32):
            nbytes = (2 if dt == BF16 else 4) * int(np.prod(shape[1:]))
            t = sb(name, shape, dt, a_z + small_used[0])
            small_used[0] += (nbytes + 31) // 32 * 32
            assert small_used[0] <= 9 * K // 2, small_used[0]
            return t

        qT = sb("qT", [P, 8, SEQ], F32, a_s)
        kT = sb("kT", [P, 8, SEQ], F32, a_s + 8 * K)
        v = sb("v", [P, M, D], F32, a_s + 16 * K)
        sr = sb("sr", [P, M, D], F32, a_s + 32 * K)
        wg_raw = sb("wg_raw", [P, 16, 16], F32, a_s + 32 * K)
        wg_hi = sb("wg_hi", [P, 16, 16], F32R, a_s + 33 * K)
        wg_lo = sb("wg_lo", [P, 16, 16], F32R, a_s + 34 * K)
        glow = sb("glow", [P, M, 16], F32, a_s + 35 * K)
        glowT = sb("glowT", [16, SEQ], F32, a_s + 36 * K)
        w_gu = sb("w_gu", [16, 1024], F32, a_s + 37 * K)
        zb = sb("zb", [P, 8, SEQ], F32, a_a)
        ez = sb("ez", [P, 8, SEQ], F32, a_a + 8 * K)
        cum = sb("cum", [P, 8, SEQ], F32, a_a + 16 * K)
        kd = sb("kd", [P, 8, SEQ], F32, a_a + 24 * K)
        qd = sb("qd", [P, 2, 6, 64], F32, a_a + 12 * K)
        sT = sb("sT", [P, 2, 3 * P], F32, a_a + 28 * K)
        onorm = small("onorm", [P, N])
        mask01 = small("mask01", [P, SEQ])
        edec = small("edec", [P, 8, 6])
        oss = small("oss", [P, 4, M])
        ovar = small("ovar", [P, 4, M])
        orstd = small("orstd", [P, 4, M])
        frow = sb("frow", [P, D], F32, a_s + 16 * K)

        small_used[0] = 0
        tri = small("tri", [P, P])
        lvl = small("lvl", [P, 6, P], BF16)
        row_p = small("row_p", [P, 3 * 8 + P])
        alog, dtb, sinks, dnorm = row_p[:, 0:8], row_p[:, 8:16], row_p[:, 16:24], row_p[:, 24:24 + P]
        ab = small("ab", [P, M, 16])
        (u8, l8, g8, beta, betah, gc, gl, egc, ekd, ssq, ssk, rq, rk, brk, nber, kds, qsc, mx, nmx, rs, es, rden,
         yss, yrs) = [small(n, [P, M, 8]) for n in ("u8", "l8", "g8", "beta", "betah", "gc", "gl", "egc", "ekd", "ssq", "ssk",
                                                  "rq", "rk", "brk", "nber", "kds", "qsc", "mx", "nmx", "rs", "es", "rden",
                                                  "yss", "yrs")]
        nega = small("nega", [P, 8])
        glb = small("glb", [P, 4, 8])
        cqT = sb("cqT", [P, 8, SEQ], F32, a_s)
        ckT = sb("ckT", [P, 8, SEQ], F32, a_s + 8 * K)
        qkT = sb("qkT", [P, 8, M, P], F32, a_s + 16 * K)
        xT = sb("xT", [P, 8, M, P], F32, a_s + 24 * K)
        vb = sb("vb", [P, M, 1024], F32, a_s + 32 * K)
        kdec = sb("kdec", [P, M, 1024], F32, a_s + 40 * K)
        dec = sb("dec", [P, 8, M, P], F32, a_a)
        xn = sb("xn", [P, 8, M, P], F32, a_a)
        nT = sb("nT", [P, 8, M, P], F32, a_a + 16 * K)
        pm = sb("pm", [P, 8, M, P], F32, a_a + 24 * K)
        diag = [sb(f"diag{k}", [P, 4, M, P], F32, a_a + (24 + 4 * k) * K) for k in range(2)]
        tri_c = sb("tri_c", [P, P], F32, a_a + 28 * K)
        same_c = sb("same_c", [P, P], F32, a_a + 28 * K + 512)
        wab_raw = sb("wab_raw", [P, 16, 16], F32, a_a + 29 * K)
        wab_hi = sb("wab_hi", [P, 16, 16], F32R, a_a + 30 * K)
        wab_lo = sb("wab_lo", [P, 16, 16], F32R, a_a + 31 * K)
        cv = sb("cv", [P, 4, SEQ], F32, a_a + 8 * K)
        th = sb("th", [P, 4, SEQ], F32, a_a + 12 * K)
        zz = sb("zz", [P, M, 1024], F32, a_a + 8 * K)
        state = sb("state", [P, 8, P], F32, a_a + 24 * K)
        rv = sb("rv", [P, 8, P], F32, a_a + 28 * K)
        ysq = sb("ysq", [P, 16, P], F32, a_s + 16 * K)
        sbq = sb("sbq", [P, 4, SEQ], F32, a_a)
        sbk = sb("sbk", [P, 4, SEQ], F32, a_a + 4 * K)
        sbv = sb("sbv", [P, M, N], F32, a_a + 16 * K)
        swq = sb("swq", [P, 4, SEQ], F32, a_a + 20 * K)
        swk = sb("swk", [P, SEQ], F32, a_s + 40 * K)
        swv = sb("swv", [P, M, P], F32, a_s + 41 * K)
        amask = sb("amask", [P, 2, 3 * P], BF16, a_s + 42 * K)
        zm = sb("zm", [P, 4, 3 * P], F32, a_s)
        sp_ = sb("sp_", [P, 4, 3 * P], F32, a_s + 6 * K)
        ysb = sb("ysb", [P, M, N], F32, a_s + 12 * K)
        sw = sb("sw", [P, 8, 3 * P], F32, a_s + 16 * K)
        yswa = sb("yswa", [P, M, N], F32, a_s + 28 * K)
        pT = sb("pT", [P, 24, P], F32, a_s)
        m_hi = sb("m_hi", [P, 16, SEQ], F32R, a_s)
        m_lo = sb("m_lo", [P, 16, SEQ], F32R, a_s + 16 * K)
        mg = [sb("mg0", [P, M, N], F32, a_s + 44 * K), sb("mg1", [P, M, N], F32, a_s + 40 * K)]
        memt = sb("memt", [P, M, D], F32, a_s + 32 * K)
        xkT = sb("xkT", [P, 4, SEQ], F32, a_s)
        xv = sb("xv", [P, M, N], F32, a_s + 4 * K)
        xqT = sb("xqT", [P, 4, SEQ], F32, a_s + 8 * K)
        xp = sb("xp", [P, M, 4, SEQ], F32, a_s + 12 * K)
        xpT = sb("xpT", [P, M, 4, 2, P], F32, a_s + 20 * K)
        yx = sb("yx", [P, M, N], F32, a_s + 28 * K)
        cw_all = sb("cw_all", [P, 2, 96], F32, a_s + 47 * K)
        cw = sb("cw", [P, 32, 3], F32, a_s + 46 * K)
        fg = sb("fg", [P, 4, SEQ], F32, a_s)
        fv = sb("fv", [P, 4, SEQ], F32, a_s + 4 * K)
        ft = sb("ft", [P, 4, SEQ], F32, a_s + 8 * K)
        frow2 = sb("frow2", [P, D], F32, a_s + 16 * K)

        acc = ctx.enter_context(nc.psum_tensor("acc", [P, 2, M, N], F32))
        tp = ctx.enter_context(nc.psum_tensor("tp", [P, 2, 4, SEQ], F32))

        def tpf(g):
            return tp[:, g % 2].rearrange("p k t -> p (k t)")

        landed = [sem(f"landed{s}") for s in range(SLOTS)]
        hi_ready, lo_ready, used = sem("hi_ready"), sem("lo_ready"), sem("used")
        tp_done = sem("tp_done")
        took = {k: {e: [sem(f"{k}_took_{e}{p}") for p in range(2)] for e in ("act", "dve")} for k in ("acc", "tp")}
        x_in, cols_in, cst_in, gla_in, row_in, out_done = [sem(s) for s in ("x_in", "cols_in", "cst_in", "gla_in", "row_in", "out_done")]
        act_step, dve_step = sem("act_step"), sem("dve_step")
        sq_done, var_ready, rstd_ready = [[sem(f"{n}{k}") for k in range(2)] for n in ("sq_done", "var_ready", "rstd_ready")]
        (dn_in, smalls_in, amask_in, mem_in, cw_in, row2_in, wab_h, wab_l, u_ready, u_ln, b_tanh, g_ready, e_gc,
         conv0, conv1, conv_t, conv_sq, ss_ready, r_pow, dg_ready, diff_ready, dec_exp, xt0, z_tanh, rv_ready,
         y_scaled, y_sq, y_var, y_pow, zm_ready, sp_ln, sp_ready, a_exp, sw_max, sw_exp, g_tanh, mg_ready, p_ready,
         f_tanh, f_hi, cw_ready, x_max, y_done, a_log, o_fin, conv_out, f_lo, ekd_in, m_half, tri_used) = [
            sem(n) for n in (
                "dn_in", "smalls_in", "amask_in", "mem_in", "cw_in", "row2_in", "wab_h", "wab_l", "u_ready", "u_ln",
                "b_tanh", "g_ready", "e_gc", "conv0", "conv1", "conv_t", "conv_sq", "ss_ready", "r_pow", "dg_ready",
                "diff_ready", "dec_exp", "xt0", "z_tanh", "rv_ready", "y_scaled", "y_sq", "y_var", "y_pow",
                "zm_ready", "sp_ln", "sp_ready", "a_exp", "sw_max", "sw_exp", "g_tanh", "mg_ready", "p_ready",
                "f_tanh", "f_hi", "cw_ready", "x_max", "y_done", "a_log", "o_fin", "conv_out", "f_lo", "ekd_in",
                "m_half", "tri_used")]
        xn_act, xn_dve, xh_done = sem("xn_act"), sem("xn_dve"), sem("xh_done")
        a_sq = sem("a_sq")
        ah_done = sem("ah_done")
        wg_h, wg_l = sem("wg_h"), sem("wg_l")
        lnz_ready, la_diff, kd_exp, e_sum, e_exp, kdec_ready = [sem(s) for s in ("lnz_ready", "la_diff", "kd_exp", "e_sum", "e_exp", "kdec_ready")]
        qd_ready, sT_zero, r_tanh = sem("qd_ready"), sem("sT_zero"), sem("r_tanh")
        osq, ovar_s, orstd_s = sem("osq"), sem("ovar_s"), sem("orstd_s")
        mh_set = sem("mh_set")
        rowdone = sem("rowdone")

        class Turns:

            def __init__(self, kind):
                self.sems, self.who, self.name = took[kind], [], {}

            def add(self, name, who):
                self.name[name] = len(self.who)
                self.who.append(who)

            def count(self, n):
                return sum(1 for k in range(n % 2, n + 1, 2) if self.who[k] == self.who[n])

            def sem(self, n):
                return self.sems[self.who[n]][n % 2]

            def wait(self, eng, n, i=None, per=0):
                eng.wait_ge(self.sem(n), at(self.count(n), i, self.count(n + per) - self.count(n) if per else 0))

        accs, tps = Turns("acc"), Turns("tp")

        for n in range(8):
            accs.add(("gla", n), "act")
        for n in range(8, 12):
            accs.add(("gla", n), "dve")
        for n in range(4):
            accs.add(("glaout", n), "dve")
        for g in range(4):
            for n in range(4):
                accs.add(("up", g, n), "act")
            for n in range(4):
                accs.add(("down", g, n), "dve")

        def add_norm(j):
            for n in range(4):
                tps.add(("norm", j, n), "dve")

        add_norm(0)
        for name, who in (("glow", "act"), (("gT", 0), "dve"), ("glowT", "act"), ("z0", "act"), ("z1", "act"),
                          (("gT", 1), "dve"), (("gT", 2), "dve"), (("gT", 3), "dve")):
            tps.add(name, who)
        for hd in range(4):
            tps.add(("s", hd), "act")
            tps.add(("o", hd), "dve")
            tps.add(("yT", hd), "dve")
        add_norm(1)
        for g in range(4):
            for n in range(4):
                tps.add(("aT", g, n), "dve")

        for b in range(6):
            accs.add(("dn", b), "act")
        for b in range(2):
            accs.add(("z", b), "dve")
        for name in ("sbq", "sbk", "sbv", "swq", "swkv"):
            accs.add(name, "act")
        for nb in range(NB):
            for br in ("sb", "swa", "dn"):
                accs.add(("gate", nb, br), "act")
                accs.add(("br", nb, br), "dve")
        for n in range(NB):
            accs.add(("wo", n), "dve")
        for name in ("xk", "xv", "xq"):
            accs.add(name, "act")
        for n in range(NB):
            accs.add(("xo", n), "dve")
        for g in range(2):
            for b in range(4):
                accs.add(("fg", g, b), "act")
                accs.add(("fv", g, b), "act")
            for n in range(NB):
                accs.add(("fdown", g, n), "dve")

        def add(*names, who="dve"):
            for name in names:
                tps.add(name, who)

        add_norm(3)
        add("ab", who="act")
        add(("dT", 0), "gc", ("ssq", 0), ("dT", 1))
        add(("ssq", 1), ("rg", 0), ("rg", 1))
        add(("dT", 2), ("ssq", 2), ("dT", 3), ("ssq", 3))
        add(("dT", 4), ("kk", 0), ("kk", 1), ("rb", 0), ("rb", 1))
        add(("vN", 4), ("qk", 0), ("qk", 1))
        add(("kN", 0), ("kN", 1))
        add(("dT", 5))
        add(("x0", 0), ("x0", 1), who="act")
        for l in range(1, 6):
            add(("P", l, 0), ("P", l, 1))
            if l == 1:
                add(("vN", 5))
            for hf in range(2):
                add(*([("D", l, hf)] if l < 5 else []), ("DT", l, hf))
        for cs in range(4):
            if cs:
                add(("kS", cs), ("qS", cs))
            if cs == 0:
                add("sbqT")
            add(("Xr", cs), who="act")
            if cs == 1:
                add("sbkT")
            add(("in", cs), *([("up", cs)] if cs < 3 else []))
        add(("sz", 0), ("sz", 1))
        add("swqT")
        add(("rev", 0), ("rev", 1))
        add("swkT")
        add("so", who="act")
        add(*[("ws", k) for k in range(4)])
        add("ysbT")
        add(*[("wp", k) for k in range(3)], who="act")
        add("wo_")
        add("yswaT", ("ydnT", 0), ("ydnT", 1))
        for nb in range(NB):
            add(("mT", nb))
        add_norm(4)
        add_norm(5)
        add("xkT", "xqT")
        add(("xs", 0), ("xs", 1), who="act")
        add(("xpT", 0))
        add(("xpT", 1), who="act")
        add("xo_", "yxT")
        add_norm(6)
        for g in range(2):
            for b in range(4):
                add(("fgT", g, b), ("fvT", g, b))

        C_GLA, C_OUT, C_MLP, C_2 = 0, 48, 64, 192
        C_BR, C_WO, C_X, C_XO, C_FFN = C_2 + 50, C_2 + 114, C_2 + 130, C_2 + 142, C_2 + 146
        assert C_FFN + 96 == NCHUNK
        COL = COLS
        block = ctx.enter_context(nc.Block())

        @block.sync
        def _(sp):
            sp.dma_start(h[:], x.rearrange("(m p) n -> p m n", p=P)).then_inc(x_in, 16)
            sp.dma_start(consts[:], shapes[:, 0:2 * P]).then_inc(cst_in, 16)
            sp.dma_start(mask01[:], shapes[:, 2 * P:2 * P + SEQ]).then_inc(cst_in, 16)
            sp.dma_start(col[:], cols[:, 0:N_COLS]).then_inc(cols_in, 16)
            for s in range(SLOTS):
                sp.dma_start(w_raw[:, s], stream[s]).then_inc(landed[s], 16)
            with sp.Fori(0, NCHUNK // SLOTS - 1) as i:
                for s in range(SLOTS):
                    sp.wait_ge(used, i * SLOTS + (s + 1))
                    sp.dma_start(w_raw[:, s], stream[(i + 1) * SLOTS + s]).then_inc(landed[s], 16)
            for c in range(NCHUNK // SLOTS * SLOTS, NCHUNK + AHEAD):
                sp.wait_ge(used, c - SLOTS + 1)
                sp.dma_start(w_raw[:, c % SLOTS], stream[min(c, NCHUNK - 1)]).then_inc(landed[c % SLOTS], 16)
            for n in range(NB):
                sp.wait_ge(o_fin, n + 1)
                sp.dma_start(out.rearrange("(m p) n -> p m n", p=P)[:, :, n * N:(n + 1) * N],
                             h[:, :, n * N:(n + 1) * N]).then_inc(out_done, 16)
            sp.wait_ge(out_done, 16 * NB)

        @block.gpsimd
        def _(pool):
            pool.dma_start(wg_raw[:], wglow).then_inc(gla_in, 16)
            pool.dma_start(w_gu[:], wgu).then_inc(gla_in, 16)
            pool.dma_start(onorm[:], rows[:, 0:N]).then_inc(gla_in, 16)
            pool.memset(mhalf[:], -0.5).then_inc(mh_set, 1)
            pool.wait_ge(mh_set, 1)
            mh8 = mhalf[:].rearrange("p (m h) -> p m h", m=M)

            def norm(j, k=0):
                pool.wait_ge(var_ready[k], j + 1)
                pool.tensor_tensor(rstd[k][:], var[k][:], mhalf[:, 0:M], ALU.pow).then_inc(rstd_ready[k], 1)

            norm(0)
            for hd in range(4):
                pool.wait_ge(ovar_s, hd + 1)
                pool.tensor_tensor(orstd[:, hd], ovar[:, hd], mhalf[:, 0:M], ALU.pow).then_inc(orstd_s, 1)
            pool.wait_ge(tp_done, tps.name[("yT", 3)] + 1)
            pool.dma_start(frow[:], rows[:, N:N + D]).then_inc(row_in, 16)
            pool.dma_start(tri[:], shapes[:, 2 * P + SEQ:3 * P + SEQ]).then_inc(smalls_in, 16)
            pool.dma_start(lvl[:], masks[:, 0:6 * P]).then_inc(smalls_in, 16)
            pool.dma_start(row_p[:], rows[:, N + 2 * D:]).then_inc(smalls_in, 16)
            norm(1)
            pool.wait_ge(used, C_2)
            pool.dma_start(tri_c[:], shapes[:, 3 * P + SEQ:4 * P + SEQ]).then_inc(dn_in, 16)
            pool.dma_start(same_c[:], shapes[:, 4 * P + SEQ:5 * P + SEQ]).then_inc(dn_in, 16)
            pool.dma_start(wab_raw[:], wab).then_inc(dn_in, 16)
            norm(2)
            norm(3)
            pool.wait_ge(ss_ready, 1)
            pool.tensor_tensor(rq[:], ssq[:], mh8, ALU.pow).then_inc(r_pow, 1)
            pool.wait_ge(ss_ready, 2)
            pool.tensor_tensor(rk[:], ssk[:], mh8, ALU.pow).then_inc(r_pow, 1)
            pool.wait_ge(tp_done, tps.name[("up", 2)] + 1)
            pool.dma_start(amask[:], masks[:, 6 * P:]).then_inc(amask_in, 16)
            pool.wait_ge(y_var, 1)
            pool.tensor_tensor(yrs[:], yss[:], mh8, ALU.pow).then_inc(y_pow, 1)
            pool.wait_ge(tp_done, tps.name[("mT", 3)] + 1)
            pool.dma_start(memt[:], mem.rearrange("(m p) n -> p m n", p=P)).then_inc(mem_in, 16)
            norm(0, 1)
            norm(4)
            pool.wait_ge(tp_done, tps.name[("norm", 4, 3)] + 1)
            pool.dma_start(cw_all[:], cols[:, N_COLS:]).then_inc(cw_in, 16)
            norm(5)
            pool.dma_start(frow2[:], rows[:, N + D:N + 2 * D]).then_inc(row2_in, 16)
            norm(6)

        @block.tensor
        def _(pe):
            def chunk(c, lhs, k0, blk, first, last, i=None, step=0, bper=0, n_k=4, width=N):
                pe.wait_ge(lo_ready, at(c + 1, i, step))
                if first and blk >= 2:
                    accs.wait(pe, blk - 2, i, bper)
                wh = w_hi[:, c % SLOTS].rearrange("p (k n) -> p k n", n=width)
                wl = w_lo[:, c % SLOTS].rearrange("p (k n) -> p k n", n=width)
                for k in range(n_k):
                    for m in range(M):
                        xh = lhs[0][:, k0 + k, m * P:(m + 1) * P]
                        xl = lhs[1][:, k0 + k, m * P:(m + 1) * P]
                        dst = acc[:, blk % 2, m, 0:width]
                        pe.matmul(dst, xh, wh[:, k], start=first and k == 0, stop=False)
                        pe.matmul(dst, xh, wl[:, k], start=False, stop=False)
                        mm = pe.matmul(dst, xl, wh[:, k], start=False, stop=last and k == n_k - 1)
                mm.then_inc(used, 1)

            opened = [0]

            def open_group(g, i=None, per=0):
                assert g == opened[0], (g, opened[0], "groups in the order of the plan")
                opened[0] += 1
                if g >= 2:
                    tps.wait(pe, g - 2, i, per)

            def transposes(g, src, i=None, per=0):
                open_group(g, i, per)
                for k in range(4):
                    for m in range(M):
                        mm = pe.transpose(tp[:, g % 2, k, m * P:(m + 1) * P], src[:, m, k * P:(k + 1) * P], ident)
                mm.then_inc(tp_done, 1)

            def norm_part(j, n):
                k = NB * (j - (j > 2)) + n + 1
                pe.wait_ge(xn_act, k)
                pe.wait_ge(xn_dve, k)
                transposes(tps.name[("norm", j, n)], nat[:, n % 2])

            def norm(j):
                for n in range(NB):
                    norm_part(j, n)

            X, A = (x_hi, x_lo), (a_hi, a_lo)

            def low_rank_gate():
                g = tps.name["glow"]
                open_group(g)
                pe.wait_ge(wg_l, 1)
                for m in range(M):
                    for k in range(16):
                        for j, (u, w) in enumerate(((x_hi, wg_hi), (x_hi, wg_lo), (x_lo, wg_hi))):
                            mm = pe.matmul(tp[:, g % 2, 2 * m, 0:16], u[:, k, m * P:(m + 1) * P], w[:, k, :],
                                           start=(k == 0 and j == 0), stop=(k == 15 and j == 2))
                mm.then_inc(tp_done, 1)

            def low_rank_transposed():
                g = tps.name["glowT"]
                open_group(g)
                tps.wait(pe, tps.name["glow"])
                for m in range(M):
                    mm = pe.transpose(tp[0:16, g % 2, 0, m * P:(m + 1) * P], glow[:, m, :], ident)
                mm.then_inc(tp_done, 1)

            def gate_logits(half):
                g = tps.name[f"z{half}"]
                open_group(g)
                tps.wait(pe, tps.name["glowT"])
                for k in range(4):
                    t = 4 * half + k
                    mm = pe.matmul(tp[:, g % 2, k, :], w_gu[:, t * P:(t + 1) * P], glowT[:], start=True, stop=True)
                mm.then_inc(tp_done, 1)

            def gla_scores(hd):
                g = tps.name[("s", hd)]
                open_group(g)
                pe.wait_ge(qd_ready, hd + 1)
                f = tpf(g)
                pair = 0
                for cs in range(4):
                    part = slice(64 * (cs % 2), 64 * (cs % 2) + 64)
                    c0 = 64 * cs if cs < 2 else 2 * P + 64 * (cs - 2)
                    later = 3 - cs
                    for kk in range(2):
                        t = 2 * hd + kk
                        mm = pe.matmul(f[part, c0:c0 + 64], kT[:, t, 64 * cs:64 * cs + 64],
                                       qT[:, t, 64 * cs:64 * cs + 64], start=kk == 0, stop=kk == 1)
                    for kk in range(2):
                        if later:
                            mm = pe.matmul(f[part, c0 + 64:c0 + 64 + 64 * later], kT[:, 2 * hd + kk, 64 * cs:64 * cs + 64],
                                           qd[:, kk, pair:pair + later, :].rearrange("p c t -> p (c t)"),
                                           start=kk == 0, stop=kk == 1)
                    pair += later
                mm.then_inc(tp_done, 1)

            def gla_values(hd):
                g = tps.name[("o", hd)]
                open_group(g)
                tps.wait(pe, tps.name[("s", hd)])
                s, f, cols = sT[:, hd % 2], tpf(g), slice(hd * N, (hd + 1) * N)
                pe.matmul(f[:, 0:N], s[:, 0:P], v[:, 0, cols], start=True, stop=True)
                pe.matmul(f[:, N:2 * N], s[:, P:2 * P], v[:, 0, cols], start=True, stop=False)
                pe.matmul(f[:, N:2 * N], s[:, 2 * P:3 * P], v[:, 1, cols], start=False, stop=True).then_inc(tp_done, 1)

            def gla_side(c):
                for hd in range(4):
                    if c == 33 + 4 * hd:
                        gla_scores(hd)
                    if c == 37 + 4 * hd:
                        tps.wait(pe, tps.name[("o", hd)])
                        transposes(tps.name[("yT", hd)], sr[:, :, hd * N:(hd + 1) * N])
                    if c == 34 + 4 * hd:
                        gla_values(hd)

            pe.wait_ge(cst_in, 32)
            norm(0)
            for c in range(48):
                b, q = divmod(c, 4)
                if c < 4:
                    tps.wait(pe, tps.name[("norm", 0, c)])
                chunk(C_GLA + c, X, 4 * q, accs.name[("gla", b)], q == 0, q == 3)
                if c == 3:
                    low_rank_gate()
                if c in (4, 8, 12, 16):
                    n = c // 4 - 1
                    accs.wait(pe, accs.name[("gla", n)])
                    transposes(tps.name[("gT", n)], nat[:, n % 2])
                if c == 5:
                    low_rank_transposed()
                if c in (6, 7):
                    gate_logits(c - 6)
                gla_side(c)
            for c in range(16):
                b, q = divmod(c, 4)
                if b == 0:
                    tps.wait(pe, tps.name[("yT", q)])
                chunk(C_OUT + c, A, 4 * q, accs.name[("glaout", b)], q == 0, q == 3)
                gla_side(48 + c)
            norm(1)
            for n in range(NB):
                tps.wait(pe, tps.name[("norm", 1, n)])
            with pe.Fori(0, 4) as i:
                for c in range(32):
                    b, q = divmod(c, 4)
                    if b == 4:
                        tps.wait(pe, tps.name[("aT", 0, q)], i, 4)
                    chunk(C_MLP + c, A if b >= 4 else X, 4 * q, accs.name[("up", 0, 0)] + b, q == 0, q == 3, i, 32, 8)
                    if c in (4, 8, 12, 16):
                        n = c // 4 - 1
                        pe.wait_ge(a_sq, at(n + 1, i, 4))
                        transposes(tps.name[("aT", 0, n)], nat[:, n % 2], i, 4)
            opened[0] += 12

            def small_product(name, w_parts):
                g = tps.name[name]
                open_group(g)
                for m in range(M):
                    for k in range(16):
                        for j, (u, w) in enumerate(((x_hi, w_parts[0]), (x_hi, w_parts[1]), (x_lo, w_parts[0]))):
                            mm = pe.matmul(tp[:, g % 2, 2 * m, 0:16], u[:, k, m * P:(m + 1) * P], w[:, k, :],
                                           start=(k == 0 and j == 0), stop=(k == 15 and j == 2))
                mm.then_inc(tp_done, 1)

            def mats(hf):
                return [(hh, m, 4 * hf + hh) for hh in range(4) for m in range(M)]

            def pairs_product(name, hf, lhs, rhs):
                g = tps.name[(*name, hf)]
                open_group(g)
                for hh, m, hd in mats(hf):
                    mm = pe.matmul(tpf(g)[:, (2 * hh + m) * P:(2 * hh + m + 1) * P], lhs(hd, m), rhs(hd, m), start=True, stop=True)
                mm.then_inc(tp_done, 1)

            def back(name, src):
                g = tps.name[name]
                open_group(g)
                for hh in range(4):
                    for m in range(M):
                        mm = pe.transpose(tpf(g)[:, m * N + hh * P:m * N + (hh + 1) * P], src(hh)[:, m * P:(m + 1) * P], ident)
                mm.then_inc(tp_done, 1)

            def dn_side(c):
                for b in range(6):
                    if c == 4 * b + 4:
                        accs.wait(pe, accs.name[("dn", b)])
                        transposes(tps.name[("dT", b)], nat[:, b % 2])
                if c == 3:
                    pe.wait_ge(wab_l, 1)
                    small_product("ab", (wab_hi, wab_lo))
                if c == 6:
                    g = tps.name["gc"]
                    open_group(g)
                    pe.wait_ge(g_ready, 1)
                    f = tpf(g)
                    for m in range(M):
                        pe.matmul(f[:, 8 * m:8 * m + 8], tri_c[:], g8[:, m], start=True, stop=True)
                        pe.matmul(f[:, 16 + 8 * m:24 + 8 * m], same_c[:], g8[:, m], start=True, stop=True)
                    for cs in range(4):
                        part = slice(64 * (cs % 2), 64 * (cs % 2) + 64)
                        c0 = (N, 32)[cs % 2] + 8 * (cs // 2)
                        mm = pe.matmul(f[:, c0:c0 + 8], ones[part], g8[part, cs // 2], start=True, stop=True)
                    mm.then_inc(tp_done, 1)
                if c in (6, 10, 14, 18):
                    b = c // 4 - 1
                    g = tps.name[("ssq", b)]
                    open_group(g)
                    pe.wait_ge(conv_sq, b + 1)
                    for m in range(M):
                        for hh in range(4):
                            mm = pe.matmul(tpf(g)[:, 4 * m + hh:4 * m + hh + 1], th[:, hh, m * P:(m + 1) * P], ones[:, 0:1],
                                           start=True, stop=True)
                    mm.then_inc(tp_done, 1)

                def row_broadcast(name, hf, count, src):
                    g = tps.name[(name, hf)]
                    open_group(g)
                    pe.wait_ge(dg_ready, count)
                    d = src[:].rearrange("p h m i -> p (h m i)")
                    for k in range(2):
                        mm = pe.matmul(tpf(g)[:, k * N:(k + 1) * N], ones, d[:, k * N:(k + 1) * N], start=True, stop=True)
                    mm.then_inc(tp_done, 1)

                if c in (10, 11):
                    row_broadcast("rg", c - 10, c - 9, diag[0])
                if c == 21:
                    pe.wait_ge(conv_out, 4)
                    for hf in range(2):
                        pairs_product(("kk",), hf, lambda hd, m: ckT[:, hd, m * P:(m + 1) * P], lambda hd, m: ckT[:, hd, m * P:(m + 1) * P])
                if c == 22:
                    row_broadcast("rb", 0, 3, diag[0])
                    row_broadcast("rb", 1, 4, diag[1])
                    pe.wait_ge(conv_out, 5)
                    back(("vN", 4), lambda hh: cv[:, hh])
                    for hf in range(2):
                        pairs_product(("qk",), hf, lambda hd, m: ckT[:, hd, m * P:(m + 1) * P], lambda hd, m: cqT[:, hd, m * P:(m + 1) * P])
                if c == 23:
                    for hf in range(2):
                        back(("kN", hf), lambda hh: ckT[:, 4 * hf + hh])
                if c == 24:
                    for hf in range(2):
                        pe.wait_ge(xt0, hf + 1)
                        g = tps.name[("x0", hf)]
                        open_group(g)
                        for hh, m, hd in mats(hf):
                            mm = pe.transpose(tpf(g)[:, (2 * hh + m) * P:(2 * hh + m + 1) * P], xT[:, hd, m], ident)
                        mm.then_inc(tp_done, 1)
                for l in range(1, 6):
                    if c == 23 + 2 * l:
                        for hf in range(2):
                            if l == 1:
                                tps.wait(pe, tps.name[("x0", hf)])
                                tps.wait(pe, tps.name[("rb", hf)])
                            else:
                                tps.wait(pe, tps.name[("D", l - 1, hf)])
                            pairs_product(("P", l), hf, lambda hd, m: nT[:, hd, m], lambda hd, m: xn[:, hd, m])
                    if c == 24 + 2 * l:
                        if l == 1:
                            pe.wait_ge(conv_out, 6)
                            back(("vN", 5), lambda hh: cv[:, hh])
                        for hf in range(2):
                            tps.wait(pe, tps.name[("P", l, hf)])
                            if l > 1:
                                tps.wait(pe, tps.name[("DT", l - 1, hf)])
                            if l < 5:
                                pairs_product(("D", l), hf, lambda hd, m: xT[:, hd, m], lambda hd, m: pm[:, hd, m])
                            pairs_product(("DT", l), hf, lambda hd, m: pm[:, hd, m], lambda hd, m: xT[:, hd, m])

            def recurrence(c):
                for cs in range(4):
                    m, part = cs // 2, slice(64 * (cs % 2), 64 * (cs % 2) + 64)
                    toks = slice(64 * cs, 64 * cs + 64)

                    def heads(name, rows_, lhs, rhs):
                        g = tps.name[name]
                        open_group(g)
                        for hd in range(8):
                            mm = pe.matmul(tpf(g)[rows_, hd * P:(hd + 1) * P], lhs(hd), rhs(hd), start=True, stop=True)
                        mm.then_inc(tp_done, 1)

                    if c == 35 + 3 * cs and cs:
                        tps.wait(pe, tps.name[("up", cs - 1)])
                        heads(("kS", cs), part, lambda hd: ckT[:, hd, toks], lambda hd: state[:, hd])
                        heads(("qS", cs), part, lambda hd: cqT[:, hd, toks], lambda hd: state[:, hd])
                    if c == 36 + 3 * cs:
                        if cs:
                            pe.wait_ge(rv_ready, cs)
                        else:
                            for hf in range(2):
                                tps.wait(pe, tps.name[("DT", 5, hf)])
                            tps.wait(pe, tps.name[("vN", 5)])
                        heads(("Xr", cs), part, lambda hd: xT[part, hd, m, part],
                              lambda hd: rv[part, hd] if cs else vb[part, m, hd * P:(hd + 1) * P])
                    if c == 37 + 3 * cs:
                        tps.wait(pe, tps.name[("Xr", cs)])
                        heads(("in", cs), part, lambda hd: qkT[part, hd, m, part], lambda hd: rv[part, hd])
                        if cs < 3:
                            heads(("up", cs), slice(0, P), lambda hd: kdec[part, m, hd * P:(hd + 1) * P], lambda hd: rv[part, hd])

            def attention_side(c):
                if c == 47:
                    for k in range(2):
                        g = tps.name[("sz", k)]
                        open_group(g)
                        tps.wait(pe, tps.name["sbqT"])
                        tps.wait(pe, tps.name["sbkT"])
                        for j in range(2):
                            hd, f = 2 * k + j, tpf(g)[:, j * N:(j + 1) * N]
                            pe.matmul(f[:, 0:SEQ], sbk[:, hd, 0:P], sbq[:, hd, :], start=True, stop=True)
                            mm = pe.matmul(f[:, SEQ:3 * P], sbk[:, hd, P:SEQ], sbq[:, hd, P:SEQ], start=True, stop=True)
                        mm.then_inc(tp_done, 1)
                if c == 48:
                    accs.wait(pe, accs.name["swq"])
                    transposes(tps.name["swqT"], nat[:, 1])
                if c == 49:
                    for k in range(2):
                        g = tps.name[("rev", k)]
                        open_group(g)
                        pe.wait_ge(sp_ready, 1)
                        for j in range(2):
                            hd, f = 2 * k + j, tpf(g)[:, j * N:(j + 1) * N]
                            pe.matmul(f[:, 0:P], tri[:], sp_[:, hd, 0:P], start=True, stop=True)
                            pe.matmul(f[:, P:SEQ], tri[:], sp_[:, hd, P:SEQ], start=True, stop=False)
                            pe.matmul(f[:, P:SEQ], ones, sp_[:, hd, SEQ:3 * P], start=False, stop=True)
                            mm = pe.matmul(f[:, SEQ:3 * P], tri[:], sp_[:, hd, SEQ:3 * P], start=True, stop=True)
                        mm.then_inc(tp_done, 1)
                if c == 50:
                    g = tps.name["swkT"]
                    open_group(g)
                    accs.wait(pe, accs.name["swkv"])
                    for m in range(M):
                        mm = pe.transpose(tpf(g)[:, m * P:(m + 1) * P], nat[:, 0, m, 0:P], ident)
                    mm.then_inc(tp_done, 1)
                    g = tps.name["so"]
                    open_group(g)
                    pe.wait_ge(a_exp, 2)
                    for hd in range(4):
                        cols_, f = slice(hd * P, (hd + 1) * P), tpf(g)
                        pe.matmul(f[:, hd * P:(hd + 1) * P], zm[:, hd, 0:P], sbv[:, 0, cols_], start=True, stop=True)
                        pe.matmul(f[:, N + hd * P:N + (hd + 1) * P], zm[:, hd, P:SEQ], sbv[:, 0, cols_], start=True, stop=False)
                        mm = pe.matmul(f[:, N + hd * P:N + (hd + 1) * P], zm[:, hd, SEQ:3 * P], sbv[:, 1, cols_], start=False, stop=True)
                    mm.then_inc(tp_done, 1)
                if c in (51, 52):
                    for k in (2 * (c - 51), 2 * (c - 51) + 1):
                        g = tps.name[("ws", k)]
                        open_group(g)
                        if k == 0:
                            tps.wait(pe, tps.name["swqT"])
                            tps.wait(pe, tps.name["swkT"])
                        for j in range(2):
                            hd, f = 2 * k + j, tpf(g)[:, j * N:(j + 1) * N]
                            part = slice(64 * (hd // 4), 64 * (hd // 4) + 64)
                            pe.matmul(f[:, 0:P], swq[part, hd % 4, 0:P], swk[part, 0:P], start=True, stop=True)
                            mm = pe.matmul(f[:, P:3 * P], swq[part, hd % 4, P:SEQ], swk[part, :], start=True, stop=True)
                        mm.then_inc(tp_done, 1)
                if c == 52:
                    tps.wait(pe, tps.name["so"])
                    transposes(tps.name["ysbT"], ysb)
                if c == 54:
                    pe.wait_ge(sw_exp, 1)
                    for k in range(3):
                        g = tps.name[("wp", k)]
                        open_group(g)
                        for j in range(8):
                            hd, b = divmod(8 * k + j, 3)
                            mm = pe.transpose(tpf(g)[:, j * P:(j + 1) * P], sw[:, hd, b * P:(b + 1) * P], ident)
                        mm.then_inc(tp_done, 1)
                if c == 55:
                    g = tps.name["wo_"]
                    open_group(g)
                    for k in range(3):
                        tps.wait(pe, tps.name[("wp", k)])
                    for hd in range(8):
                        f, cols_ = tpf(g), slice(64 * (hd // 4), 64 * (hd // 4) + 64)
                        pe.matmul(f[:, 64 * hd:64 * hd + 64], pT[:, 3 * hd], swv[:, 0, cols_], start=True, stop=True)
                        pe.matmul(f[:, N + 64 * hd:N + 64 * hd + 64], pT[:, 3 * hd + 1], swv[:, 0, cols_], start=True, stop=False)
                        mm = pe.matmul(f[:, N + 64 * hd:N + 64 * hd + 64], pT[:, 3 * hd + 2], swv[:, 1, cols_], start=False, stop=True)
                    mm.then_inc(tp_done, 1)
                if c == 57:
                    tps.wait(pe, tps.name["wo_"])
                    transposes(tps.name["yswaT"], yswa)
                if c in (58, 59):
                    pe.wait_ge(y_done, 1)
                    transposes(tps.name[("ydnT", c - 58)], vb[:, :, (c - 58) * N:(c - 57) * N])

            norm(3)
            for c in range(50):
                if c < 48:
                    b, q = divmod(c, 4)
                    if c < 4:
                        tps.wait(pe, tps.name[("norm", 3, c)])
                    chunk(C_2 + c, X, 4 * q, accs.name[("dn", 0)] + b, q == 0, q == 3)
                else:
                    chunk(C_2 + c, X, 8 * (c - 48), accs.name["swkv"], c == 48, c == 49, n_k=8, width=256)
                if c in (36, 40):
                    accs.wait(pe, accs.name["sbq" if c == 36 else "sbk"])
                    transposes(tps.name["sbqT" if c == 36 else "sbkT"], nat[:, c // 4 % 2 ^ 1])
                dn_side(c)
                recurrence(c)
                attention_side(c)
            for nb in range(NB):
                for j in range(16):
                    c = 50 + 16 * nb + j
                    br, first, k0 = BRANCH[j]
                    if j == first + 4:
                        chunk(C_2 + c, A, k0, accs.name[("br", nb, br)], True, br != "dn")
                    elif j == first + 5:
                        chunk(C_2 + c, A, k0 + 4, accs.name[("br", nb, br)], False, True)
                    else:
                        q = j - first
                        chunk(C_2 + c, X, 4 * q, accs.name[("gate", nb, br)], q == 0, q == 3)
                    if nb == 0:
                        attention_side(c)
                        if j == 3:
                            tps.wait(pe, tps.name["ysbT"])
                        if j == 8:
                            tps.wait(pe, tps.name["yswaT"])
                        if j == 13:
                            tps.wait(pe, tps.name[("ydnT", 0)])
                            tps.wait(pe, tps.name[("ydnT", 1)])
                    elif j == 0:
                        pe.wait_ge(mg_ready, 2 * nb)
                        transposes(tps.name[("mT", nb - 1)], mg[(nb - 1) % 2])
            for c in range(16):
                b, q = divmod(c, 4)
                if b == 0:
                    tps.wait(pe, tps.name[("mT", q)])
                chunk(C_WO + c, (m_hi, m_lo), 4 * q, accs.name[("wo", b)], q == 0, q == 3)
                if c == 0:
                    pe.wait_ge(mg_ready, 2 * NB)
                    transposes(tps.name[("mT", 3)], mg[1])
                if 7 <= c < 11:
                    norm_part(4, c - 7)
            for c in range(8):
                b, q = divmod(c, 4)
                if b == 0:
                    tps.wait(pe, tps.name[("norm", 4, q)])
                chunk(C_X + c, A, 4 * q, accs.name["xk"] + b, q == 0, q == 3)
                if c < 4:
                    norm_part(5, c)
                if c == 4:
                    accs.wait(pe, accs.name["xk"])
                    transposes(tps.name["xkT"], nat[:, 0])
            for q in range(4):
                tps.wait(pe, tps.name[("norm", 5, q)])
                chunk(C_X + 8 + q, X, 4 * q, accs.name["xq"], q == 0, q == 3)
            accs.wait(pe, accs.name["xq"])
            transposes(tps.name["xqT"], nat[:, 1])
            tps.wait(pe, tps.name["xqT"])
            tps.wait(pe, tps.name["xkT"])
            for m in range(M):
                g = tps.name[("xs", m)]
                open_group(g)
                for hd in range(4):
                    mm = pe.matmul(tp[:, g % 2, hd], xqT[:, hd, m * P:(m + 1) * P], xkT[:, hd], start=True, stop=True)
                mm.then_inc(tp_done, 1)
            for m in range(M):
                g = tps.name[("xpT", m)]
                open_group(g)
                tps.wait(pe, tps.name[("xs", m)])
                for hd in range(4):
                    for b in range(2):
                        mm = pe.transpose(tpf(g)[:, (2 * hd + b) * P:(2 * hd + b + 1) * P], xp[:, m, hd, b * P:(b + 1) * P], ident)
                mm.then_inc(tp_done, 1)
            g = tps.name["xo_"]
            open_group(g)
            for m in range(M):
                tps.wait(pe, tps.name[("xpT", m)])
                for hd in range(4):
                    for b in range(2):
                        mm = pe.matmul(tpf(g)[:, m * N + hd * P:m * N + (hd + 1) * P], xpT[:, m, hd, b],
                                       xv[:, b, hd * P:(hd + 1) * P], start=b == 0, stop=b == 1)
            mm.then_inc(tp_done, 1)
            tps.wait(pe, tps.name["xo_"])
            transposes(tps.name["yxT"], yx)
            tps.wait(pe, tps.name["yxT"])
            for c in range(4):
                chunk(C_XO + c, A, 0, accs.name[("xo", c)], True, True)
            norm(6)
            for n in range(NB):
                tps.wait(pe, tps.name[("norm", 6, n)])
            with pe.Fori(0, 2) as i:
                for c in range(48):
                    b, q = divmod(c, 4)
                    if b == 8:
                        pe.wait_ge(f_lo, at(q + 2, i, 4))
                    chunk(C_FFN + c, A if b >= 8 else X, 4 * q, accs.name[("fg", 0, 0)] + b, q == 0, q == 3, i, 48, 12)
                    if q == 0 and 1 <= b <= 8:
                        accs.wait(pe, accs.name[("fg", 0, 0)] + b - 1, i, 12)
                        transposes(tps.name[("fgT", 0, 0)] + b - 1, nat[:, (b - 1) % 2], i, 8)
            assert opened[0] + 8 == len(tps.who)

        @block.scalar
        def _(act):
            steps = [0]

            def link(ins):
                steps[0] += 1
                ins.then_inc(act_step, 1)
                act.wait_ge(act_step, steps[0])

            def split(c, i=None, step=0):
                act.wait_ge(landed[c % SLOTS], at(16 * (c // SLOTS + 1), i, 4 * step))
                if c >= SLOTS:
                    act.wait_ge(used, at(c - SLOTS + 1, i, step))
                act.activation(w_hi[:, c % SLOTS], w_raw[:, c % SLOTS], ACT.Copy).then_inc(hi_ready, 1)

            def stats(j, n, src=h, k=0):
                for m in range(M):
                    act.activation(junk[:], src[:, m, n * N:(n + 1) * N], ACT.Square, accum_out=ss[k][:, m, n:n + 1]).then_inc(sq_done[k], 1)
                    act.wait_ge(sq_done[k], 2 * (4 * j + n) + m + 1)

            def scaled(j, n, src=h, k=0):
                if n >= 2:
                    act.wait_ge(tp_done, tps.name[("norm", j, n - 2)] + 1)
                act.activation(nat[:, n % 2, 1], src[:, 1, n * N:(n + 1) * N], ACT.Copy, scale=rstd[k][:, 1:2]).then_inc(xn_act, 1)

            def high(j, n, gains, dst=x_hi):
                g = tps.name[("norm", j, n)]
                act.wait_ge(tp_done, g + 1)
                for q in range(4):
                    t = 4 * n + q
                    ins = act.activation(dst[:, t], tp[:, g % 2, q], ACT.Copy, scale=col[:, gains + t:gains + t + 1])
                ins.then_inc(xh_done, 1)

            def norm(j, gains, ordinal):
                act.wait_ge(rstd_ready[0], ordinal + 1)
                scaled(j, 0)
                scaled(j, 1)
                for n in range(NB):
                    high(j, n, gains)
                    if n + 2 < NB:
                        scaled(j, n + 2)

            def gla_side(c):
                for hd in range(4):
                    if c == 33 + 4 * hd:
                        g = tps.name[("s", hd)]
                        act.wait_ge(tp_done, g + 1)
                        if hd == 0:
                            act.wait_ge(sT_zero, 2)
                        if hd >= 2:
                            act.wait_ge(tp_done, tps.name[("o", hd - 2)] + 1)
                        f = tpf(g)
                        scale = 256 ** -0.5
                        act.activation(sT[0:64, hd % 2], f[0:64, 0:3 * P], ACT.Copy, scale=scale)
                        act.activation(sT[64:P, hd % 2, 64:2 * P], f[64:P, 64:2 * P], ACT.Copy, scale=scale)
                        act.activation(sT[64:P, hd % 2, 2 * P + 64:3 * P], f[64:P, 2 * P + 64:3 * P], ACT.Copy,
                                       scale=scale).then_inc(tps.sem(g), 1)
                    if c == 35 + 4 * hd:
                        act.wait_ge(used, c + 1)
                        if hd >= 2:
                            accs.wait(act, accs.name[("gla", 8 + hd - 2)])
                        else:
                            act.wait_ge(tp_done, tps.name[("gT", 2 + hd)] + 1)
                        act.activation(nat[:, hd % 2].rearrange("p m n -> p (m n)"),
                                       acc[:, hd % 2].rearrange("p m n -> p (m n)"), ACT.Tanh, scale=0.5).then_inc(r_tanh, 1)
                        g = tps.name[("o", hd)]
                        act.wait_ge(tp_done, g + 1)
                        for m in range(M):
                            act.activation(junk[:], tpf(g)[:, m * N:(m + 1) * N], ACT.Square, accum_out=oss[:, hd, m:m + 1]).then_inc(osq, 1)
                            act.wait_ge(osq, 2 * hd + m + 1)
                    if c == 37 + 4 * hd:
                        g = tps.name[("yT", hd)]
                        act.wait_ge(tp_done, g + 1)
                        act.activation(a_hi[:, 4 * hd:4 * hd + 4].rearrange("p k t -> p (k t)"), tpf(g), ACT.Copy).then_inc(ah_done, 1)

            act.wait_ge(x_in, 16)
            for n in range(NB):
                stats(0, n)
            act.wait_ge(gla_in, 48)
            act.activation(wg_hi[:], wg_raw[:], ACT.Copy).then_inc(wg_h, 1)
            act.wait_ge(cols_in, 16)
            norm(0, COL["gla_norm"], 0)
            for c in range(AHEAD):
                split(c)
            for c in range(64):
                split(c + AHEAD)
                if c in (3, 7, 11, 15, 19, 23, 27, 31):
                    n = c // 4
                    act.wait_ge(used, c + 1)
                    if n in (2, 3):
                        act.wait_ge(tp_done, tps.name[("gT", n - 2)] + 1)
                    dst = nat[:, n % 2] if n < 4 else v[:, :, (n - 4) * N:(n - 3) * N]
                    act.activation(dst, acc[:, n % 2], ACT.Copy).then_inc(accs.sem(n), 1)
                if c == 4:
                    g = tps.name["glow"]
                    act.wait_ge(tp_done, g + 1)
                    act.activation(glow[:], tp[:, g % 2].rearrange("p (m z) t -> p m (z t)", m=2)[:, :, 0:16], ACT.Copy).then_inc(tps.sem(g), 1)
                if c == 5:
                    g = tps.name["glowT"]
                    act.wait_ge(tp_done, g + 1)
                    act.activation(glowT[:], tp[0:16, g % 2, 0, :], ACT.Copy).then_inc(tps.sem(g), 1)
                if c in (6, 7):
                    g = tps.name[f"z{c - 6}"]
                    act.wait_ge(tp_done, g + 1)
                    for k in range(4):
                        t = 4 * (c - 6) + k
                        ins = act.activation(zb[:, t], tp[:, g % 2, k], ACT.Identity, bias=col[:, COL["b_gate"] + t:COL["b_gate"] + t + 1])
                    ins.then_inc(tps.sem(g), 1)
                if c == 8:
                    tps.wait(act, tps.name["z0"])
                    tps.wait(act, tps.name["z1"])
                    link(act.activation(ez[:], zb[:], ACT.Abs))
                    link(act.activation(ez[:], ez[:], ACT.Exp, scale=-1.0))
                if c == 9:
                    act.activation(ez[:], ez[:], ACT.Ln, bias=1.0).then_inc(lnz_ready, 1)
                if c == 15:
                    act.wait_ge(la_diff, 1)
                    act.activation(kd[:], kd[:], ACT.Exp, scale=1.0 / 16.0).then_inc(kd_exp, 1)
                    act.wait_ge(e_sum, 1)
                    act.activation(edec[:], edec[:], ACT.Exp, scale=1.0 / 16.0).then_inc(e_exp, 1)
                gla_side(c)
                if c >= 48 and c % 4 == 3:
                    n = (c - 48) // 4
                    accs.wait(act, accs.name[("glaout", n)])
                    stats(1, n)
            norm(1, COL["mlp_norm"], 1)

            def mlp_high(n, i):
                g = tps.name[("aT", 0, n)]
                act.wait_ge(tp_done, at(g + 1, i, 4))
                act.activation(a_hi[:, 4 * n:4 * n + 4].rearrange("p k t -> p (k t)"), tpf(g), ACT.Copy).then_inc(ah_done, 1)

            with act.Fori(0, 4) as i:
                for c in range(32):
                    split(C_MLP + c + AHEAD, i, 32)
                    if c in (3, 7, 11, 15):
                        n = c // 4
                        act.wait_ge(used, at(C_MLP + c + 1, i, 32))
                        act.wait_ge(tp_done, at(tps.name[("aT", 0, n)] - 2 + 1, i, 4))
                        blk = accs.name[("up", 0, n)]
                        act.activation(nat[:, n % 2], acc[:, blk % 2], ACT.Relu).then_inc(accs.sem(blk), 1)
                    if c in (4, 8, 12, 16):
                        mlp_high(c // 4 - 1, i)
            for n in range(NB):
                if n == 0:
                    for k in range(NB):
                        accs.wait(act, accs.name[("down", 3, k)])
                stats(2, n)

            for n in range(NB):
                act.wait_ge(rowdone, n + 1)
                stats(3, n)
            act.wait_ge(dn_in, 48)
            act.activation(wab_hi[:], wab_raw[:], ACT.Copy).then_inc(wab_h, 1)
            norm(3, COL["norm_mix"], 3)

            def evac(name, dst, c, width=N):
                blk = accs.name[name]
                act.wait_ge(used, C_2 + c + 1)
                act.activation(dst, acc[:, blk % 2, :, 0:width], ACT.Copy).then_inc(accs.sem(blk), 1)

            def take(g, dst, src, scale=1.0, s=None):
                act.wait_ge(tp_done, g + 1)
                act.activation(dst, src, ACT.Copy, scale=scale).then_inc(s or tps.sem(g), 1)

            def flat(t):
                return t.rearrange("p k t -> p (k t)")

            def dn_side(c):
                for b in range(6):
                    g = tps.name[("dT", b)]
                    if c == 4 * b + 3:
                        act.wait_ge(tp_done, tps.name[("dT", b - 2) if b >= 2 else ("norm", 3, 2 + b)] + 1)
                        evac(("dn", b), nat[:, b % 2], c)
                    if c == 4 * b + 4:
                        if b:
                            act.wait_ge(conv_out, b)
                        if b == 5:
                            act.wait_ge(tp_done, tps.name[("vN", 4)] + 1)
                        act.wait_ge(tp_done, g + 1)
                        for k in range(4):
                            w = COL["dn_conv"] + 4 * (4 * b + k) + 3
                            ins = act.activation(cv[:, k], tp[:, g % 2, k], ACT.Copy, scale=col[:, w:w + 1])
                        ins.then_inc(conv0, 1)
                    if c == 4 * b + 5:
                        tps.wait(act, g)
                        if 1 <= b <= 4:
                            act.wait_ge(tp_done, tps.name[("ssq", b - 1)] + 1)
                        act.activation(th[:], cv[:], ACT.Tanh, scale=0.5).then_inc(conv_t, 1)
                    if c == 4 * b + 6 and b < 4:
                        act.wait_ge(conv_out, b + 1)
                        src = (cqT if b < 2 else ckT)[:, 4 * (b % 2):4 * (b % 2) + 4]
                        act.activation(th[:], src, ACT.Square).then_inc(conv_sq, 1)
                if c == 3:
                    g = tps.name["ab"]
                    take(g, ab[:], tp[:, g % 2].rearrange("p (m z) t -> p m (z t)", m=2)[:, :, 0:16])
                if c == 4:
                    act.wait_ge(smalls_in, 48)
                    act.wait_ge(u_ready, 1)
                    link(act.activation(l8[:], u8[:], ACT.Abs))
                    link(act.activation(l8[:], l8[:], ACT.Exp, scale=-1.0))
                    act.activation(l8[:], l8[:], ACT.Ln, bias=1.0).then_inc(u_ln, 1)
                    act.activation(nega[:], alog, ACT.Exp).then_inc(a_log, 1)
                    act.activation(beta[:], ab[:, :, 8:16], ACT.Tanh, scale=0.5).then_inc(b_tanh, 1)
                if c == 7:
                    act.wait_ge(ekd_in, 1)
                    act.activation(egc[:], gc[:], ACT.Exp)
                    act.activation(ekd[:], ekd[:], ACT.Exp)
                    act.activation(glb[:], glb[:], ACT.Exp).then_inc(e_gc, 1)
                if c == 12:
                    act.wait_ge(diff_ready, 1)
                    act.activation(dec[:], dec[:], ACT.Exp).then_inc(dec_exp, 1)
                if c == 24:
                    for hf in range(2):
                        tps.wait(act, tps.name[("qk", hf)])
                    for hf in range(2):
                        g = tps.name[("x0", hf)]
                        take(g, xn[:, 4 * hf:4 * hf + 4].rearrange("p h m i -> p (h m i)"), tpf(g))
                for b in range(2):
                    if c == 27 + 4 * b:
                        blk = accs.name[("z", b)]
                        act.wait_ge(used, C_2 + c + 1)
                        act.wait_ge(tp_done, tps.name[("dT", 4 + b)] + 1)
                        act.activation(nat[:, b], acc[:, blk % 2], ACT.Tanh, scale=0.5).then_inc(z_tanh, 1)

            def attention_side(c):
                for cs in range(4):
                    if c == 36 + 3 * cs:
                        part = slice(64 * (cs % 2), 64 * (cs % 2) + 64)
                        g = tps.name[("Xr", cs)]
                        take(g, rv[part].rearrange("p h d -> p (h d)"), tpf(g)[part])
                if c == 35:
                    accs.wait(act, accs.name[("z", 0)])
                    evac("sbq", nat[:, 0], c)
                if c == 39:
                    accs.wait(act, accs.name[("z", 1)])
                    evac("sbk", nat[:, 1], c)
                if c == 43:
                    evac("sbv", sbv[:], c)
                if c == 47:
                    act.wait_ge(tp_done, tps.name["sbkT"] + 1)
                    evac("swq", nat[:, 1], c)
                    act.wait_ge(y_scaled, 1)
                    act.activation(ysq[:], vb[:].rearrange("p m (h d) -> p (m h) d", d=P), ACT.Square).then_inc(y_sq, 1)
                if c == 48:
                    act.wait_ge(zm_ready, 1)
                    link(act.activation(sp_[:], zm[:], ACT.Abs))
                    link(act.activation(sp_[:], sp_[:], ACT.Exp, scale=-1.0))
                    act.activation(sp_[:], sp_[:], ACT.Ln, bias=1.0).then_inc(sp_ln, 1)
                if c == 49:
                    act.wait_ge(used, C_2 + c + 1)
                    blk = accs.name["swkv"]
                    act.activation(swv[:], acc[:, blk % 2, :, P:2 * P], ACT.Copy)
                    evac("swkv", nat[:, 0, :, 0:P], c, P)
                    for k in range(2):
                        tps.wait(act, tps.name[("rev", k)])
                        act.activation(zm[:, 2 * k:2 * k + 2], zm[:, 2 * k:2 * k + 2], ACT.Exp).then_inc(a_exp, 1)
                if c == 50:
                    g = tps.name["so"]
                    take(g, ysb[:].rearrange("p m n -> p (m n)"), tpf(g))
                for slot, name, k0 in ((52, "ysbT", 12), (57, "yswaT", 8), (58, ("ydnT", 0), 0), (59, ("ydnT", 1), 4)):
                    if c == slot:
                        act.wait_ge(y_done, 1)
                        g = tps.name[name]
                        take(g, flat(a_hi[:, k0:k0 + 4]), tpf(g), s=ah_done)
                if c == 53:
                    act.wait_ge(sw_max, 1)
                    for hd in range(8):
                        for m in range(M):
                            part = sw[:, hd, P * m:P * (1 + 2 * m)]
                            act.activation(part, part, ACT.Exp, bias=nmx[:, m, hd:hd + 1], accum_out=rs[:, m, hd:hd + 1])
                    act.activation(es[:], es[:], ACT.Exp).then_inc(sw_exp, 1)
                if c == 54:
                    for k in range(3):
                        g = tps.name[("wp", k)]
                        take(g, flat(pT[:, 8 * k:8 * k + 8]), tpf(g))

            for c in range(50):
                split(C_2 + c + AHEAD)
                dn_side(c)
                attention_side(c)
            for nb in range(NB):
                for j in range(16):
                    c = 50 + 16 * nb + j
                    split(C_2 + c + AHEAD)
                    br, first, _ = BRANCH[j]
                    if j == first + 3:
                        gk = 3 * nb + ("sb", "swa", "dn").index(br)
                        blk = accs.name[("gate", nb, br)]
                        act.wait_ge(used, C_2 + c + 1)
                        if gk < 2:
                            act.wait_ge(tp_done, tps.name["swkT" if gk == 0 else "swqT"] + 1)
                        else:
                            act.wait_ge(mg_ready, 2 * nb - 1 + gk % 3)
                        act.activation(nat[:, gk % 2], acc[:, blk % 2], ACT.Tanh, scale=0.5).then_inc(accs.sem(blk), 1)
                    if nb == 0:
                        attention_side(c)
                    elif j == 0:
                        g = tps.name[("mT", nb - 1)]
                        take(g, flat(m_hi[:, 4 * nb - 4:4 * nb]), tpf(g), 0.5, m_half)
            for c in range(16):
                split(C_WO + c + AHEAD)
                if c == 0:
                    g = tps.name[("mT", 3)]
                    take(g, flat(m_hi[:, 12:16]), tpf(g), 0.5, m_half)
                if 3 <= c < 7:
                    act.wait_ge(mem_in, 16)
                    stats(0, c - 3, memt, 1)
                if 7 <= c < 11:
                    n = c - 7
                    act.wait_ge(rstd_ready[1], 1)
                    scaled(4, n, memt, 1)
                    high(4, n, COL["norm_mem"], a_hi)
                if c % 4 == 3:
                    accs.wait(act, accs.name[("wo", c // 4)])
                    stats(4, c // 4)
            for c in range(12):
                split(C_X + c + AHEAD)
                if c < 4:
                    act.wait_ge(rstd_ready[0], 5)
                    scaled(5, c)
                    high(5, c, COL["norm_xattn"])
                if c == 3:
                    evac("xk", nat[:, 0], C_X - C_2 + c)
                if c == 7:
                    evac("xv", xv[:], C_X - C_2 + c)
                if c == 11:
                    evac("xq", nat[:, 1], C_X - C_2 + c)
            for m in range(M):
                act.wait_ge(x_max, m + 1)
                g = tps.name[("xs", m)]
                for hd in range(4):
                    ins = act.activation(xp[:, m, hd], tp[:, g % 2, hd], ACT.Exp, bias=nmx[:, m, hd:hd + 1],
                                         accum_out=rs[:, m, hd:hd + 1])
                ins.then_inc(tps.sem(g), 1)
            g = tps.name[("xpT", 1)]
            take(g, xpT[:, 1].rearrange("p h b q -> p (h b q)"), tpf(g))
            g = tps.name["yxT"]
            take(g, flat(a_hi[:, 0:4]), tpf(g), s=ah_done)
            for c in range(4):
                split(C_XO + c + AHEAD)
                accs.wait(act, accs.name[("xo", c)])
                stats(5, c)
            norm(6, COL["norm_ffn"], 5)
            base = tps.name[("fgT", 0, 0)]
            with act.Fori(0, 2) as i:
                for c in range(48):
                    split(C_FFN + c + AHEAD, i, 48)
                    b, q = divmod(c, 4)
                    if q == 3 and b < 8:
                        blk = accs.name[("fg", 0, 0)] + b
                        act.wait_ge(used, at(C_FFN + c + 1, i, 48))
                        act.wait_ge(tp_done, at(base + b - 2 + 1, i, 8))
                        act.activation(nat[:, b % 2], acc[:, blk % 2], ACT.Copy).then_inc(accs.sem(blk), 1)
                    if q == 0 and 1 <= b <= 8:
                        b -= 1
                        hb, val = divmod(b, 2)
                        g = base + b
                        dst = fv if val else fg
                        act.wait_ge(tp_done, at(g + 1, i, 8))
                        if b == 0:
                            act.wait_ge(cw_ready, at(1, i, 1))
                        act.wait_ge(f_lo, at(hb + 1, i, 4))
                        for k in range(4):
                            t = 16 * val + 4 * hb + k
                            ins = act.activation(dst[:, k], tp[:, g % 2, k], ACT.Copy, scale=cw[:, t, 2:3])
                        ins.then_inc(conv1, 1)
                        if not val:
                            tps.wait(act, g, i, 8)
                            act.activation(ft[:], fg[:], ACT.Tanh, scale=0.5).then_inc(f_tanh, 1)
                        else:
                            act.wait_ge(p_ready, at(hb + 1, i, 4))
                            act.activation(a_hi[:, 4 * hb:4 * hb + 4], fg[:], ACT.Copy).then_inc(f_hi, 1)
            for n in range(NB):
                accs.wait(act, accs.name[("fdown", 1, n)])
                stats(6, n)

        @block.vector
        def _(dve):
            steps = [0]

            def link(ins, i=None, per=0):
                steps[0] += 1
                ins.then_inc(dve_step, 1)
                dve.wait_ge(dve_step, at(steps[0], i, per))

            def split(c, i=None, step=0):
                dve.wait_ge(hi_ready, at(c + 1, i, step))
                dve.tensor_tensor(w_lo[:, c % SLOTS], w_raw[:, c % SLOTS], w_hi[:, c % SLOTS].bitcast(F32),
                                  ALU.subtract).then_inc(lo_ready, 1)

            def rms(j, k=0):
                dve.wait_ge(sq_done[k], 8 * (j + 1))
                link(dve.tensor_reduce(ms[k][:], ss[k][:], AX.X, ALU.add))
                dve.tensor_scalar(var[k][:], ms[k][:], 1.0 / D, EPS, ALU.mult, ALU.add).then_inc(var_ready[k], 1)
                dve.wait_ge(rstd_ready[k], j + 1)

            def scaled(j, n, src=h, k=0):
                if n >= 2:
                    dve.wait_ge(tp_done, tps.name[("norm", j, n - 2)] + 1)
                dve.tensor_scalar(nat[:, n % 2, 0], src[:, 0, n * N:(n + 1) * N], rstd[k][:, 0:1], None, ALU.mult).then_inc(xn_dve, 1)

            def low_x(j, n, gains, hi=x_hi, lo=x_lo):
                g = tps.name[("norm", j, n)]
                dve.wait_ge(xh_done, NB * (j - (j > 2)) + n + 1)
                for q in range(4):
                    t = 4 * n + q
                    ins = dve.scalar_tensor_tensor(lo[:, t], tp[:, g % 2, q], col[:, gains + t:gains + t + 1],
                                                   hi[:, t].bitcast(F32), ALU.mult, ALU.subtract)
                ins.then_inc(tps.sem(g), 1)

            def norm(j, gains, ordinal):
                rms(ordinal)
                scaled(j, 0)
                scaled(j, 1)
                for n in range(NB):
                    low_x(j, n, gains)
                    if n + 2 < NB:
                        scaled(j, n + 2)

            def normed_rows(ordinal, gain_row, done):
                rms(ordinal)
                for n in range(NB):
                    for m in range(M):
                        hn = h[:, m, n * N:(n + 1) * N]
                        ins = dve.scalar_tensor_tensor(hn, hn, rstd[0][:, m:m + 1], gain_row[:, n * N:(n + 1) * N], ALU.mult, ALU.mult)
                    ins.then_inc(done, 1)

            def add_to_h(name, n, i=None, step=0, last=0, per=0):
                blk = accs.name[name]
                dve.wait_ge(used, at(last + 1, i, step))
                hn = h[:, :, n * N:(n + 1) * N]
                dve.tensor_tensor(hn, acc[:, blk % 2], hn, ALU.add).then_inc(accs.sem(blk), 1)

            def low(g, n, hi_count, i=None, per=0):
                dve.wait_ge(ah_done, at(hi_count, i, per))
                dve.tensor_tensor(a_lo[:, 4 * n:4 * n + 4].rearrange("p k t -> p (k t)"), tpf(g),
                                  a_hi[:, 4 * n:4 * n + 4].rearrange("p k t -> p (k t)").bitcast(F32),
                                  ALU.subtract).then_inc(tps.sem(g), 1)

            def scaled_q(hd):
                if hd:
                    dve.wait_ge(tp_done, tps.name[("s", hd - 1)] + 1)
                pair = 0
                for cs in range(3):
                    later = 3 - cs
                    ins = dve.tensor_tensor(
                        qd[:, :, pair:pair + later, :],
                        qT[:, 2 * hd:2 * hd + 2, 64 * (cs + 1):].rearrange("p k (c t) -> p k c t", t=64),
                        edec[:, 2 * hd:2 * hd + 2, pair:pair + later].unsqueeze(3).to_broadcast([P, 2, later, 64]), ALU.mult)
                    pair += later
                ins.then_inc(qd_ready, 1)

            def gla_side(c):
                for hd in range(4):
                    cols = slice(hd * N, (hd + 1) * N)
                    if hd and c == 30 + 4 * hd:
                        scaled_q(hd)
                    if c == 35 + 4 * hd:
                        blk = accs.name[("gla", 8 + hd)]
                        dve.wait_ge(r_tanh, hd + 1)
                        dve.scalar_tensor_tensor(sr[:, :, cols], nat[:, hd % 2], 1.0, acc[:, blk % 2], ALU.add, ALU.mult).then_inc(accs.sem(blk), 1)
                        accs.wait(dve, blk)
                        link(dve.scalar_tensor_tensor(sr[:, :, cols], sr[:, :, cols], 0.5,
                                                      onorm[:].unsqueeze(1).to_broadcast([P, M, N]), ALU.mult, ALU.mult))
                        dve.wait_ge(osq, 2 * hd + 2)
                        dve.tensor_scalar(ovar[:, hd], oss[:, hd], 1.0 / N, EPS, ALU.mult, ALU.add).then_inc(ovar_s, 1)
                        dve.wait_ge(orstd_s, hd + 1)
                        g = tps.name[("o", hd)]
                        for m in range(M):
                            ins = dve.scalar_tensor_tensor(sr[:, m, cols], tpf(g)[:, m * N:(m + 1) * N], orstd[:, hd, m:m + 1],
                                                           sr[:, m, cols], ALU.mult, ALU.mult)
                        ins.then_inc(tps.sem(g), 1)
                    if c == 37 + 4 * hd:
                        low(tps.name[("yT", hd)], hd, hd + 1)

            dve.wait_ge(gla_in, 48)
            dve.wait_ge(wg_h, 1)
            dve.tensor_tensor(wg_lo[:], wg_raw[:], wg_hi[:].bitcast(F32), ALU.subtract).then_inc(wg_l, 1)
            dve.wait_ge(cols_in, 16)
            norm(0, COL["gla_norm"], 0)
            for c in range(AHEAD):
                split(c)
            dve.wait_ge(cst_in, 32)
            cum_c = cum[:].rearrange("p t (c s) -> p (t c) s", s=64)
            tot = cum[:].rearrange("p t (c s) -> p t c s", s=64)[:, :, :, 63]
            for c in range(64):
                split(c + AHEAD)
                if c in (4, 8, 12, 16):
                    n = c // 4 - 1
                    g = tps.name[("gT", n)]
                    dve.wait_ge(tp_done, g + 1)
                    dst = (qT if n < 2 else kT)[:, 4 * (n % 2):4 * (n % 2) + 4].rearrange("p k t -> p (k t)")
                    dve.tensor_copy(dst, tpf(g)).then_inc(tps.sem(g), 1)
                if c == 10:
                    dve.wait_ge(lnz_ready, 1)
                    link(dve.scalar_tensor_tensor(zb[:], zb[:], 0.0, ez[:], ALU.min, ALU.subtract))
                if c in (11, 12, 13, 14):
                    for t in (2 * (c - 11), 2 * (c - 11) + 1):
                        link(dve.tensor_tensor_scan(cum[:, t], mask01[:], zb[:, t], 0.0, ALU.mult, ALU.add))
                if c == 14:
                    dve.tensor_tensor(kd[:].rearrange("p t (c s) -> p (t c) s", s=64),
                                      cum_c[:, :, 63:64].to_broadcast([P, 32, 64]), cum_c, ALU.subtract).then_inc(la_diff, 1)
                if c == 15:
                    for pair, k in ((0, 1), (3, 2), (5, 3)):
                        ins = dve.tensor_copy(edec[:, :, pair], tot[:, :, k])
                    dve.tensor_tensor(edec[:, :, 4], tot[:, :, 2], tot[:, :, 3], ALU.add)
                    link(dve.tensor_tensor(edec[:, :, 1], tot[:, :, 1], tot[:, :, 2], ALU.add))
                    dve.tensor_tensor(edec[:, :, 2], edec[:, :, 1], tot[:, :, 3], ALU.add).then_inc(e_sum, 1)
                if c == 18:
                    dve.wait_ge(kd_exp, 1)
                    tps.wait(dve, tps.name[("gT", 3)])
                    link(dve.tensor_tensor(kT[:], kT[:], kd[:], ALU.mult))
                    dve.memset(sT[64:P, :, 0:64], 0.0).then_inc(sT_zero, 1)
                    dve.memset(sT[64:P, :, 2 * P:2 * P + 64], 0.0).then_inc(sT_zero, 1)
                if c == 19:
                    dve.wait_ge(e_exp, 1)
                    scaled_q(0)
                gla_side(c)
                if c >= 48 and c % 4 == 3:
                    add_to_h(("glaout", (c - 48) // 4), (c - 48) // 4, last=c)
            norm(1, COL["mlp_norm"], 1)
            with dve.Fori(0, 4) as i:
                for c in range(32):
                    split(C_MLP + c + AHEAD, i, 32)
                    if c in (3, 7, 11, 15):
                        n = c // 4
                        blk = accs.name[("up", 0, n)]
                        accs.wait(dve, blk, i, 8)
                        dve.tensor_tensor(nat[:, n % 2], nat[:, n % 2], nat[:, n % 2], ALU.mult).then_inc(a_sq, 1)
                    if c in (4, 8, 12, 16):
                        n = c // 4 - 1
                        low(tps.name[("aT", 0, n)], n, 4 + n + 1, i, 4)
                    if c >= 16 and c % 4 == 3:
                        n = c // 4 - 4
                        add_to_h(("down", 0, n), n, i, 32, C_MLP + c)
            dve.wait_ge(row_in, 16)
            normed_rows(2, frow, rowdone)

            dve.wait_ge(wab_h, 1)
            dve.tensor_tensor(wab_lo[:], wab_raw[:], wab_hi[:].bitcast(F32), ALU.subtract).then_inc(wab_l, 1)
            norm(3, COL["norm_mix"], 3)

            def taken(g, ins):
                ins.then_inc(tps.sem(g), 1)
                tps.wait(dve, g)

            def mat4(t):
                return t.rearrange("p h m i -> p (h m) i")

            def per_mat(t, hf=None):
                t = t[:] if hf is None else t[:, :, 4 * hf:4 * hf + 4]
                return t.rearrange("p m h -> p h m").unsqueeze(3).to_broadcast([P, t.shape[2], M, P])

            def flat(t):
                return t.rearrange("p k t -> p (k t)")

            def group4(g):
                return tpf(g).rearrange("p (h m i) -> p h m i", h=4, m=M)

            def dn_side(c):
                for b in range(6):
                    g = tps.name[("dT", b)]
                    if c == 4 * b + 4:
                        dve.wait_ge(conv0, b + 1)
                        for sh in (1, 2, 3):
                            for k in range(4):
                                w = COL["dn_conv"] + 4 * (4 * b + k) + 3 - sh
                                ins = dve.scalar_tensor_tensor(cv[:, k, sh:], tp[:, g % 2, k, 0:SEQ - sh], col[:, w:w + 1],
                                                               cv[:, k, sh:], ALU.mult, ALU.add)
                            if sh < 3:
                                link(ins)
                        ins.then_inc(tps.sem(g), 1)
                    if c == 4 * b + 5:
                        dve.wait_ge(conv_t, b + 1)
                        dst = cv[:] if b >= 4 else (cqT, ckT)[b // 2][:, 4 * (b % 2):4 * (b % 2) + 4]
                        dve.scalar_tensor_tensor(flat(dst), flat(th[:]), 1.0, flat(cv[:]), ALU.add, ALU.mult).then_inc(conv_out, 1)
                    if c == 4 * b + 6 and b < 4:
                        g = tps.name[("ssq", b)]
                        dst = ssq if b < 2 else ssk
                        dve.wait_ge(tp_done, g + 1)
                        taken(g, dve.tensor_copy(dst[:, :, 4 * (b % 2):4 * (b % 2) + 4], tpf(g)[:, 0:8].rearrange("p (m h) -> p m h", m=M)))
                        if b % 2:
                            dve.tensor_scalar(dst[:], dst[:], 4.0 * EPS, None, ALU.add).then_inc(ss_ready, 1)
                if c == 4:
                    tps.wait(dve, tps.name["ab"])
                    dve.wait_ge(smalls_in, 48)
                    dve.tensor_tensor(u8[:], ab[:, :, 0:8], dtb.unsqueeze(1).to_broadcast([P, M, 8]), ALU.add).then_inc(u_ready, 1)
                if c == 5:
                    dve.wait_ge(u_ln, 1)
                    dve.wait_ge(a_log, 1)
                    link(dve.scalar_tensor_tensor(g8[:], u8[:], 0.0, l8[:], ALU.max, ALU.add))
                    dve.scalar_tensor_tensor(g8[:], g8[:], -1.0, nega[:].unsqueeze(1).to_broadcast([P, M, 8]), ALU.mult, ALU.mult).then_inc(g_ready, 1)
                    dve.wait_ge(b_tanh, 1)
                    link(dve.tensor_scalar(beta[:], beta[:], 0.5, 0.5, ALU.mult, ALU.add))
                    link(dve.tensor_scalar(betah[:], beta[:], 0.5, None, ALU.mult))
                if c == 6:
                    g = tps.name["gc"]
                    dve.wait_ge(tp_done, g + 1)
                    f = tpf(g)
                    dve.tensor_copy(gc[:].rearrange("p m h -> p (m h)"), f[:, 0:16])
                    dve.tensor_copy(gl[:].rearrange("p m h -> p (m h)"), f[:, 16:32])
                    glb_m = glb[:].rearrange("p (m c) h -> p m c h", c=2)
                    dve.tensor_copy(glb_m[:, :, 0], f[:, N:N + 16].rearrange("p (m h) -> p m h", m=M))
                    taken(g, dve.tensor_copy(glb_m[:, :, 1], f[:, 32:48].rearrange("p (m h) -> p m h", m=M)))
                    dve.tensor_tensor(ekd[:], gl[:], gc[:], ALU.subtract).then_inc(ekd_in, 1)
                ident_b = ident.unsqueeze(1).to_broadcast([P, 8, P])

                def diagonal(hf, t, dst):
                    dve.tensor_tensor(dst[:], ident.unsqueeze(1).unsqueeze(1).to_broadcast([P, 4, M, P]), per_mat(t, hf),
                                      ALU.mult).then_inc(dg_ready, 1)

                if c == 9:
                    diagonal(0, gc, diag[0])
                if c in (10, 11):
                    hf = c - 10
                    g = tps.name[("rg", hf)]
                    dve.wait_ge(tp_done, g + 1)
                    if hf == 0:
                        diagonal(1, gc, diag[0])
                    taken(g, dve.tensor_tensor(dec[:, 4 * hf:4 * hf + 4], group4(g), per_mat(gc, hf), ALU.subtract))
                    if hf:
                        dve.tensor_scalar(dec[:], dec[:], 0.0, None, ALU.min).then_inc(diff_ready, 1)
                if c == 13:
                    dve.wait_ge(dec_exp, 1)
                    dve.tensor_tensor(mat4(dec[:]), mat4(dec[:]), tri_c[:].unsqueeze(1).to_broadcast([P, 16, P]), ALU.mult).then_inc(tri_used, 1)
                if c == 19:
                    dve.wait_ge(r_pow, 2)
                    dve.wait_ge(e_gc, 1)
                    link(dve.tensor_tensor(brk[:], beta[:], rk[:], ALU.mult))
                    dve.scalar_tensor_tensor(nber[:], brk[:], -1.0, egc[:], ALU.mult, ALU.mult)
                    dve.tensor_tensor(kds[:], rk[:], ekd[:], ALU.mult)
                    link(dve.tensor_scalar(qsc[:], rq[:], 128 ** -0.5, None, ALU.mult))
                if c == 20:
                    dve.wait_ge(tri_used, 1)
                    link(dve.tensor_tensor(dec[:], dec[:], per_mat(rk), ALU.mult))
                if c == 21:
                    diagonal(0, brk, diag[0])
                    diagonal(1, brk, diag[1])
                    for hf in range(2):
                        g = tps.name[("kk", hf)]
                        dve.wait_ge(tp_done, g + 1)
                        taken(g, dve.tensor_tensor(nT[:, 4 * hf:4 * hf + 4], group4(g), dec[:, 4 * hf:4 * hf + 4], ALU.mult))
                if c == 22:
                    for hf in range(2):
                        g = tps.name[("rb", hf)]
                        dve.wait_ge(tp_done, g + 1)
                        taken(g, dve.tensor_tensor(nT[:, 4 * hf:4 * hf + 4], group4(g), nT[:, 4 * hf:4 * hf + 4], ALU.mult))
                if c == 22 or c == 26:
                    b = 4 if c == 22 else 5
                    g = tps.name[("vN", b)]
                    hs = slice(4 * b - 16, 4 * b - 12)
                    dve.wait_ge(tp_done, g + 1)
                    dve.tensor_tensor(vb[:, :, hs.start * P:hs.stop * P].rearrange("p m (h d) -> p m h d", d=P),
                                      tpf(g).rearrange("p (m h d) -> p m h d", m=M, h=4),
                                      betah[:, :, hs].unsqueeze(3).to_broadcast([P, M, 4, P]), ALU.mult).then_inc(tps.sem(g), 1)
                if c == 22:
                    for hf in range(2):
                        g = tps.name[("qk", hf)]
                        dve.wait_ge(tp_done, g + 1)
                        dve.tensor_tensor(qkT[:, 4 * hf:4 * hf + 4], group4(g), dec[:, 4 * hf:4 * hf + 4], ALU.mult).then_inc(tps.sem(g), 1)
                if c == 23:
                    for hf in range(2):
                        g = tps.name[("kN", hf)]
                        dve.wait_ge(tp_done, g + 1)
                        dve.tensor_tensor(kdec[:, :, hf * N:(hf + 1) * N].rearrange("p m (h d) -> p m h d", d=P),
                                          tpf(g).rearrange("p (m h d) -> p m h d", m=M, h=4),
                                          kds[:, :, 4 * hf:4 * hf + 4].unsqueeze(3).to_broadcast([P, M, 4, P]), ALU.mult).then_inc(tps.sem(g), 1)
                    for hf in range(2):
                        hs = slice(4 * hf, 4 * hf + 4)
                        link(dve.tensor_tensor(mat4(xT[:, hs]), mat4(nT[:, hs]), lvl[:, 0].unsqueeze(1).to_broadcast([P, 8, P]), ALU.mult))
                        dve.tensor_tensor(mat4(xT[:, hs]), ident_b, mat4(xT[:, hs]), ALU.subtract).then_inc(xt0, 1)
                for l in range(1, 6):
                    for hf in range(2):
                        hs = slice(4 * hf, 4 * hf + 4)
                        if c == 23 + 2 * l:
                            g = tps.name[("P", l, hf)]
                            dve.wait_ge(tp_done, g + 1)
                            dve.tensor_tensor(mat4(pm[:, hs]), mat4(group4(g)), lvl[:, l].unsqueeze(1).to_broadcast([P, 8, P]),
                                              ALU.mult).then_inc(tps.sem(g), 1)
                        if c == 24 + 2 * l:
                            for name, x_ in ((("D", l, hf), xn), (("DT", l, hf), xT)):
                                if name in tps.name:
                                    g = tps.name[name]
                                    dve.wait_ge(tp_done, g + 1)
                                    dve.tensor_tensor(x_[:, hs], x_[:, hs], group4(g), ALU.subtract).then_inc(tps.sem(g), 1)
                for b in range(2):
                    if c == 27 + 4 * b:
                        blk = accs.name[("z", b)]
                        dve.wait_ge(z_tanh, b + 1)
                        zb_ = zz[:, :, b * N:(b + 1) * N]
                        dve.scalar_tensor_tensor(zb_, nat[:, b], 1.0, acc[:, blk % 2], ALU.add, ALU.mult).then_inc(accs.sem(blk), 1)
                        accs.wait(dve, blk)
                        for m in range(M):
                            zm_ = zz[:, m, b * N:(b + 1) * N].rearrange("p (h d) -> p h d", d=P)
                            ins = dve.scalar_tensor_tensor(zm_, zm_, 0.5, dnorm.unsqueeze(1).to_broadcast([P, 4, P]), ALU.mult, ALU.mult)
                        link(ins)

            def copied(name, dst, scale=None):
                g = tps.name[name]
                dve.wait_ge(tp_done, g + 1)
                src = tpf(g)[:, 0:dst.shape[1]]
                ins = dve.tensor_copy(dst, src) if scale is None else dve.tensor_scalar(dst, src, scale, None, ALU.mult)
                ins.then_inc(tps.sem(g), 1)

            def recurrence(c):
                if c == 36:
                    copied("sbqT", flat(sbq[:]))
                if c == 40:
                    copied("sbkT", flat(sbk[:]))
                for cs in range(4):
                    m, part = cs // 2, slice(64 * (cs % 2), 64 * (cs % 2) + 64)
                    vrow = vb[part, m].rearrange("p (h d) -> p h d", d=P)

                    def grp(name, rows_=part):
                        g = tps.name[name]
                        dve.wait_ge(tp_done, g + 1)
                        return g, tpf(g)[rows_].rearrange("p (h d) -> p h d", d=P)

                    if cs and c == 35 + 3 * cs:
                        g, f = grp(("kS", cs))
                        taken(g, dve.tensor_tensor(rv[part], f, nber[part, m].unsqueeze(2).to_broadcast([64, 8, P]), ALU.mult))
                        dve.tensor_tensor(rv[part], rv[part], vrow, ALU.add).then_inc(rv_ready, 1)
                        dve.wait_ge(rv_ready, cs)
                        g, f = grp(("qS", cs))
                        taken(g, dve.tensor_tensor(vrow, f, egc[part, m].unsqueeze(2).to_broadcast([64, 8, P]), ALU.mult))
                    if c == 37 + 3 * cs:
                        g, f = grp(("in", cs))
                        if cs:
                            dve.tensor_tensor(vrow, vrow, f, ALU.add).then_inc(tps.sem(g), 1)
                        else:
                            dve.tensor_copy(vrow, f).then_inc(tps.sem(g), 1)
                        if cs < 3:
                            if cs:
                                link(dve.tensor_tensor(state[:], state[:], glb[:, cs].unsqueeze(2).to_broadcast([P, 8, P]), ALU.mult))
                            g, f = grp(("up", cs), slice(0, P))
                            if cs:
                                dve.tensor_tensor(state[:], state[:], f, ALU.add).then_inc(tps.sem(g), 1)
                            else:
                                dve.tensor_copy(state[:], f).then_inc(tps.sem(g), 1)

            def attention_side(c):
                y16 = vb[:].rearrange("p m (h d) -> p (m h) d", d=P)

                if c == 47:
                    tps.wait(dve, tps.name[("in", 3)])
                    dve.tensor_tensor(y16, y16, qsc[:].rearrange("p m h -> p (m h)").unsqueeze(2).to_broadcast([P, 16, P]), ALU.mult).then_inc(y_scaled, 1)
                    dve.wait_ge(amask_in, 16)
                    for k in range(2):
                        g = tps.name[("sz", k)]
                        dve.wait_ge(tp_done, g + 1)
                        taken(g, dve.scalar_tensor_tensor(zm[:, 2 * k:2 * k + 2], tpf(g).rearrange("p (j n) -> p j n", j=2)[:, :, 0:3 * P],
                                                          128 ** -0.5, amask[:, 0].unsqueeze(1).to_broadcast([P, 2, 3 * P]), ALU.mult, ALU.add))
                    dve.tensor_copy(ms[1][:], mhalf[:, 0:M]).then_inc(zm_ready, 1)
                if c == 48:
                    copied("swqT", flat(swq[:]), 0.125)
                    dve.wait_ge(y_sq, 1)
                    link(dve.tensor_reduce(yss[:].rearrange("p m h -> p (m h)"), ysq[:], AX.X, ALU.add))
                    dve.tensor_scalar(yss[:], yss[:], 1.0 / P, EPS, ALU.mult, ALU.add).then_inc(y_var, 1)
                    dve.wait_ge(sp_ln, 1)
                    dve.scalar_tensor_tensor(sp_[:], zm[:], 0.0, sp_[:], ALU.max, ALU.add).then_inc(sp_ready, 1)
                if c == 49:
                    for k in range(2):
                        g = tps.name[("rev", k)]
                        dve.wait_ge(tp_done, g + 1)
                        dve.tensor_tensor(zm[:, 2 * k:2 * k + 2], zm[:, 2 * k:2 * k + 2],
                                          tpf(g).rearrange("p (j n) -> p j n", j=2)[:, :, 0:3 * P], ALU.subtract).then_inc(tps.sem(g), 1)
                    dve.wait_ge(y_pow, 1)
                    link(dve.tensor_tensor(y16, y16, yrs[:].rearrange("p m h -> p (m h)").unsqueeze(2).to_broadcast([P, 16, P]), ALU.mult))
                    dve.tensor_tensor(vb[:], vb[:], zz[:], ALU.mult).then_inc(y_done, 1)
                if c == 50:
                    copied("swkT", swk[:])
                if c in (51, 52):
                    for k in (2 * (c - 51), 2 * (c - 51) + 1):
                        g = tps.name[("ws", k)]
                        dve.wait_ge(tp_done, g + 1)
                        for j in range(2):
                            hd = 2 * k + j
                            ins = dve.scalar_tensor_tensor(sw[:, hd], amask[:, 1], -(2.0 ** -(hd + 1)), tpf(g)[:, j * N:j * N + 3 * P],
                                                           ALU.mult, ALU.add)
                        taken(g, ins)
                for slot, name, k0, count in ((52, "ysbT", 12, 21), (57, "yswaT", 8, 22), (58, ("ydnT", 0), 0, 23), (59, ("ydnT", 1), 4, 24)):
                    if c == slot:
                        low(tps.name[name], k0 // 4, count)
                if c == 52:
                    dve.tensor_reduce(mx[:, 0], sw[:, :, 0:P], AX.X, ALU.max)
                    link(dve.tensor_reduce(mx[:, 1], sw[:, :, P:3 * P], AX.X, ALU.max))
                    sink_b = sinks.unsqueeze(1).to_broadcast([P, M, 8])
                    link(dve.tensor_tensor(mx[:], mx[:], sink_b, ALU.max))
                    dve.tensor_tensor(es[:], sink_b, mx[:], ALU.subtract)
                    dve.tensor_scalar(nmx[:], mx[:], -1.0, None, ALU.mult).then_inc(sw_max, 1)
                if c == 54:
                    dve.wait_ge(sw_exp, 1)
                    link(dve.tensor_tensor(rs[:], rs[:], es[:], ALU.add))
                    link(dve.reciprocal(rden[:], rs[:]))
                if c == 55:
                    g = tps.name["wo_"]
                    dve.wait_ge(tp_done, g + 1)
                    dve.tensor_tensor(yswa[:].rearrange("p m (h d) -> p (m h) d", d=64), tpf(g).rearrange("p (k d) -> p k d", d=64),
                                      rden[:].rearrange("p m h -> p (m h)").unsqueeze(2).to_broadcast([P, 16, 64]), ALU.mult).then_inc(tps.sem(g), 1)

            for c in range(50):
                split(C_2 + c + AHEAD)
                dn_side(c)
                recurrence(c)
                attention_side(c)

            def merged_low(nb):
                g = tps.name[("mT", nb)]
                dve.wait_ge(m_half, nb + 1)
                dve.scalar_tensor_tensor(flat(m_lo[:, 4 * nb:4 * nb + 4]), tpf(g), 0.5, flat(m_hi[:, 4 * nb:4 * nb + 4]).bitcast(F32),
                                         ALU.mult, ALU.subtract).then_inc(tps.sem(g), 1)

            for nb in range(NB):
                for j in range(16):
                    c = 50 + 16 * nb + j
                    split(C_2 + c + AHEAD)
                    br, first, _ = BRANCH[j]
                    if j in (4, 9, 15):
                        gk = 3 * nb + (4, 9, 15).index(j)
                        gate, blk = accs.name[("gate", nb, br)], accs.name[("br", nb, br)]
                        dve.wait_ge(used, C_2 + c + 1)
                        accs.wait(dve, gate)
                        t = nat[:, gk % 2]
                        dve.scalar_tensor_tensor(t, t, 1.0, acc[:, blk % 2], ALU.add, ALU.mult).then_inc(accs.sem(blk), 1)
                        accs.wait(dve, blk)
                        if br == "swa":
                            if nb >= 2:
                                dve.wait_ge(tp_done, tps.name[("mT", nb - 2)] + 1)
                            dve.tensor_tensor(mg[nb % 2][:], nat[:, 0], nat[:, 1], ALU.add).then_inc(mg_ready, 1)
                        if br == "dn":
                            dve.wait_ge(mg_ready, 2 * nb + 1)
                            dve.tensor_tensor(mg[nb % 2][:], mg[nb % 2][:], t, ALU.add).then_inc(mg_ready, 1)
                    if nb == 0:
                        attention_side(c)
                    elif j == 0:
                        merged_low(nb - 1)
            for c in range(16):
                split(C_WO + c + AHEAD)
                if c == 0:
                    merged_low(3)
                if c == 7:
                    rms(0, 1)
                if 7 <= c < 11:
                    scaled(4, c - 7, memt, 1)
                    low_x(4, c - 7, COL["norm_mem"], a_hi, a_lo)
                if c % 4 == 3:
                    add_to_h(("wo", c // 4), c // 4, last=C_WO + c)
            for c in range(12):
                split(C_X + c + AHEAD)
                if c == 0:
                    rms(4)
                if c < 4:
                    scaled(5, c)
                    low_x(5, c, COL["norm_xattn"])
                if c == 4:
                    g = tps.name["xkT"]
                    dve.wait_ge(tp_done, g + 1)
                    dve.tensor_copy(flat(xkT[:]), tpf(g)).then_inc(tps.sem(g), 1)
            g = tps.name["xqT"]
            dve.wait_ge(tp_done, g + 1)
            dve.tensor_scalar(flat(xqT[:]), tpf(g), 128 ** -0.5, None, ALU.mult).then_inc(tps.sem(g), 1)
            for m in range(M):
                g = tps.name[("xs", m)]
                dve.wait_ge(tp_done, g + 1)
                link(dve.tensor_reduce(mx[:, m, 0:4], tp[:, g % 2], AX.X, ALU.max))
                dve.tensor_scalar(nmx[:, m, 0:4], mx[:, m, 0:4], -1.0, None, ALU.mult).then_inc(x_max, 1)
            g = tps.name[("xpT", 0)]
            dve.wait_ge(tp_done, g + 1)
            dve.tensor_copy(xpT[:, 0].rearrange("p h b q -> p (h b q)"), tpf(g)).then_inc(tps.sem(g), 1)
            tps.wait(dve, tps.name[("xs", 1)])
            link(dve.reciprocal(rden[:, :, 0:4], rs[:, :, 0:4]))
            g = tps.name["xo_"]
            dve.wait_ge(tp_done, g + 1)
            dve.tensor_tensor(yx[:].rearrange("p m (h d) -> p m h d", d=P), tpf(g).rearrange("p (m h d) -> p m h d", m=M, h=4),
                              rden[:, :, 0:4].unsqueeze(3).to_broadcast([P, M, 4, P]), ALU.mult).then_inc(tps.sem(g), 1)
            low(tps.name["yxT"], 0, 25)
            for c in range(4):
                split(C_XO + c + AHEAD)
                add_to_h(("xo", c), c, last=C_XO + c)
            norm(6, COL["norm_ffn"], 5)
            dve.memset(ft[:, 0], 0.0).then_inc(f_lo, 1)
            dve.wait_ge(cw_in, 16)
            base = tps.name[("fgT", 0, 0)]
            LINKS = 8
            with dve.Fori(0, 2) as i:
                start = steps[0]
                dve.tensor_copy(cw[:].rearrange("p t s -> p (t s)"), cw_all[:, i]).then_inc(cw_ready, 1)
                for c in range(48):
                    split(C_FFN + c + AHEAD, i, 48)
                    b, q = divmod(c, 4)
                    if q == 0 and 1 <= b <= 8:
                        b -= 1
                        hb, val = divmod(b, 2)
                        g = base + b
                        dst = fv if val else fg
                        if b == 0:
                            dve.wait_ge(cw_ready, at(1, i, 1))
                        dve.wait_ge(conv1, at(b + 1, i, 8))
                        for sh in (1, 2):
                            for k in range(4):
                                t = 16 * val + 4 * hb + k
                                ins = dve.scalar_tensor_tensor(dst[:, k, sh:], tp[:, g % 2, k, 0:SEQ - sh], cw[:, t, 2 - sh:3 - sh],
                                                               dst[:, k, sh:], ALU.mult, ALU.add)
                            if sh == 1:
                                link(ins, i, LINKS)
                        ins.then_inc(tps.sem(g), 1)
                        hcols = slice(4 * hb, 4 * hb + 4)
                        if not val:
                            dve.wait_ge(f_tanh, at(hb + 1, i, 4))
                            dve.scalar_tensor_tensor(flat(fg[:]), flat(ft[:]), 1.0, flat(fg[:]), ALU.add, ALU.mult).then_inc(g_tanh, 1)
                        else:
                            dve.wait_ge(g_tanh, at(hb + 1, i, 4))
                            tps.wait(dve, g, i, 8)
                            dve.scalar_tensor_tensor(flat(fg[:]), flat(fg[:]), 0.5, flat(fv[:]), ALU.mult, ALU.mult).then_inc(p_ready, 1)
                            dve.wait_ge(f_hi, at(hb + 1, i, 4))
                            dve.tensor_tensor(flat(a_lo[:, hcols]), flat(fg[:]), flat(a_hi[:, hcols]).bitcast(F32), ALU.subtract).then_inc(f_lo, 1)
                    if b >= 8 and q == 3:
                        add_to_h(("fdown", 0, b - 8), b - 8, i, 48, C_FFN + c, 12)
                assert steps[0] - start == LINKS
            steps[0] += LINKS
            dve.wait_ge(row2_in, 16)
            normed_rows(6, frow2, o_fin)


def _stream(parts):
    out = []
    for w, width in parts:
        k, n = w.shape
        kt = k // P
        per = CH // width
        a = w.reshape(kt // per, per, P, n // width, width).transpose(3, 0, 2, 1, 4)
        out.append(a.reshape(-1, P, CH))
    return np.concatenate(out, 0)


def _cols(v):
    return np.asarray(v).reshape(-1, P).T


def _shapes():
    r = np.arange(P)
    same = (r[:, None] // 64 == r[None, :] // 64)
    start = np.broadcast_to(np.arange(SEQ) % 64 != 0, (P, SEQ))
    return np.concatenate([np.eye(P), np.ones((P, P)), start, r[:, None] >= r[None, :], same & (r[:, None] <= r[None, :]),
                           same], 1).astype(np.float32)


def _masks():
    from concourse import mybir
    r = np.arange(P)
    i, j = r[:, None], r[None, :]

    def couples(i, j, s):
        return (i // s == j // s + 1) & (i // (2 * s) == j // (2 * s))

    levels = [couples(j, i, 1)] + [couples(i, j, 2 ** l) for l in range(1, 6)]
    before = np.where(i < j, 0.0, -1e30)
    sb = np.concatenate([before, np.zeros((P, P)), before], 1)
    dist = np.concatenate([np.where(i >= j, i - j, 1e30), np.where(j > i, i + P - j, 1e30), np.where(i >= j, i - j, 1e30)], 1)
    return np.concatenate(levels + [sb, dist], 1).astype(mybir.dt.np(mybir.dt.bfloat16))


def kernel(**inputs):
    import concourse.bacc as bacc
    from concourse import mybir
    from concourse.bass_utils import run_bass_kernel_spmd

    a = {k: np.asarray(v) for k, v in inputs.items()}
    w1 = a["gla_w_in"][0]
    up, down = a["mlp_w_up"][0], a["mlp_w_down"][0]
    parts = [(w1[:, :6144], 512), (a["gla_w_out"][0], 512)]
    for g in range(4):
        parts += [(up[:, 2048 * g:2048 * (g + 1)], 512), (down[2048 * g:2048 * (g + 1)], 512)]
    w2 = a["w_in_2"][0]
    at = np.cumsum([0, 3072, 1024, 8, 8, 512, 256, 1536, 6144])
    qkv, z, aw, bw, swq, swkv, sbqkv, gates = [w2[:, at[k]:at[k + 1]] for k in range(8)]
    swq = swq.reshape(D, 2, 4, 64).transpose(0, 2, 1, 3).reshape(D, 512)
    parts += [(qkv, 512), (z, 512), (sbqkv, 512), (swq, 512), (swkv, 256)]
    brs = {"dn": (0, a["w_br_dn_2"][0]), "swa": (1, a["w_br_swa_2"][0]), "sb": (2, a["w_br_sb_2"][0])}
    for nb in range(4):
        for br in ("sb", "swa", "dn"):
            k, wb = brs[br]
            c = slice(512 * nb, 512 * (nb + 1))
            parts += [(gates[:, D * k:D * (k + 1)][:, c], 512), (wb[:, c], 512)]
    parts += [(a["w_o_2"][0], 512), (a["w_xkv_2"][0], 512), (a["w_xq_2"][0], 512), (a["w_xo_2"][0], 512)]
    up2, down2 = a["w_up_2"][0], a["w_down_2"][0]
    for g in range(2):
        for b in range(4):
            c = 2048 * g + 512 * b
            parts += [(up2[:, c:c + 512], 512), (up2[:, 4096 + c:4096 + c + 512], 512)]
        parts += [(down2[2048 * g:2048 * (g + 1)], 512)]
    stream = _stream(parts)
    dn_conv = a["dn_conv_2"][0].reshape(4, 24, P).transpose(2, 1, 0).reshape(P, 96)
    ffn_conv = a["ffn_conv_2"][0].reshape(3, 2, 2, 16, P).transpose(4, 2, 1, 3, 0).reshape(P, 192)
    cols = np.concatenate([_cols(a[k].reshape(-1)) for k in ("gla_norm", "mlp_norm", "gla_b_gate", "norm_mix_2", "norm_xattn_2",
                                                            "norm_mem_2", "norm_ffn_2")] + [dn_conv, ffn_conv], 1)
    rows = np.concatenate([a[k].reshape(-1) for k in ("gla_o_norm", "final_norm", "norm_final_2", "dn_a_log_2", "dn_dt_bias_2",
                                                      "swa_sinks_2", "dn_norm_2")])
    rows = np.broadcast_to(rows, (P, rows.size))
    wglow = w1[:, 6144:].reshape(16, P, 16).transpose(1, 0, 2)
    wab = np.concatenate([aw, bw], 1).reshape(16, P, 16).transpose(1, 0, 2)
    data = {"x": a["x"][0], "mem": a["mem_2"][0], "stream": stream, "cols": cols, "rows": rows, "wglow": wglow, "wab": wab,
            "wgu": a["gla_w_gate_up"][0], "shapes": _shapes(), "masks": _masks()}
    data = {k: np.ascontiguousarray(v) for k, v in data.items()}
    nc = bacc.Bacc("TRN2", target_bir_lowering=False, num_devices=1)
    arrays, args = {}, []
    for name, v in data.items():
        arrays["in_" + name] = v
        args.append(nc.dram_tensor("in_" + name, v.shape, mybir.dt.from_np(v.dtype), kind="ExternalInput").ap())
    out = nc.dram_tensor("out_y", (SEQ, D), mybir.dt.float32, kind="ExternalOutput").ap()
    build(nc, *args, out)
    r = run_bass_kernel_spmd(nc, [arrays], core_ids=[0])
    return r.results[0]["out_y"].reshape(1, SEQ, D)
```

```python
import numpy as np

P = 128
SEQ = 256
M = SEQ // P
D = 2048
CH = 2048
EPS = 1e-6
COLS = {"gla_norm": 0, "mlp_norm": 16, "b_gate": 32, "norm_mix": 40, "norm_xattn": 56, "norm_mem": 72, "norm_ffn": 88,
        "dn_conv": 104, "final_norm": 200}
N_COLS = 200 + 16
BRANCH = [("sb", 0, 12)] * 5 + [("swa", 5, 8)] * 5 + [("dn", 10, 0)] * 6


def build(nc, x, mem, stream, cols, rows, wglow, wab, wgu, shapes, masks, out):
    import concourse.bass as bass
    from concourse import mybir
    from contextlib import ExitStack

    F32, F32R, BF16 = mybir.dt.float32, mybir.dt.float32r, mybir.dt.bfloat16
    ACT, ALU, AX = mybir.ActivationFunctionType, mybir.AluOpType, mybir.AxisListType
    N = 512
    NB = D // N
    SLOTS = 4
    AHEAD = 3
    NCHUNK = stream.shape[0]

    def at(n, i=None, step=0):
        return n if i is None else i * step + n

    with ExitStack() as ctx:
        def sem(name):
            return ctx.enter_context(nc.semaphore(name))

        cursor = [(nc.sbuf_base + 31) // 32 * 32]

        def take(nbytes):
            a = cursor[0]
            cursor[0] += (nbytes + 31) // 32 * 32
            return a

        def sb(name, shape, dt=F32, offset=None):
            nbytes = (2 if dt == BF16 else 4) * int(np.prod(shape[1:]))
            return nc.alloc_sbuf_tensor_at(name, shape, dt, offset=take(nbytes) if offset is None else offset)

        K = 1024
        h = sb("h", [P, M, D])
        a_raw = take(SLOTS * CH * 4)
        w_raw = sb("w_raw", [P, SLOTS, CH], F32, a_raw)
        w_lo = sb("w_lo", [P, SLOTS, CH], F32R, a_raw)
        w_hi = sb("w_hi", [P, SLOTS, CH], F32R)
        x_hi = sb("x_hi", [P, 16, SEQ], F32R)
        x_lo = sb("x_lo", [P, 16, SEQ], F32R)
        a_a = take(32 * K)
        a_hi = sb("a_hi", [P, 16, SEQ], F32R, a_a)
        a_lo = sb("a_lo", [P, 16, SEQ], F32R, a_a + 16 * K)
        nat = sb("nat", [P, 2, M, N])
        col = sb("col", [P, N_COLS])
        consts = sb("consts", [P, 2 * P])
        junk = sb("junk", [P, N], BF16)
        ss = [sb(f"ss{k}", [P, M, NB]) for k in range(2)]
        ms = [sb(f"ms{k}", [P, M]) for k in range(2)]
        var = [sb(f"var{k}", [P, M]) for k in range(2)]
        rstd = sb("rstd", [P, 8, M])
        rhalf = sb("rhalf", [P, 8, M])
        mhalf = sb("mhalf", [P, M * 8])
        a_s = take(48 * K)
        a_z = take(9 * K // 2)
        assert cursor[0] <= nc.sbuf_usable_end, (cursor[0], nc.sbuf_usable_end)
        ident, ones = consts[:, 0:P], consts[:, P:2 * P]

        small_used = [0]

        def small(name, shape, dt=F32):
            nbytes = (2 if dt == BF16 else 4) * int(np.prod(shape[1:]))
            t = sb(name, shape, dt, a_z + small_used[0])
            small_used[0] += (nbytes + 31) // 32 * 32
            assert small_used[0] <= 9 * K // 2, small_used[0]
            return t

        qT = sb("qT", [P, 8, SEQ], F32, a_s)
        kT = sb("kT", [P, 8, SEQ], F32, a_s + 8 * K)
        v = sb("v", [P, M, D], F32, a_s + 16 * K)
        sr = sb("sr", [P, M, D], F32, a_s + 32 * K)
        wg_raw = sb("wg_raw", [P, 16, 16], F32, a_s + 32 * K)
        wg_hi = sb("wg_hi", [P, 16, 16], F32R, a_s + 33 * K)
        wg_lo = sb("wg_lo", [P, 16, 16], F32R, a_s + 34 * K)
        glow = sb("glow", [P, M, 16], F32, a_s + 35 * K)
        glow_rows = sb("glow_rows", [16, SEQ], F32, a_s + 42 * K)
        glowT = sb("glowT", [16, SEQ], F32, a_s + 36 * K)
        w_gu = sb("w_gu", [16, 1024], F32, a_s + 37 * K)
        zb = sb("zb", [P, 8, SEQ], F32, a_a)
        ez = sb("ez", [P, 8, SEQ], F32, a_a + 8 * K)
        cum = sb("cum", [P, 8, SEQ], F32, a_a + 16 * K)
        kd = sb("kd", [P, 8, SEQ], F32, a_a + 24 * K)
        qd = sb("qd", [P, 2, 6, 64], F32, a_a + 12 * K)
        sT = sb("sT", [P, 2, 3 * P], F32, a_a + 28 * K)
        onorm = small("onorm", [P, N])
        mask01 = small("mask01", [P, SEQ])
        edec = small("edec", [P, 8, 6])
        oss = small("oss", [P, 4, M])
        ovar = small("ovar", [P, 4, M])
        orstd = small("orstd", [P, 4, M])
        frow = sb("frow", [P, D], F32, a_s + 16 * K)

        small_used[0] = 0
        tri = small("tri", [P, P])
        lvl = small("lvl", [P, 6, P], BF16)
        row_p = small("row_p", [P, 3 * 8 + P])
        alog, dtb, sinks, dnorm = row_p[:, 0:8], row_p[:, 8:16], row_p[:, 16:24], row_p[:, 24:24 + P]
        ab = small("ab", [P, M, 16])
        (u8, l8, g8, beta, betah, gc, gl, egc, ekd, ssq, ssk, rq, rk, brk, nber, kds, qsc, mx, nmx, rs, es, rden,
         yss, yrs) = [small(n, [P, M, 8]) for n in ("u8", "l8", "g8", "beta", "betah", "gc", "gl", "egc", "ekd", "ssq", "ssk",
                                                  "rq", "rk", "brk", "nber", "kds", "qsc", "mx", "nmx", "rs", "es", "rden",
                                                  "yss", "yrs")]
        nega = small("nega", [P, 8])
        glb = small("glb", [P, 4, 8])
        cqT = sb("cqT", [P, 8, SEQ], F32, a_s)
        ckT = sb("ckT", [P, 8, SEQ], F32, a_s + 8 * K)
        qkT = sb("qkT", [P, 8, M, P], F32, a_s + 16 * K)
        xT = sb("xT", [P, 8, M, P], F32, a_s + 24 * K)
        vb = sb("vb", [P, M, 1024], F32, a_s + 32 * K)
        kdec = sb("kdec", [P, M, 1024], F32, a_s + 40 * K)
        dec = sb("dec", [P, 8, M, P], F32, a_a)
        xn = sb("xn", [P, 8, M, P], F32, a_a)
        nT = sb("nT", [P, 8, M, P], F32, a_a + 16 * K)
        pm = sb("pm", [P, 8, M, P], F32, a_a + 24 * K)
        diag = [sb(f"diag{k}", [P, 4, M, P], F32, a_a + (24 + 4 * k) * K) for k in range(2)]
        tri_c = sb("tri_c", [P, P], F32, a_a + 28 * K)
        same_c = sb("same_c", [P, P], F32, a_a + 28 * K + 512)
        wab_raw = sb("wab_raw", [P, 16, 16], F32, a_a + 29 * K)
        wab_hi = sb("wab_hi", [P, 16, 16], F32R, a_a + 30 * K)
        wab_lo = sb("wab_lo", [P, 16, 16], F32R, a_a + 31 * K)
        ab_rows = sb("ab_rows", [16, SEQ], F32, a_a + 20 * K)
        cv = sb("cv", [P, 4, SEQ], F32, a_a + 8 * K)
        th = sb("th", [P, 4, SEQ], F32, a_a + 12 * K)
        zz = sb("zz", [P, M, 1024], F32, a_a + 8 * K)
        state = sb("state", [P, 8, P], F32, a_a + 24 * K)
        rv = sb("rv", [P, 8, P], F32, a_a + 28 * K)
        ysq = sb("ysq", [P, 16, P], F32, a_s + 16 * K)
        sbq = sb("sbq", [P, 4, SEQ], F32, a_a)
        sbk = sb("sbk", [P, 4, SEQ], F32, a_a + 4 * K)
        sbv = sb("sbv", [P, M, N], F32, a_a + 16 * K)
        swq = sb("swq", [P, 4, SEQ], F32, a_a + 20 * K)
        swk = sb("swk", [P, SEQ], F32, a_s + 40 * K)
        swv = sb("swv", [P, M, P], F32, a_s + 41 * K)
        amask = sb("amask", [P, 2, 3 * P], BF16, a_s + 42 * K)
        zm = sb("zm", [P, 4, 3 * P], F32, a_s)
        sp_ = sb("sp_", [P, 4, 3 * P], F32, a_s + 6 * K)
        ysb = sb("ysb", [P, M, N], F32, a_s + 12 * K)
        sw = sb("sw", [P, 8, 3 * P], F32, a_s + 16 * K)
        yswa = sb("yswa", [P, M, N], F32, a_s + 28 * K)
        pT = sb("pT", [P, 24, P], F32, a_s)
        m_hi = sb("m_hi", [P, 16, SEQ], F32R, a_s)
        m_lo = sb("m_lo", [P, 16, SEQ], F32R, a_s + 16 * K)
        mg = [sb("mg0", [P, M, N], F32, a_s + 44 * K), sb("mg1", [P, M, N], F32, a_s + 40 * K)]
        memt = sb("memt", [P, M, D], F32, a_s + 32 * K)
        xkT = sb("xkT", [P, 4, SEQ], F32, a_s)
        xv = sb("xv", [P, M, N], F32, a_s + 4 * K)
        xqT = sb("xqT", [P, 4, SEQ], F32, a_s + 8 * K)
        xp = sb("xp", [P, M, 4, SEQ], F32, a_s + 12 * K)
        xpT = sb("xpT", [P, M, 4, 2, P], F32, a_s + 20 * K)
        yx = sb("yx", [P, M, N], F32, a_s + 28 * K)
        cw_all = sb("cw_all", [P, 2, 96], F32, a_s + 47 * K)
        cw = sb("cw", [P, 32, 3], F32, a_s + 46 * K)
        fg = sb("fg", [P, 4, SEQ], F32, a_s)
        fv = sb("fv", [P, 4, SEQ], F32, a_s + 4 * K)
        ft = sb("ft", [P, 4, SEQ], F32, a_s + 8 * K)
        frow2 = sb("frow2", [P, D], F32, a_s + 16 * K)

        acc = ctx.enter_context(nc.psum_tensor("acc", [P, 2, M, N], F32))
        tp = ctx.enter_context(nc.psum_tensor("tp", [P, 2, 4, SEQ], F32))

        def tpf(g):
            return tp[:, g % 2].rearrange("p k t -> p (k t)")

        landed = [sem(f"landed{s}") for s in range(SLOTS)]
        hi_ready, lo_ready, used = sem("hi_ready"), sem("lo_ready"), sem("used")
        tp_done = sem("tp_done")
        took = {k: {e: [sem(f"{k}_took_{e}{p}") for p in range(2)] for e in ("act", "dve")} for k in ("acc", "tp")}
        cols_in, cst_in, mask_in, gla_in, row_in, out_done = [sem(s) for s in ("cols_in", "cst_in", "mask_in", "gla_in", "row_in", "out_done")]
        x_in = [sem(f"x_in{n}") for n in range(NB)]
        act_step, dve_step = sem("act_step"), sem("dve_step")
        sq_done, var_ready, rstd_ready = [[sem(f"{n}{k}") for k in range(2)] for n in ("sq_done", "var_ready", "rstd_ready")]
        (dn_in, smalls_in, amask_in, mem_in, cw_in, row2_in, wab_h, wab_l, u_ready, u_ln, b_tanh, g_ready, e_gc,
         conv0, conv1, conv_t, conv_sq, ss_ready, r_pow, dg_ready, diff_ready, dec_exp, xt0, z_tanh, rv_ready,
         y_scaled, y_sq, y_var, y_pow, zm_ready, sp_ln, sp_ready, a_exp, sw_max, sw_exp, g_tanh, mg_ready, p_ready,
         f_tanh, f_hi, cw_ready, x_max, y_done, a_log, o_fin, conv_out, f_lo, ekd_in, m_half, tri_used) = [
            sem(n) for n in (
                "dn_in", "smalls_in", "amask_in", "mem_in", "cw_in", "row2_in", "wab_h", "wab_l", "u_ready", "u_ln",
                "b_tanh", "g_ready", "e_gc", "conv0", "conv1", "conv_t", "conv_sq", "ss_ready", "r_pow", "dg_ready",
                "diff_ready", "dec_exp", "xt0", "z_tanh", "rv_ready", "y_scaled", "y_sq", "y_var", "y_pow",
                "zm_ready", "sp_ln", "sp_ready", "a_exp", "sw_max", "sw_exp", "g_tanh", "mg_ready", "p_ready",
                "f_tanh", "f_hi", "cw_ready", "x_max", "y_done", "a_log", "o_fin", "conv_out", "f_lo", "ekd_in",
                "m_half", "tri_used")]
        xh_done, scale_ready = sem("xh_done"), sem("scale_ready")
        a_sq = sem("a_sq")
        ah_done = sem("ah_done")
        wg_h, wg_l = sem("wg_h"), sem("wg_l")
        brk_ready, dgb_ready = sem("brk_ready"), sem("dgb_ready")
        lnz_ready, la_diff, kd_exp, e_sum, e_exp = [sem(s) for s in ("lnz_ready", "la_diff", "kd_exp", "e_sum", "e_exp")]
        qd_ready, sT_zero, r_tanh = sem("qd_ready"), sem("sT_zero"), sem("r_tanh")
        osq, ovar_s, orstd_s = sem("osq"), sem("ovar_s"), sem("orstd_s")
        mh_set = sem("mh_set")
        rowdone = sem("rowdone")

        class Turns:

            def __init__(self, kind):
                self.sems, self.who, self.name = took[kind], [], {}

            def add(self, name, who):
                self.name[name] = len(self.who)
                self.who.append(who)

            def count(self, n):
                return sum(1 for k in range(n % 2, n + 1, 2) if self.who[k] == self.who[n])

            def sem(self, n):
                return self.sems[self.who[n]][n % 2]

            def wait(self, eng, n, i=None, per=0):
                eng.wait_ge(self.sem(n), at(self.count(n), i, self.count(n + per) - self.count(n) if per else 0))

        accs, tps = Turns("acc"), Turns("tp")

        for n in range(8):
            accs.add(("gla", n), "act")
        for n in range(8, 12):
            accs.add(("gla", n), "dve")
        for n in range(4):
            accs.add(("glaout", n), "dve")
        for g in range(4):
            for n in range(4):
                accs.add(("up", g, n), "act")
            for n in range(4):
                accs.add(("down", g, n), "dve")

        SCALES = {j: k + 1 for k, j in enumerate((0, 1, 3, 4, 5, 6))}
        WO_PARTS = {5: (5, 0), 7: (4, 0), 8: (4, 1), 9: (5, 1), 10: (4, 2), 11: (4, 3), 13: (5, 2)}
        quarter = {}

        def add_quarter(j, n):
            quarter[j, n] = len(quarter)
            tps.add(("norm", j, n), "dve")

        def add_norm(j):
            for n in range(4):
                add_quarter(j, n)

        add_norm(0)
        for name, who in (("glow_rows", "act"), ("glow", "act"), (("gT", 0), "dve"), ("glowT", "act"), ("z0", "act"), ("z1", "act"),
                          (("gT", 1), "dve"), (("gT", 2), "dve"), (("gT", 3), "dve")):
            tps.add(name, who)
        for hd in range(4):
            tps.add(("s", hd), "act")
            tps.add(("o", hd), "dve")
            tps.add(("yT", hd), "dve")
        add_norm(1)
        for g in range(4):
            for n in range(4):
                tps.add(("aT", g, n), "dve")

        for b in range(6):
            accs.add(("dn", b), "act")
        for b in range(2):
            accs.add(("z", b), "dve")
        for name in ("sbq", "sbk", "sbv", "swq", "swkv"):
            accs.add(name, "act")
        for nb in range(NB):
            for br in ("sb", "swa", "dn"):
                accs.add(("gate", nb, br), "act")
                accs.add(("br", nb, br), "dve")
        for n in range(NB):
            accs.add(("wo", n), "dve")
        for name in ("xk", "xq", "xv"):
            accs.add(name, "act")
        for n in range(NB):
            accs.add(("xo", n), "dve")
        for g in range(2):
            for b in range(4):
                accs.add(("fg", g, b), "act")
                accs.add(("fv", g, b), "act")
            for n in range(NB):
                accs.add(("fdown", g, n), "dve")

        def add(*names, who="dve"):
            for name in names:
                tps.add(name, who)

        add_norm(3)
        add("ab_rows", "ab", who="act")
        add(("dT", 0), "gc", ("ssq", 0), ("dT", 1))
        add(("rg", 0), ("ssq", 1), ("rg", 1))
        add(("dT", 2), ("ssq", 2), ("dT", 3), ("ssq", 3))
        add(("dT", 4), ("kk", 0), ("kk", 1), ("rb", 0), ("rb", 1))
        add(("vN", 4), ("qk", 0), ("qk", 1))
        add(("x0", 0), ("x0", 1), who="act")
        add(("dT", 5))
        for l in range(1, 6):
            add(("P", l, 0), ("P", l, 1))
            if l <= 2:
                add(("kN", l - 1))
            if l == 1:
                add(("vN", 5))
            for hf in range(2):
                add(*([("D", l, hf)] if l < 5 else []), ("DT", l, hf))
        for cs in range(4):
            if cs:
                add(("kS", cs), ("qS", cs))
            if cs == 0:
                add("sbqT")
            add(("Xr", cs), who="act")
            if cs == 1:
                add("sbkT")
            add(("in", cs), *([("up", cs)] if cs < 3 else []))
        add(("sz", 0), ("sz", 1))
        add("swqT")
        add(("rev", 0), ("rev", 1))
        add("swkT")
        add("so", who="act")
        add(*[("ws", k) for k in range(4)])
        add("ysbT")
        add(*[("wp", k) for k in range(3)], who="act")
        add("wo_")
        add("yswaT", ("ydnT", 0), ("ydnT", 1))
        for nb in range(NB):
            add(("mT", nb))
        for c in sorted(WO_PARTS):
            add_quarter(*WO_PARTS[c])
        add_quarter(5, 3)
        add("xkT", "xqT")
        add(("xs", 0), ("xs", 1), who="act")
        add(("xpT", 0))
        add(("xpT", 1), who="act")
        add("xo_", "yxT")
        add_norm(6)
        for g in range(2):
            for b in range(4):
                add(("fgT", g, b), ("fvT", g, b))

        C_GLA, C_OUT, C_MLP, C_2 = 0, 48, 64, 192
        C_BR, C_WO, C_X, C_XO, C_FFN = C_2 + 50, C_2 + 114, C_2 + 130, C_2 + 142, C_2 + 146
        assert C_FFN + 96 == NCHUNK
        COL = COLS
        block = ctx.enter_context(nc.Block())

        @block.sync
        def _(sp):
            sp.dma_start(consts[:], shapes[:, 0:2 * P]).then_inc(cst_in, 16)
            sp.dma_start(col[:], cols[:, 0:N_COLS]).then_inc(cols_in, 16)
            for s in range(SLOTS):
                if s < 2:
                    for n in (2 * s, 2 * s + 1):
                        sp.dma_start(h[:, :, n * N:(n + 1) * N], x.rearrange("(m p) n -> p m n", p=P)[:, :, n * N:(n + 1) * N]).then_inc(x_in[n], 16)
                sp.dma_start(w_raw[:, s], stream[s]).then_inc(landed[s], 16)
            sp.dma_start(mask01[:], shapes[:, 2 * P:2 * P + SEQ]).then_inc(mask_in, 16)
            with sp.Fori(0, NCHUNK // SLOTS - 1) as i:
                for s in range(SLOTS):
                    sp.wait_ge(used, i * SLOTS + (s + 1))
                    sp.dma_start(w_raw[:, s], stream[(i + 1) * SLOTS + s]).then_inc(landed[s], 16)
            for c in range(NCHUNK // SLOTS * SLOTS, NCHUNK + AHEAD):
                sp.wait_ge(used, c - SLOTS + 1)
                sp.dma_start(w_raw[:, c % SLOTS], stream[min(c, NCHUNK - 1)]).then_inc(landed[c % SLOTS], 16)
            for n in range(NB):
                sp.wait_ge(o_fin, n + 1)
                sp.dma_start(out.rearrange("(m p) n -> p m n", p=P)[:, :, n * N:(n + 1) * N],
                             h[:, :, n * N:(n + 1) * N]).then_inc(out_done, 16)
            sp.wait_ge(out_done, 16 * NB)

        @block.gpsimd
        def _(pool):
            pool.dma_start(wg_raw[:], wglow).then_inc(gla_in, 16)
            pool.dma_start(w_gu[:], wgu).then_inc(gla_in, 16)
            pool.dma_start(onorm[:], rows[:, 0:N]).then_inc(gla_in, 16)
            pool.memset(mhalf[:], -0.5).then_inc(mh_set, 1)
            pool.wait_ge(mh_set, 1)
            mh8 = mhalf[:].rearrange("p (m h) -> p m h", m=M)

            def norm(j, count, k=0):
                pool.wait_ge(var_ready[k], count)
                pool.tensor_tensor(rstd[:, j], var[k][:], mhalf[:, 0:M], ALU.pow).then_inc(rstd_ready[k], 1)

            norm(0, 1)
            for hd in range(4):
                pool.wait_ge(ovar_s, hd + 1)
                pool.tensor_tensor(orstd[:, hd], ovar[:, hd], mhalf[:, 0:M], ALU.pow).then_inc(orstd_s, 1)
            pool.wait_ge(tp_done, tps.name[("yT", 3)] + 1)
            pool.dma_start(frow[:], rows[:, N:N + D]).then_inc(row_in, 16)
            pool.dma_start(tri[:], shapes[:, 2 * P + SEQ:3 * P + SEQ]).then_inc(smalls_in, 16)
            pool.dma_start(lvl[:], masks[:, 0:6 * P]).then_inc(smalls_in, 16)
            pool.dma_start(row_p[:], rows[:, N + 2 * D:]).then_inc(smalls_in, 16)
            norm(1, 2)
            pool.wait_ge(used, C_2)
            pool.dma_start(tri_c[:], shapes[:, 3 * P + SEQ:4 * P + SEQ]).then_inc(dn_in, 16)
            pool.dma_start(same_c[:], shapes[:, 4 * P + SEQ:5 * P + SEQ]).then_inc(dn_in, 16)
            pool.dma_start(wab_raw[:], wab).then_inc(dn_in, 16)
            norm(2, 3)
            norm(3, 4)
            pool.wait_ge(ss_ready, 1)
            pool.tensor_tensor(rq[:], ssq[:], mh8, ALU.pow).then_inc(r_pow, 1)
            pool.wait_ge(ss_ready, 2)
            pool.tensor_tensor(rk[:], ssk[:], mh8, ALU.pow).then_inc(r_pow, 1)
            pool.wait_ge(brk_ready, 1)
            pool.wait_ge(tri_used, 1)
            pool.wait_ge(tp_done, tps.name[("rg", 1)] + 1)
            for hf in range(2):
                pool.tensor_tensor(diag[hf][:], ident.unsqueeze(1).unsqueeze(1).to_broadcast([P, 4, M, P]),
                                   brk[:, :, 4 * hf:4 * hf + 4].rearrange("p m h -> p h m").unsqueeze(3).to_broadcast([P, 4, M, P]),
                                   ALU.mult).then_inc(dgb_ready, 1)
            pool.wait_ge(tp_done, tps.name[("up", 2)] + 1)
            pool.dma_start(amask[:], masks[:, 6 * P:]).then_inc(amask_in, 16)
            pool.wait_ge(y_var, 1)
            pool.tensor_tensor(yrs[:], yss[:], mh8, ALU.pow).then_inc(y_pow, 1)
            pool.wait_ge(tp_done, tps.name[("mT", 3)] + 1)
            pool.dma_start(memt[:], mem.rearrange("(m p) n -> p m n", p=P)).then_inc(mem_in, 16)
            norm(4, 1, 1)
            norm(5, 5)
            pool.wait_ge(tp_done, tps.name[("norm", 4, 3)] + 1)
            pool.dma_start(cw_all[:], cols[:, N_COLS:]).then_inc(cw_in, 16)
            norm(6, 6)
            pool.dma_start(frow2[:], rows[:, N + D:N + 2 * D]).then_inc(row2_in, 16)
            norm(7, 7)

        @block.tensor
        def _(pe):
            def chunk(c, lhs, k0, blk, first, last, i=None, step=0, bper=0, n_k=4, width=N):
                pe.wait_ge(lo_ready, at(c + 1, i, step))
                if first and blk >= 2:
                    accs.wait(pe, blk - 2, i, bper)
                wh = w_hi[:, c % SLOTS].rearrange("p (k n) -> p k n", n=width)
                wl = w_lo[:, c % SLOTS].rearrange("p (k n) -> p k n", n=width)
                for k in range(n_k):
                    for m in range(M):
                        xh = lhs[0][:, k0 + k, m * P:(m + 1) * P]
                        xl = lhs[1][:, k0 + k, m * P:(m + 1) * P]
                        dst = acc[:, blk % 2, m, 0:width]
                        pe.matmul(dst, xh, wh[:, k], start=first and k == 0, stop=False)
                        pe.matmul(dst, xh, wl[:, k], start=False, stop=False)
                        mm = pe.matmul(dst, xl, wh[:, k], start=False, stop=last and k == n_k - 1)
                mm.then_inc(used, 1)

            opened = [0]

            def open_group(g, i=None, per=0):
                assert g == opened[0], (g, opened[0], "groups in the order of the plan")
                opened[0] += 1
                if g >= 2:
                    tps.wait(pe, g - 2, i, per)

            def transposes(g, src, i=None, per=0):
                open_group(g, i, per)
                for k in range(4):
                    for m in range(M):
                        mm = pe.transpose(tp[:, g % 2, k, m * P:(m + 1) * P], src[:, m, k * P:(k + 1) * P], ident)
                mm.then_inc(tp_done, 1)

            def norm_part(j, n):
                if j == 0:
                    pe.wait_ge(x_in[n], 16)
                elif j == 4:
                    pe.wait_ge(mem_in, 16)
                else:
                    accs.wait(pe, accs.name[{1: ("glaout", n), 3: ("down", 3, n), 5: ("wo", n), 6: ("xo", n)}[j]])
                transposes(tps.name[("norm", j, n)], (memt if j == 4 else h)[:, :, n * N:(n + 1) * N])

            X, A = (x_hi, x_lo), (a_hi, a_lo)

            def sixteen_columns(name, w_hi_, w_lo_):
                g = tps.name[name]
                open_group(g)
                for k in range(16):
                    for j, (u, w) in enumerate(((x_hi, w_hi_), (x_hi, w_lo_), (x_lo, w_hi_))):
                        mm = pe.matmul(tp[0:16, g % 2, 0, :], w[:, k, :], u[:, k, :], start=(k == 0 and j == 0), stop=(k == 15 and j == 2))
                mm.then_inc(tp_done, 1)

            def sixteen_rows_back(name, src_name, src):
                g = tps.name[name]
                open_group(g)
                tps.wait(pe, tps.name[src_name])
                for m in range(M):
                    mm = pe.transpose(tpf(g)[:, 16 * m:16 * m + 16], src[:, m * P:(m + 1) * P], ident[0:16, 0:16])
                mm.then_inc(tp_done, 1)

            def low_rank_transposed():
                g = tps.name["glowT"]
                open_group(g)
                tps.wait(pe, tps.name["glow"])
                for m in range(M):
                    mm = pe.transpose(tp[0:16, g % 2, 0, m * P:(m + 1) * P], glow[:, m, :], ident)
                mm.then_inc(tp_done, 1)

            def gate_logits(half):
                g = tps.name[f"z{half}"]
                open_group(g)
                tps.wait(pe, tps.name["glowT"])
                for k in range(4):
                    t = 4 * half + k
                    mm = pe.matmul(tp[:, g % 2, k, :], w_gu[:, t * P:(t + 1) * P], glowT[:], start=True, stop=True)
                mm.then_inc(tp_done, 1)

            def gla_scores(hd):
                g = tps.name[("s", hd)]
                open_group(g)
                pe.wait_ge(qd_ready, hd + 1)
                f = tpf(g)
                pair = 0
                for cs in range(4):
                    part = slice(64 * (cs % 2), 64 * (cs % 2) + 64)
                    c0 = 64 * cs if cs < 2 else 2 * P + 64 * (cs - 2)
                    later = 3 - cs
                    for kk in range(2):
                        t = 2 * hd + kk
                        mm = pe.matmul(f[part, c0:c0 + 64], kT[:, t, 64 * cs:64 * cs + 64],
                                       qT[:, t, 64 * cs:64 * cs + 64], start=kk == 0, stop=kk == 1)
                    for kk in range(2):
                        if later:
                            mm = pe.matmul(f[part, c0 + 64:c0 + 64 + 64 * later], kT[:, 2 * hd + kk, 64 * cs:64 * cs + 64],
                                           qd[:, kk, pair:pair + later, :].rearrange("p c t -> p (c t)"),
                                           start=kk == 0, stop=kk == 1)
                    pair += later
                mm.then_inc(tp_done, 1)

            def gla_values(hd):
                g = tps.name[("o", hd)]
                open_group(g)
                tps.wait(pe, tps.name[("s", hd)])
                s, f, cols = sT[:, hd % 2], tpf(g), slice(hd * N, (hd + 1) * N)
                pe.matmul(f[:, 0:N], s[:, 0:P], v[:, 0, cols], start=True, stop=True)
                pe.matmul(f[:, N:2 * N], s[:, P:2 * P], v[:, 0, cols], start=True, stop=False)
                pe.matmul(f[:, N:2 * N], s[:, 2 * P:3 * P], v[:, 1, cols], start=False, stop=True).then_inc(tp_done, 1)

            def gla_side(c):
                for hd in range(4):
                    if c == 33 + 4 * hd:
                        gla_scores(hd)
                    if c == 37 + 4 * hd:
                        tps.wait(pe, tps.name[("o", hd)])
                        transposes(tps.name[("yT", hd)], sr[:, :, hd * N:(hd + 1) * N])
                    if c == 34 + 4 * hd:
                        gla_values(hd)

            pe.wait_ge(cst_in, 16)
            norm_part(0, 0)
            norm_part(0, 1)
            for c in range(48):
                b, q = divmod(c, 4)
                if c < 4:
                    tps.wait(pe, tps.name[("norm", 0, c)])
                chunk(C_GLA + c, X, 4 * q, accs.name[("gla", b)], q == 0, q == 3)
                if c < 2:
                    norm_part(0, c + 2)
                if c == 3:
                    pe.wait_ge(wg_l, 1)
                    sixteen_columns("glow_rows", wg_hi, wg_lo)
                if c == 4:
                    sixteen_rows_back("glow", "glow_rows", glow_rows)
                if c in (4, 8, 12, 16):
                    n = c // 4 - 1
                    accs.wait(pe, accs.name[("gla", n)])
                    transposes(tps.name[("gT", n)], nat[:, n % 2])
                if c == 5:
                    low_rank_transposed()
                if c in (6, 7):
                    gate_logits(c - 6)
                gla_side(c)
            for c in range(16):
                b, q = divmod(c, 4)
                if b == 0:
                    tps.wait(pe, tps.name[("yT", q)])
                chunk(C_OUT + c, A, 4 * q, accs.name[("glaout", b)], q == 0, q == 3)
                gla_side(48 + c)
                if c in (5, 9, 13):
                    norm_part(1, c // 4 - 1)
            norm_part(1, 3)
            with pe.Fori(0, 4) as i:
                for c in range(32):
                    b, q = divmod(c, 4)
                    if c < 4:
                        tps.wait(pe, tps.name[("norm", 1, c)])
                    if b == 4:
                        tps.wait(pe, tps.name[("aT", 0, q)], i, 4)
                    chunk(C_MLP + c, A if b >= 4 else X, 4 * q, accs.name[("up", 0, 0)] + b, q == 0, q == 3, i, 32, 8)
                    if c in (4, 8, 12, 16):
                        n = c // 4 - 1
                        pe.wait_ge(a_sq, at(n + 1, i, 4))
                        transposes(tps.name[("aT", 0, n)], nat[:, n % 2], i, 4)
            opened[0] += 12

            def mats(hf):
                return [(hh, m, 4 * hf + hh) for hh in range(4) for m in range(M)]

            def pairs_product(name, hf, lhs, rhs):
                g = tps.name[(*name, hf)]
                open_group(g)
                for hh, m, hd in mats(hf):
                    mm = pe.matmul(tpf(g)[:, (2 * hh + m) * P:(2 * hh + m + 1) * P], lhs(hd, m), rhs(hd, m), start=True, stop=True)
                mm.then_inc(tp_done, 1)

            def back(name, src):
                g = tps.name[name]
                open_group(g)
                for hh in range(4):
                    for m in range(M):
                        mm = pe.transpose(tpf(g)[:, m * N + hh * P:m * N + (hh + 1) * P], src(hh)[:, m * P:(m + 1) * P], ident)
                mm.then_inc(tp_done, 1)

            def keys_queries(hf):
                pairs_product(("qk",), hf, lambda hd, m: ckT[:, hd, m * P:(m + 1) * P], lambda hd, m: cqT[:, hd, m * P:(m + 1) * P])

            def dn_side(c):
                if c == 3:
                    pe.wait_ge(wab_l, 1)
                    sixteen_columns("ab_rows", wab_hi, wab_lo)
                if c == 4:
                    sixteen_rows_back("ab", "ab_rows", ab_rows)
                if c == 24:
                    keys_queries(1)
                    for hf in range(2):
                        pe.wait_ge(xt0, hf + 1)
                        g = tps.name[("x0", hf)]
                        open_group(g)
                        for hh, m, hd in mats(hf):
                            mm = pe.transpose(tpf(g)[:, (2 * hh + m) * P:(2 * hh + m + 1) * P], xT[:, hd, m], ident)
                        mm.then_inc(tp_done, 1)
                for b in range(6):
                    if c == 4 * b + 4:
                        accs.wait(pe, accs.name[("dn", b)])
                        transposes(tps.name[("dT", b)], nat[:, b % 2])
                if c == 7:
                    g = tps.name["gc"]
                    open_group(g)
                    pe.wait_ge(g_ready, 1)
                    f = tpf(g)
                    for m in range(M):
                        pe.matmul(f[:, 8 * m:8 * m + 8], tri_c[:], g8[:, m], start=True, stop=True)
                        pe.matmul(f[:, 16 + 8 * m:24 + 8 * m], same_c[:], g8[:, m], start=True, stop=True)
                    for cs in range(4):
                        part = slice(64 * (cs % 2), 64 * (cs % 2) + 64)
                        c0 = (N, 32)[cs % 2] + 8 * (cs // 2)
                        mm = pe.matmul(f[:, c0:c0 + 8], ones[part], g8[part, cs // 2], start=True, stop=True)
                    mm.then_inc(tp_done, 1)
                if c in (7, 11, 15, 19):
                    b = c // 4 - 1
                    g = tps.name[("ssq", b)]
                    open_group(g)
                    pe.wait_ge(conv_sq, b + 1)
                    for m in range(M):
                        for hh in range(4):
                            mm = pe.matmul(tpf(g)[:, 4 * m + hh:4 * m + hh + 1], th[:, hh, m * P:(m + 1) * P], ones[:, 0:1],
                                           start=True, stop=True)
                    mm.then_inc(tp_done, 1)

                def row_broadcast(name, hf, count, src, ready=dg_ready):
                    g = tps.name[(name, hf)]
                    open_group(g)
                    pe.wait_ge(ready, count)
                    d = src[:].rearrange("p h m i -> p (h m i)")
                    for k in range(2):
                        mm = pe.matmul(tpf(g)[:, k * N:(k + 1) * N], ones, d[:, k * N:(k + 1) * N], start=True, stop=True)
                    mm.then_inc(tp_done, 1)

                if c in (10, 11):
                    row_broadcast("rg", c - 10, c - 9, diag[0])
                if c == 21:
                    pe.wait_ge(conv_out, 4)
                    for hf in range(2):
                        pairs_product(("kk",), hf, lambda hd, m: ckT[:, hd, m * P:(m + 1) * P], lambda hd, m: ckT[:, hd, m * P:(m + 1) * P])
                if c == 22:
                    row_broadcast("rb", 0, 1, diag[0], dgb_ready)
                    row_broadcast("rb", 1, 2, diag[1], dgb_ready)
                if c == 23:
                    pe.wait_ge(conv_out, 5)
                    back(("vN", 4), lambda hh: cv[:, hh])
                    keys_queries(0)
                for l in range(1, 6):
                    if c == 23 + 2 * l:
                        for hf in range(2):
                            if l == 1:
                                tps.wait(pe, tps.name[("x0", hf)])
                                tps.wait(pe, tps.name[("rb", hf)])
                            else:
                                tps.wait(pe, tps.name[("D", l - 1, hf)])
                            pairs_product(("P", l), hf, lambda hd, m: nT[:, hd, m], lambda hd, m: xn[:, hd, m])
                        if l <= 2:
                            back(("kN", l - 1), lambda hh: ckT[:, 4 * (l - 1) + hh])
                    if c == 24 + 2 * l:
                        if l == 1:
                            pe.wait_ge(conv_out, 6)
                            back(("vN", 5), lambda hh: cv[:, hh])
                        for hf in range(2):
                            tps.wait(pe, tps.name[("P", l, hf)])
                            if l > 1:
                                tps.wait(pe, tps.name[("DT", l - 1, hf)])
                            if l < 5:
                                pairs_product(("D", l), hf, lambda hd, m: xT[:, hd, m], lambda hd, m: pm[:, hd, m])
                            pairs_product(("DT", l), hf, lambda hd, m: pm[:, hd, m], lambda hd, m: xT[:, hd, m])

            def recurrence(c):
                for cs in range(4):
                    m, part = cs // 2, slice(64 * (cs % 2), 64 * (cs % 2) + 64)
                    toks = slice(64 * cs, 64 * cs + 64)

                    def heads(name, rows_, lhs, rhs):
                        g = tps.name[name]
                        open_group(g)
                        for hd in range(8):
                            mm = pe.matmul(tpf(g)[rows_, hd * P:(hd + 1) * P], lhs(hd), rhs(hd), start=True, stop=True)
                        mm.then_inc(tp_done, 1)

                    if c == 35 + 3 * cs and cs:
                        tps.wait(pe, tps.name[("up", cs - 1)])
                        heads(("kS", cs), part, lambda hd: ckT[:, hd, toks], lambda hd: state[:, hd])
                        heads(("qS", cs), part, lambda hd: cqT[:, hd, toks], lambda hd: state[:, hd])
                    if c == 36 + 3 * cs:
                        if cs:
                            pe.wait_ge(rv_ready, cs)
                        else:
                            for hf in range(2):
                                tps.wait(pe, tps.name[("DT", 5, hf)])
                            tps.wait(pe, tps.name[("vN", 5)])
                        heads(("Xr", cs), part, lambda hd: xT[part, hd, m, part],
                              lambda hd: rv[part, hd] if cs else vb[part, m, hd * P:(hd + 1) * P])
                    if c == 37 + 3 * cs:
                        tps.wait(pe, tps.name[("Xr", cs)])
                        heads(("in", cs), part, lambda hd: qkT[part, hd, m, part], lambda hd: rv[part, hd])
                        if cs < 3:
                            heads(("up", cs), slice(0, P), lambda hd: kdec[part, m, hd * P:(hd + 1) * P], lambda hd: rv[part, hd])

            def attention_side(c):
                if c == 47:
                    for k in range(2):
                        g = tps.name[("sz", k)]
                        open_group(g)
                        tps.wait(pe, tps.name["sbqT"])
                        tps.wait(pe, tps.name["sbkT"])
                        for j in range(2):
                            hd, f = 2 * k + j, tpf(g)[:, j * N:(j + 1) * N]
                            pe.matmul(f[:, 0:SEQ], sbk[:, hd, 0:P], sbq[:, hd, :], start=True, stop=True)
                            mm = pe.matmul(f[:, SEQ:3 * P], sbk[:, hd, P:SEQ], sbq[:, hd, P:SEQ], start=True, stop=True)
                        mm.then_inc(tp_done, 1)
                if c == 48:
                    accs.wait(pe, accs.name["swq"])
                    transposes(tps.name["swqT"], nat[:, 1])
                if c == 49:
                    for k in range(2):
                        g = tps.name[("rev", k)]
                        open_group(g)
                        pe.wait_ge(sp_ready, 1)
                        for j in range(2):
                            hd, f = 2 * k + j, tpf(g)[:, j * N:(j + 1) * N]
                            pe.matmul(f[:, 0:P], tri[:], sp_[:, hd, 0:P], start=True, stop=True)
                            pe.matmul(f[:, P:SEQ], tri[:], sp_[:, hd, P:SEQ], start=True, stop=False)
                            pe.matmul(f[:, P:SEQ], ones, sp_[:, hd, SEQ:3 * P], start=False, stop=True)
                            mm = pe.matmul(f[:, SEQ:3 * P], tri[:], sp_[:, hd, SEQ:3 * P], start=True, stop=True)
                        mm.then_inc(tp_done, 1)
                if c == 50:
                    g = tps.name["swkT"]
                    open_group(g)
                    accs.wait(pe, accs.name["swkv"])
                    for m in range(M):
                        mm = pe.transpose(tpf(g)[:, m * P:(m + 1) * P], nat[:, 0, m, 0:P], ident)
                    mm.then_inc(tp_done, 1)
                    g = tps.name["so"]
                    open_group(g)
                    pe.wait_ge(a_exp, 2)
                    for hd in range(4):
                        cols_, f = slice(hd * P, (hd + 1) * P), tpf(g)
                        pe.matmul(f[:, hd * P:(hd + 1) * P], zm[:, hd, 0:P], sbv[:, 0, cols_], start=True, stop=True)
                        pe.matmul(f[:, N + hd * P:N + (hd + 1) * P], zm[:, hd, P:SEQ], sbv[:, 0, cols_], start=True, stop=False)
                        mm = pe.matmul(f[:, N + hd * P:N + (hd + 1) * P], zm[:, hd, SEQ:3 * P], sbv[:, 1, cols_], start=False, stop=True)
                    mm.then_inc(tp_done, 1)
                if c in (51, 52):
                    for k in (2 * (c - 51), 2 * (c - 51) + 1):
                        g = tps.name[("ws", k)]
                        open_group(g)
                        if k == 0:
                            tps.wait(pe, tps.name["swqT"])
                            tps.wait(pe, tps.name["swkT"])
                        for j in range(2):
                            hd, f = 2 * k + j, tpf(g)[:, j * N:(j + 1) * N]
                            part = slice(64 * (hd // 4), 64 * (hd // 4) + 64)
                            pe.matmul(f[:, 0:P], swq[part, hd % 4, 0:P], swk[part, 0:P], start=True, stop=True)
                            mm = pe.matmul(f[:, P:3 * P], swq[part, hd % 4, P:SEQ], swk[part, :], start=True, stop=True)
                        mm.then_inc(tp_done, 1)
                if c == 52:
                    tps.wait(pe, tps.name["so"])
                    transposes(tps.name["ysbT"], ysb)
                if c == 55:
                    pe.wait_ge(sw_exp, 1)
                    for k in range(3):
                        g = tps.name[("wp", k)]
                        open_group(g)
                        for j in range(8):
                            hd, b = divmod(8 * k + j, 3)
                            mm = pe.transpose(tpf(g)[:, j * P:(j + 1) * P], sw[:, hd, b * P:(b + 1) * P], ident)
                        mm.then_inc(tp_done, 1)
                if c == 56:
                    g = tps.name["wo_"]
                    open_group(g)
                    for k in range(3):
                        tps.wait(pe, tps.name[("wp", k)])
                    for hd in range(8):
                        f, cols_ = tpf(g), slice(64 * (hd // 4), 64 * (hd // 4) + 64)
                        pe.matmul(f[:, 64 * hd:64 * hd + 64], pT[:, 3 * hd], swv[:, 0, cols_], start=True, stop=True)
                        pe.matmul(f[:, N + 64 * hd:N + 64 * hd + 64], pT[:, 3 * hd + 1], swv[:, 0, cols_], start=True, stop=False)
                        mm = pe.matmul(f[:, N + 64 * hd:N + 64 * hd + 64], pT[:, 3 * hd + 2], swv[:, 1, cols_], start=False, stop=True)
                    mm.then_inc(tp_done, 1)
                if c == 57:
                    tps.wait(pe, tps.name["wo_"])
                    transposes(tps.name["yswaT"], yswa)
                if c in (58, 59):
                    pe.wait_ge(y_done, 1)
                    transposes(tps.name[("ydnT", c - 58)], vb[:, :, (c - 58) * N:(c - 57) * N])

            norm_part(3, 0)
            norm_part(3, 1)
            for c in range(50):
                if c < 48:
                    b, q = divmod(c, 4)
                    if c < 4:
                        tps.wait(pe, tps.name[("norm", 3, c)])
                    chunk(C_2 + c, X, 4 * q, accs.name[("dn", 0)] + b, q == 0, q == 3)
                else:
                    chunk(C_2 + c, X, 8 * (c - 48), accs.name["swkv"], c == 48, c == 49, n_k=8, width=256)
                if c in (36, 40):
                    accs.wait(pe, accs.name["sbq" if c == 36 else "sbk"])
                    transposes(tps.name["sbqT" if c == 36 else "sbkT"], nat[:, c // 4 % 2 ^ 1])
                if c == 0:
                    norm_part(3, 2)
                    norm_part(3, 3)
                dn_side(c)
                recurrence(c)
                attention_side(c)
            for nb in range(NB):
                for j in range(16):
                    c = 50 + 16 * nb + j
                    br, first, k0 = BRANCH[j]
                    if j == first + 4:
                        chunk(C_2 + c, A, k0, accs.name[("br", nb, br)], True, br != "dn")
                    elif j == first + 5:
                        chunk(C_2 + c, A, k0 + 4, accs.name[("br", nb, br)], False, True)
                    else:
                        q = j - first
                        chunk(C_2 + c, X, 4 * q, accs.name[("gate", nb, br)], q == 0, q == 3)
                    if nb == 0:
                        attention_side(c)
                        if j == 3:
                            tps.wait(pe, tps.name["ysbT"])
                        if j == 8:
                            tps.wait(pe, tps.name["yswaT"])
                        if j == 13:
                            tps.wait(pe, tps.name[("ydnT", 0)])
                            tps.wait(pe, tps.name[("ydnT", 1)])
                    elif j == 1:
                        pe.wait_ge(mg_ready, 2 * nb)
                        transposes(tps.name[("mT", nb - 1)], mg[(nb - 1) % 2])
            for c in range(16):
                b, q = divmod(c, 4)
                if b == 0:
                    tps.wait(pe, tps.name[("mT", q)])
                chunk(C_WO + c, (m_hi, m_lo), 4 * q, accs.name[("wo", b)], q == 0, q == 3)
                if c == 1:
                    pe.wait_ge(mg_ready, 2 * NB)
                    transposes(tps.name[("mT", 3)], mg[1])
                if c in WO_PARTS:
                    norm_part(*WO_PARTS[c])
            def memory_scores(c):
                if c == 9:
                    tps.wait(pe, tps.name["xqT"])
                    tps.wait(pe, tps.name["xkT"])
                    for m in range(M):
                        g = tps.name[("xs", m)]
                        open_group(g)
                        for hd in range(4):
                            mm = pe.matmul(tp[:, g % 2, hd], xqT[:, hd, m * P:(m + 1) * P], xkT[:, hd], start=True, stop=True)
                        mm.then_inc(tp_done, 1)
                if c == 10:
                    for m in range(M):
                        g = tps.name[("xpT", m)]
                        open_group(g)
                        tps.wait(pe, tps.name[("xs", m)])
                        for hd in range(4):
                            for b in range(2):
                                mm = pe.transpose(tpf(g)[:, (2 * hd + b) * P:(2 * hd + b + 1) * P], xp[:, m, hd, b * P:(b + 1) * P], ident)
                        mm.then_inc(tp_done, 1)

            for c in range(12):
                b, q = divmod(c, 4)
                if b == 0:
                    tps.wait(pe, tps.name[("norm", 4, q)])
                if b == 1:
                    tps.wait(pe, tps.name[("norm", 5, q)])
                chunk(C_X + c, X if b == 1 else A, 4 * q, accs.name["xk"] + b, q == 0, q == 3)
                if c == 0:
                    norm_part(5, 3)
                if c in (4, 8):
                    accs.wait(pe, accs.name["xk" if c == 4 else "xq"])
                    transposes(tps.name["xkT" if c == 4 else "xqT"], nat[:, c // 4 - 1])
                memory_scores(c)
            accs.wait(pe, accs.name["xv"])
            g = tps.name["xo_"]
            open_group(g)
            for m in range(M):
                tps.wait(pe, tps.name[("xpT", m)])
                for hd in range(4):
                    for b in range(2):
                        mm = pe.matmul(tpf(g)[:, m * N + hd * P:m * N + (hd + 1) * P], xpT[:, m, hd, b],
                                       xv[:, b, hd * P:(hd + 1) * P], start=b == 0, stop=b == 1)
            mm.then_inc(tp_done, 1)
            tps.wait(pe, tps.name["xo_"])
            transposes(tps.name["yxT"], yx)
            tps.wait(pe, tps.name["yxT"])
            for c in range(4):
                chunk(C_XO + c, A, 0, accs.name[("xo", c)], True, True)
                if c:
                    norm_part(6, c - 1)
            norm_part(6, 3)
            with pe.Fori(0, 2) as i:
                for c in range(48):
                    b, q = divmod(c, 4)
                    if c < 4:
                        tps.wait(pe, tps.name[("norm", 6, c)])
                    if b == 8:
                        pe.wait_ge(f_lo, at(q + 2, i, 4))
                    chunk(C_FFN + c, A if b >= 8 else X, 4 * q, accs.name[("fg", 0, 0)] + b, q == 0, q == 3, i, 48, 12)
                    if q == 0 and 1 <= b <= 8:
                        accs.wait(pe, accs.name[("fg", 0, 0)] + b - 1, i, 12)
                        transposes(tps.name[("fgT", 0, 0)] + b - 1, nat[:, (b - 1) % 2], i, 8)
            assert opened[0] + 8 == len(tps.who)

        @block.scalar
        def _(act):
            steps = [0]

            def link(ins):
                steps[0] += 1
                ins.then_inc(act_step, 1)
                act.wait_ge(act_step, steps[0])

            def split(c, i=None, step=0):
                act.wait_ge(landed[c % SLOTS], at(16 * (c // SLOTS + 1), i, 4 * step))
                if c >= SLOTS:
                    act.wait_ge(used, at(c - SLOTS + 1, i, step))
                act.activation(w_hi[:, c % SLOTS], w_raw[:, c % SLOTS], ACT.Copy).then_inc(hi_ready, 1)

            def stats(j, n, src=h, k=0, i=None):
                for m in range(M):
                    act.activation(junk[:], src[:, m, n * N:(n + 1) * N], ACT.Square, accum_out=ss[k][:, m, n:n + 1]).then_inc(sq_done[k], 1)
                    act.wait_ge(sq_done[k], at(2 * (4 * j + n) + m + 1, i, 8))

            def row_scaled(j, dst, src, func=ACT.Copy, scales=rstd):
                for m in range(M):
                    ins = act.activation(dst[:, m], src[:, m], func, scale=scales[:, j, m:m + 1])
                return ins

            def high(j, n, gains, dst=x_hi):
                g = tps.name[("norm", j, n)]
                act.wait_ge(tp_done, g + 1)
                for q in range(4):
                    t = 4 * n + q
                    ins = act.activation(dst[:, t], tp[:, g % 2, q], ACT.Copy, scale=col[:, gains + t:gains + t + 1])
                    if q % 2:
                        ins.then_inc(xh_done, 1)

            def gla_side(c):
                for hd in range(4):
                    if c == 33 + 4 * hd:
                        g = tps.name[("s", hd)]
                        act.wait_ge(tp_done, g + 1)
                        if hd == 0:
                            act.wait_ge(sT_zero, 2)
                        if hd >= 2:
                            act.wait_ge(tp_done, tps.name[("o", hd - 2)] + 1)
                        f = tpf(g)
                        scale = 256 ** -0.5
                        act.activation(sT[0:64, hd % 2], f[0:64, 0:3 * P], ACT.Copy, scale=scale)
                        act.activation(sT[64:P, hd % 2, 64:2 * P], f[64:P, 64:2 * P], ACT.Copy, scale=scale)
                        act.activation(sT[64:P, hd % 2, 2 * P + 64:3 * P], f[64:P, 2 * P + 64:3 * P], ACT.Copy,
                                       scale=scale).then_inc(tps.sem(g), 1)
                    if c == 35 + 4 * hd:
                        act.wait_ge(used, c + 1)
                        if hd >= 2:
                            accs.wait(act, accs.name[("gla", 8 + hd - 2)])
                        else:
                            act.wait_ge(tp_done, tps.name[("gT", 2 + hd)] + 1)
                        row_scaled(0, nat[:, hd % 2], acc[:, hd % 2], ACT.Tanh, rhalf).then_inc(r_tanh, 1)
                        g = tps.name[("o", hd)]
                        act.wait_ge(tp_done, g + 1)
                        for m in range(M):
                            act.activation(junk[:], tpf(g)[:, m * N:(m + 1) * N], ACT.Square, accum_out=oss[:, hd, m:m + 1]).then_inc(osq, 1)
                            act.wait_ge(osq, 2 * hd + m + 1)
                    if c == 37 + 4 * hd:
                        g = tps.name[("yT", hd)]
                        act.wait_ge(tp_done, g + 1)
                        act.activation(a_hi[:, 4 * hd:4 * hd + 4].rearrange("p k t -> p (k t)"), tpf(g), ACT.Copy).then_inc(ah_done, 1)

            act.wait_ge(cols_in, 16)
            for n in range(NB):
                if n >= 2:
                    split(n)
                high(0, n, COL["gla_norm"])
                if n < 2:
                    split(n)
            act.wait_ge(gla_in, 48)
            act.activation(wg_hi[:], wg_raw[:], ACT.Copy).then_inc(wg_h, 1)
            for c in range(64):
                if c < NB:
                    stats(0, c)
                if c in (3, 7, 11, 15, 19, 23, 27, 31):
                    n = c // 4
                    act.wait_ge(used, c + 1)
                    if n in (2, 3):
                        act.wait_ge(tp_done, tps.name[("gT", n - 2)] + 1)
                    dst = nat[:, n % 2] if n < 4 else v[:, :, (n - 4) * N:(n - 3) * N]
                    if n == 0:
                        act.wait_ge(scale_ready, SCALES[0])
                    row_scaled(0, dst, acc[:, n % 2]).then_inc(accs.sem(n), 1)
                if c == 3:
                    g = tps.name["glow_rows"]
                    act.wait_ge(tp_done, g + 1)
                    act.activation(glow_rows[:], tp[0:16, g % 2, 0, :], ACT.Copy).then_inc(tps.sem(g), 1)
                if c == 4:
                    g = tps.name["glow"]
                    act.wait_ge(tp_done, g + 1)
                    row_scaled(0, glow, tpf(g)[:, 0:32].rearrange("p (m n) -> p m n", m=M)).then_inc(tps.sem(g), 1)
                if c == 5:
                    g = tps.name["glowT"]
                    act.wait_ge(tp_done, g + 1)
                    act.activation(glowT[:], tp[0:16, g % 2, 0, :], ACT.Copy).then_inc(tps.sem(g), 1)
                if c in (6, 7):
                    g = tps.name[f"z{c - 6}"]
                    act.wait_ge(tp_done, g + 1)
                    for k in range(4):
                        t = 4 * (c - 6) + k
                        ins = act.activation(zb[:, t], tp[:, g % 2, k], ACT.Identity, bias=col[:, COL["b_gate"] + t:COL["b_gate"] + t + 1])
                    ins.then_inc(tps.sem(g), 1)
                if c == 8:
                    tps.wait(act, tps.name["z0"])
                    tps.wait(act, tps.name["z1"])
                    link(act.activation(ez[:], zb[:], ACT.Abs))
                    link(act.activation(ez[:], ez[:], ACT.Exp, scale=-1.0))
                if c == 9:
                    act.activation(ez[:], ez[:], ACT.Ln, bias=1.0).then_inc(lnz_ready, 1)
                if c == 15:
                    act.wait_ge(la_diff, 1)
                    act.activation(kd[:], kd[:], ACT.Exp, scale=1.0 / 16.0).then_inc(kd_exp, 1)
                    act.wait_ge(e_sum, 1)
                    act.activation(edec[:], edec[:], ACT.Exp, scale=1.0 / 16.0).then_inc(e_exp, 1)
                gla_side(c)
                if c - 48 in (5, 9, 13):
                    high(1, (c - 48) // 4 - 1, COL["mlp_norm"])
                    stats(1, (c - 48) // 4 - 1)
                if c:
                    split(c + AHEAD)
            high(1, 3, COL["mlp_norm"])
            stats(1, 3)

            def mlp_high(n, i):
                g = tps.name[("aT", 0, n)]
                act.wait_ge(tp_done, at(g + 1, i, 4))
                act.activation(a_hi[:, 4 * n:4 * n + 4].rearrange("p k t -> p (k t)"), tpf(g), ACT.Copy).then_inc(ah_done, 1)

            with act.Fori(0, 4) as i:
                for c in range(32):
                    if c in (3, 7, 11, 15):
                        n = c // 4
                        act.wait_ge(used, at(C_MLP + c + 1, i, 32))
                        act.wait_ge(tp_done, at(tps.name[("aT", 0, n)] - 2 + 1, i, 4))
                        blk = accs.name[("up", 0, n)]
                        if n == 0:
                            act.wait_ge(scale_ready, SCALES[1])
                        row_scaled(1, nat[:, n % 2], acc[:, blk % 2], ACT.Relu).then_inc(accs.sem(blk), 1)
                    if c in (4, 8, 12, 16):
                        mlp_high(c // 4 - 1, i)
                    split(C_MLP + c + AHEAD, i, 32)
            high(3, 0, COL["norm_mix"])
            high(3, 1, COL["norm_mix"])
            for n in range(NB):
                accs.wait(act, accs.name[("down", 3, n)])
                stats(2, n)

            def evac(name, dst, c, width=N, j=3):
                blk = accs.name[name]
                act.wait_ge(used, C_2 + c + 1)
                row_scaled(j, dst, acc[:, blk % 2, :, 0:width]).then_inc(accs.sem(blk), 1)

            def take(g, dst, src, scale=1.0, s=None):
                act.wait_ge(tp_done, g + 1)
                act.activation(dst, src, ACT.Copy, scale=scale).then_inc(s or tps.sem(g), 1)

            def flat(t):
                return t.rearrange("p k t -> p (k t)")

            def dn_side(c):
                if c == 0:
                    high(3, 2, COL["norm_mix"])
                    high(3, 3, COL["norm_mix"])
                if c in (0, 1):
                    for n in (2 * c, 2 * c + 1):
                        act.wait_ge(rowdone, n + 1)
                        stats(3, n)
                if c == 2:
                    act.wait_ge(dn_in, 48)
                    act.activation(wab_hi[:], wab_raw[:], ACT.Copy).then_inc(wab_h, 1)
                if c == 3:
                    act.wait_ge(scale_ready, SCALES[3])
                if c == 4:
                    g = tps.name["ab"]
                    act.wait_ge(tp_done, g + 1)
                    row_scaled(3, ab, tpf(g)[:, 0:32].rearrange("p (m n) -> p m n", m=M)).then_inc(tps.sem(g), 1)
                if c == 24:
                    for hf in range(2):
                        tps.wait(act, tps.name[("qk", hf)])
                    for hf in range(2):
                        g = tps.name[("x0", hf)]
                        take(g, xn[:, 4 * hf:4 * hf + 4].rearrange("p h m i -> p (h m i)"), tpf(g))
                for b in range(6):
                    g = tps.name[("dT", b)]
                    if c == 4 * b + 3:
                        act.wait_ge(tp_done, tps.name[("dT", b - 2) if b >= 2 else ("aT", 3, 2 + b)] + 1)
                        evac(("dn", b), nat[:, b % 2], c)
                    if c == 4 * b + 4:
                        if b:
                            act.wait_ge(conv_out, b)
                        if b == 5:
                            act.wait_ge(tp_done, tps.name[("vN", 4)] + 1)
                        act.wait_ge(tp_done, g + 1)
                        for k in range(4):
                            w = COL["dn_conv"] + 4 * (4 * b + k) + 3
                            ins = act.activation(cv[:, k], tp[:, g % 2, k], ACT.Copy, scale=col[:, w:w + 1])
                        ins.then_inc(conv0, 1)
                    if c == 4 * b + 5:
                        tps.wait(act, g)
                        if 1 <= b <= 4:
                            act.wait_ge(tp_done, tps.name[("ssq", b - 1)] + 1)
                        act.activation(th[:], cv[:], ACT.Tanh, scale=0.5).then_inc(conv_t, 1)
                    if c == 4 * b + 6 and b < 4:
                        act.wait_ge(conv_out, b + 1)
                        src = (cqT if b < 2 else ckT)[:, 4 * (b % 2):4 * (b % 2) + 4]
                        act.activation(th[:], src, ACT.Square).then_inc(conv_sq, 1)
                if c == 3:
                    g = tps.name["ab_rows"]
                    take(g, ab_rows[:], tp[0:16, g % 2, 0, :])
                if c == 4:
                    act.wait_ge(smalls_in, 48)
                    act.wait_ge(u_ready, 1)
                    link(act.activation(l8[:], u8[:], ACT.Abs))
                    link(act.activation(l8[:], l8[:], ACT.Exp, scale=-1.0))
                    act.activation(l8[:], l8[:], ACT.Ln, bias=1.0).then_inc(u_ln, 1)
                    act.activation(nega[:], alog, ACT.Exp).then_inc(a_log, 1)
                    act.activation(beta[:], ab[:, :, 8:16], ACT.Tanh, scale=0.5).then_inc(b_tanh, 1)
                if c == 8:
                    act.wait_ge(ekd_in, 1)
                    act.activation(egc[:], gc[:], ACT.Exp)
                    act.activation(ekd[:], ekd[:], ACT.Exp)
                    act.activation(glb[:], glb[:], ACT.Exp).then_inc(e_gc, 1)
                if c == 12:
                    act.wait_ge(diff_ready, 1)
                    act.activation(dec[:], dec[:], ACT.Exp).then_inc(dec_exp, 1)
                for b in range(2):
                    if c == 27 + 4 * b:
                        blk = accs.name[("z", b)]
                        act.wait_ge(used, C_2 + c + 1)
                        act.wait_ge(tp_done, tps.name[("dT", 4 + b)] + 1)
                        row_scaled(3, nat[:, b], acc[:, blk % 2], ACT.Tanh, rhalf).then_inc(z_tanh, 1)

            def attention_side(c):
                for cs in range(4):
                    if c == 36 + 3 * cs:
                        part = slice(64 * (cs % 2), 64 * (cs % 2) + 64)
                        g = tps.name[("Xr", cs)]
                        take(g, rv[part].rearrange("p h d -> p (h d)"), tpf(g)[part])
                if c == 35:
                    accs.wait(act, accs.name[("z", 0)])
                    evac("sbq", nat[:, 0], c)
                if c == 39:
                    accs.wait(act, accs.name[("z", 1)])
                    evac("sbk", nat[:, 1], c)
                if c == 43:
                    evac("sbv", sbv[:], c)
                if c == 47:
                    act.wait_ge(tp_done, tps.name["sbkT"] + 1)
                    evac("swq", nat[:, 1], c)
                    act.wait_ge(y_scaled, 1)
                    act.activation(ysq[:], vb[:].rearrange("p m (h d) -> p (m h) d", d=P), ACT.Square).then_inc(y_sq, 1)
                if c == 48:
                    act.wait_ge(zm_ready, 1)
                    link(act.activation(sp_[:], zm[:], ACT.Abs))
                    link(act.activation(sp_[:], sp_[:], ACT.Exp, scale=-1.0))
                    act.activation(sp_[:], sp_[:], ACT.Ln, bias=1.0).then_inc(sp_ln, 1)
                if c == 49:
                    act.wait_ge(used, C_2 + c + 1)
                    blk = accs.name["swkv"]
                    row_scaled(3, swv, acc[:, blk % 2, :, P:2 * P])
                    evac("swkv", nat[:, 0, :, 0:P], c, P)
                    for k in range(2):
                        tps.wait(act, tps.name[("rev", k)])
                        act.activation(zm[:, 2 * k:2 * k + 2], zm[:, 2 * k:2 * k + 2], ACT.Exp).then_inc(a_exp, 1)
                if c == 50:
                    g = tps.name["so"]
                    take(g, ysb[:].rearrange("p m n -> p (m n)"), tpf(g))
                for slot, name, k0 in ((52, "ysbT", 12), (57, "yswaT", 8), (58, ("ydnT", 0), 0), (59, ("ydnT", 1), 4)):
                    if c == slot:
                        act.wait_ge(y_done, 1)
                        g = tps.name[name]
                        take(g, flat(a_hi[:, k0:k0 + 4]), tpf(g), s=ah_done)
                if c == 53:
                    act.wait_ge(sw_max, 1)
                    for hd in range(8):
                        for m in range(M):
                            part = sw[:, hd, P * m:P * (1 + 2 * m)]
                            act.activation(part, part, ACT.Exp, bias=nmx[:, m, hd:hd + 1], accum_out=rs[:, m, hd:hd + 1])
                    act.activation(es[:], es[:], ACT.Exp).then_inc(sw_exp, 1)
                if c == 55:
                    for k in range(3):
                        g = tps.name[("wp", k)]
                        take(g, flat(pT[:, 8 * k:8 * k + 8]), tpf(g))

            for c in range(50):
                dn_side(c)
                attention_side(c)
                split(C_2 + c + AHEAD)
            for nb in range(NB):
                for j in range(16):
                    c = 50 + 16 * nb + j
                    br, first, _ = BRANCH[j]
                    if j == first + 3:
                        gk = 3 * nb + ("sb", "swa", "dn").index(br)
                        blk = accs.name[("gate", nb, br)]
                        act.wait_ge(used, C_2 + c + 1)
                        if gk < 2:
                            act.wait_ge(tp_done, tps.name["swkT" if gk == 0 else "swqT"] + 1)
                        else:
                            act.wait_ge(mg_ready, 2 * nb - 1 + gk % 3)
                        row_scaled(3, nat[:, gk % 2], acc[:, blk % 2], ACT.Tanh, rhalf).then_inc(accs.sem(blk), 1)
                    if nb == 0:
                        attention_side(c)
                    elif j == 1:
                        g = tps.name[("mT", nb - 1)]
                        take(g, flat(m_hi[:, 4 * nb - 4:4 * nb]), tpf(g), 0.5, m_half)
                    split(C_2 + c + AHEAD)
            for c in range(16):
                if c == 1:
                    g = tps.name[("mT", 3)]
                    take(g, flat(m_hi[:, 12:16]), tpf(g), 0.5, m_half)
                if c in WO_PARTS:
                    j, n = WO_PARTS[c]
                    if j == 4:
                        high(4, n, COL["norm_mem"], a_hi)
                        stats(0, n, memt, 1)
                    else:
                        high(5, n, COL["norm_xattn"])
                        stats(4, n)
                split(C_WO + c + AHEAD)
            for c in range(12):
                if c == 0:
                    high(5, 3, COL["norm_xattn"])
                    stats(4, 3)
                if c == 3:
                    act.wait_ge(scale_ready, SCALES[4])
                    evac("xk", nat[:, 0], C_X - C_2 + c, j=4)
                if c == 7:
                    act.wait_ge(scale_ready, SCALES[5])
                    evac("xq", nat[:, 1], C_X - C_2 + c, j=5)
                if c == 9:
                    for m in range(M):
                        act.wait_ge(x_max, m + 1)
                        g = tps.name[("xs", m)]
                        for hd in range(4):
                            ins = act.activation(xp[:, m, hd], tp[:, g % 2, hd], ACT.Exp, bias=nmx[:, m, hd:hd + 1],
                                                 accum_out=rs[:, m, hd:hd + 1])
                        ins.then_inc(tps.sem(g), 1)
                if c == 10:
                    g = tps.name[("xpT", 1)]
                    take(g, xpT[:, 1].rearrange("p h b q -> p (h b q)"), tpf(g))
                if c == 11:
                    evac("xv", xv, C_X - C_2 + c, j=4)
                split(C_X + c + AHEAD)
            g = tps.name["yxT"]
            take(g, flat(a_hi[:, 0:4]), tpf(g), s=ah_done)
            for c in range(4):
                if c:
                    high(6, c - 1, COL["norm_ffn"])
                    stats(5, c - 1)
                split(C_XO + c + AHEAD)
            high(6, 3, COL["norm_ffn"])
            stats(5, 3)
            base = tps.name[("fgT", 0, 0)]
            LAST_STATS = (36, 40, 44, 47)
            with act.Fori(0, 2) as i:
                for c in range(48):
                    b, q = divmod(c, 4)
                    if q == 3 and b < 8:
                        blk = accs.name[("fg", 0, 0)] + b
                        act.wait_ge(used, at(C_FFN + c + 1, i, 48))
                        act.wait_ge(tp_done, at(base + b - 2 + 1, i, 8))
                        if b == 0:
                            act.wait_ge(scale_ready, SCALES[6])
                        row_scaled(6, nat[:, b % 2], acc[:, blk % 2]).then_inc(accs.sem(blk), 1)
                    if q == 0 and 1 <= b <= 8:
                        b -= 1
                        hb, val = divmod(b, 2)
                        g = base + b
                        dst = fv if val else fg
                        act.wait_ge(tp_done, at(g + 1, i, 8))
                        if b == 0:
                            act.wait_ge(cw_ready, at(1, i, 1))
                        act.wait_ge(f_lo, at(hb + 1, i, 4))
                        for k in range(4):
                            t = 16 * val + 4 * hb + k
                            ins = act.activation(dst[:, k], tp[:, g % 2, k], ACT.Copy, scale=cw[:, t, 2:3])
                        ins.then_inc(conv1, 1)
                        if not val:
                            tps.wait(act, g, i, 8)
                            act.activation(ft[:], fg[:], ACT.Tanh, scale=0.5).then_inc(f_tanh, 1)
                    if q == 1 and b in (2, 4, 6, 8):
                        hb = b // 2 - 1
                        act.wait_ge(p_ready, at(hb + 1, i, 4))
                        act.activation(a_hi[:, 4 * hb:4 * hb + 4], fg[:], ACT.Copy).then_inc(f_hi, 1)
                    split(C_FFN + c + AHEAD, i, 48)
                    if c in LAST_STATS:
                        n = LAST_STATS.index(c)
                        accs.wait(act, accs.name[("fdown", 0, n)], i, 12)
                        stats(6, n, i=i)

        @block.vector
        def _(dve):
            steps = [0]

            def link(ins, i=None, per=0):
                steps[0] += 1
                ins.then_inc(dve_step, 1)
                dve.wait_ge(dve_step, at(steps[0], i, per))

            def split(c, i=None, step=0):
                dve.wait_ge(hi_ready, at(c + 1, i, step))
                dve.tensor_tensor(w_lo[:, c % SLOTS], w_raw[:, c % SLOTS], w_hi[:, c % SLOTS].bitcast(F32),
                                  ALU.subtract).then_inc(lo_ready, 1)

            def rms(ordinal, k=0, passes=1):
                dve.wait_ge(sq_done[k], 8 * (ordinal + passes))
                link(dve.tensor_reduce(ms[k][:], ss[k][:], AX.X, ALU.add))
                dve.tensor_scalar(var[k][:], ms[k][:], 1.0 / D, EPS, ALU.mult, ALU.add).then_inc(var_ready[k], 1)
                dve.wait_ge(rstd_ready[k], ordinal + 1)

            def row_scales(j, ordinal, k=0):
                rms(ordinal, k)
                if j == 3:
                    link(dve.tensor_tensor(rstd[:, 3], rstd[:, 3], rstd[:, 2], ALU.mult))
                dve.tensor_scalar(rhalf[:, j], rstd[:, j], 0.5, None, ALU.mult).then_inc(scale_ready, 1)
                dve.wait_ge(scale_ready, SCALES[j])

            def low_x(j, n, gains, hi=x_hi, lo=x_lo):
                g = tps.name[("norm", j, n)]
                for q in range(4):
                    t = 4 * n + q
                    if q % 2 == 0:
                        dve.wait_ge(xh_done, 2 * quarter[j, n] + q // 2 + 1)
                    ins = dve.scalar_tensor_tensor(lo[:, t], tp[:, g % 2, q], col[:, gains + t:gains + t + 1],
                                                   hi[:, t].bitcast(F32), ALU.mult, ALU.subtract)
                ins.then_inc(tps.sem(g), 1)

            def normed_rows(j, n, gain_row, done):
                for m in range(M):
                    hn = h[:, m, n * N:(n + 1) * N]
                    ins = dve.scalar_tensor_tensor(hn, hn, rstd[:, j, m:m + 1], gain_row[:, n * N:(n + 1) * N], ALU.mult, ALU.mult)
                ins.then_inc(done, 1)

            def add_to_h(name, n, i=None, step=0, last=0, per=0):
                blk = accs.name[name]
                dve.wait_ge(used, at(last + 1, i, step))
                hn = h[:, :, n * N:(n + 1) * N]
                dve.tensor_tensor(hn, acc[:, blk % 2], hn, ALU.add).then_inc(accs.sem(blk), 1)

            def low(g, n, hi_count, i=None, per=0):
                dve.wait_ge(ah_done, at(hi_count, i, per))
                dve.tensor_tensor(a_lo[:, 4 * n:4 * n + 4].rearrange("p k t -> p (k t)"), tpf(g),
                                  a_hi[:, 4 * n:4 * n + 4].rearrange("p k t -> p (k t)").bitcast(F32),
                                  ALU.subtract).then_inc(tps.sem(g), 1)

            def scaled_q(hd):
                if hd:
                    dve.wait_ge(tp_done, tps.name[("s", hd - 1)] + 1)
                pair = 0
                for cs in range(3):
                    later = 3 - cs
                    ins = dve.tensor_tensor(
                        qd[:, :, pair:pair + later, :],
                        qT[:, 2 * hd:2 * hd + 2, 64 * (cs + 1):].rearrange("p k (c t) -> p k c t", t=64),
                        edec[:, 2 * hd:2 * hd + 2, pair:pair + later].unsqueeze(3).to_broadcast([P, 2, later, 64]), ALU.mult)
                    pair += later
                ins.then_inc(qd_ready, 1)

            def gla_side(c):
                for hd in range(4):
                    cols = slice(hd * N, (hd + 1) * N)
                    if hd and c == 30 + 4 * hd:
                        scaled_q(hd)
                    if c == 35 + 4 * hd:
                        blk = accs.name[("gla", 8 + hd)]
                        dve.wait_ge(r_tanh, hd + 1)
                        dve.scalar_tensor_tensor(sr[:, :, cols], nat[:, hd % 2], 1.0, acc[:, blk % 2], ALU.add, ALU.mult).then_inc(accs.sem(blk), 1)
                        accs.wait(dve, blk)
                        for m in range(M):
                            ins = dve.scalar_tensor_tensor(sr[:, m, cols], sr[:, m, cols], rhalf[:, 0, m:m + 1], onorm[:], ALU.mult, ALU.mult)
                        link(ins)
                        dve.wait_ge(osq, 2 * hd + 2)
                        dve.tensor_scalar(ovar[:, hd], oss[:, hd], 1.0 / N, EPS, ALU.mult, ALU.add).then_inc(ovar_s, 1)
                        dve.wait_ge(orstd_s, hd + 1)
                        g = tps.name[("o", hd)]
                        for m in range(M):
                            ins = dve.scalar_tensor_tensor(sr[:, m, cols], tpf(g)[:, m * N:(m + 1) * N], orstd[:, hd, m:m + 1],
                                                           sr[:, m, cols], ALU.mult, ALU.mult)
                        ins.then_inc(tps.sem(g), 1)
                    if c == 37 + 4 * hd:
                        low(tps.name[("yT", hd)], hd, hd + 1)

            dve.wait_ge(cols_in, 16)
            for n in range(NB):
                if n >= 2:
                    split(n)
                low_x(0, n, COL["gla_norm"])
                if n < 2:
                    split(n)
            dve.wait_ge(wg_h, 1)
            dve.tensor_tensor(wg_lo[:], wg_raw[:], wg_hi[:].bitcast(F32), ALU.subtract).then_inc(wg_l, 1)
            mix = col[:, COL["norm_mix"]:COL["norm_mix"] + 16]
            link(dve.tensor_tensor(mix, mix, col[:, COL["final_norm"]:COL["final_norm"] + 16], ALU.mult))
            dve.wait_ge(mask_in, 16)
            cum_c = cum[:].rearrange("p t (c s) -> p (t c) s", s=64)
            tot = cum[:].rearrange("p t (c s) -> p t c s", s=64)[:, :, :, 63]
            for c in range(64):
                if c == 3:
                    row_scales(0, 0)
                if c in (4, 8, 12, 16):
                    n = c // 4 - 1
                    g = tps.name[("gT", n)]
                    dve.wait_ge(tp_done, g + 1)
                    dst = (qT if n < 2 else kT)[:, 4 * (n % 2):4 * (n % 2) + 4].rearrange("p k t -> p (k t)")
                    dve.tensor_copy(dst, tpf(g)).then_inc(tps.sem(g), 1)
                if c == 10:
                    dve.wait_ge(lnz_ready, 1)
                    link(dve.scalar_tensor_tensor(zb[:], zb[:], 0.0, ez[:], ALU.min, ALU.subtract))
                if c in (11, 12, 13, 14):
                    for t in (2 * (c - 11), 2 * (c - 11) + 1):
                        link(dve.tensor_tensor_scan(cum[:, t], mask01[:], zb[:, t], 0.0, ALU.mult, ALU.add))
                if c == 14:
                    dve.tensor_tensor(kd[:].rearrange("p t (c s) -> p (t c) s", s=64),
                                      cum_c[:, :, 63:64].to_broadcast([P, 32, 64]), cum_c, ALU.subtract).then_inc(la_diff, 1)
                if c == 15:
                    for pair, k in ((0, 1), (3, 2), (5, 3)):
                        ins = dve.tensor_copy(edec[:, :, pair], tot[:, :, k])
                    dve.tensor_tensor(edec[:, :, 4], tot[:, :, 2], tot[:, :, 3], ALU.add)
                    link(dve.tensor_tensor(edec[:, :, 1], tot[:, :, 1], tot[:, :, 2], ALU.add))
                    dve.tensor_tensor(edec[:, :, 2], edec[:, :, 1], tot[:, :, 3], ALU.add).then_inc(e_sum, 1)
                if c == 18:
                    dve.wait_ge(kd_exp, 1)
                    tps.wait(dve, tps.name[("gT", 3)])
                    link(dve.tensor_tensor(kT[:], kT[:], kd[:], ALU.mult))
                    dve.memset(sT[64:P, :, 0:64], 0.0).then_inc(sT_zero, 1)
                    dve.memset(sT[64:P, :, 2 * P:2 * P + 64], 0.0).then_inc(sT_zero, 1)
                if c == 19:
                    dve.wait_ge(e_exp, 1)
                    scaled_q(0)
                gla_side(c)
                if c >= 48 and c % 4 == 3:
                    add_to_h(("glaout", (c - 48) // 4), (c - 48) // 4, last=c)
                if c - 48 in (5, 9, 13):
                    low_x(1, (c - 48) // 4 - 1, COL["mlp_norm"])
                if c:
                    split(c + AHEAD)
            low_x(1, 3, COL["mlp_norm"])
            row_scales(1, 1)
            with dve.Fori(0, 4) as i:
                for c in range(32):
                    if c in (3, 7, 11, 15):
                        n = c // 4
                        blk = accs.name[("up", 0, n)]
                        accs.wait(dve, blk, i, 8)
                        dve.tensor_tensor(nat[:, n % 2], nat[:, n % 2], nat[:, n % 2], ALU.mult).then_inc(a_sq, 1)
                    if c in (4, 8, 12, 16):
                        n = c // 4 - 1
                        low(tps.name[("aT", 0, n)], n, 4 + n + 1, i, 4)
                    if c >= 16 and c % 4 == 3:
                        n = c // 4 - 4
                        add_to_h(("down", 0, n), n, i, 32, C_MLP + c)
                    split(C_MLP + c + AHEAD, i, 32)
            low_x(3, 0, COL["norm_mix"])
            low_x(3, 1, COL["norm_mix"])
            rms(2)
            dve.wait_ge(row_in, 16)
            normed_rows(2, 0, frow, rowdone)
            normed_rows(2, 1, frow, rowdone)

            def taken(g, ins):
                ins.then_inc(tps.sem(g), 1)
                tps.wait(dve, g)

            def mat4(t):
                return t.rearrange("p h m i -> p (h m) i")

            def per_mat(t, hf=None):
                t = t[:] if hf is None else t[:, :, 4 * hf:4 * hf + 4]
                return t.rearrange("p m h -> p h m").unsqueeze(3).to_broadcast([P, t.shape[2], M, P])

            def flat(t):
                return t.rearrange("p k t -> p (k t)")

            def group4(g):
                return tpf(g).rearrange("p (h m i) -> p h m i", h=4, m=M)

            def keys_queries(hf):
                g = tps.name[("qk", hf)]
                dve.wait_ge(tp_done, g + 1)
                dve.tensor_tensor(qkT[:, 4 * hf:4 * hf + 4], group4(g), dec[:, 4 * hf:4 * hf + 4], ALU.mult).then_inc(tps.sem(g), 1)

            def dn_side(c):
                if c == 24:
                    keys_queries(1)
                if c == 0:
                    low_x(3, 2, COL["norm_mix"])
                    low_x(3, 3, COL["norm_mix"])
                    normed_rows(2, 2, frow, rowdone)
                    normed_rows(2, 3, frow, rowdone)
                if c == 1:
                    row_scales(3, 3)
                if c == 2:
                    dve.wait_ge(wab_h, 1)
                    dve.tensor_tensor(wab_lo[:], wab_raw[:], wab_hi[:].bitcast(F32), ALU.subtract).then_inc(wab_l, 1)
                if c == 4:
                    tps.wait(dve, tps.name["ab"])
                    dve.wait_ge(smalls_in, 48)
                    dve.tensor_tensor(u8[:], ab[:, :, 0:8], dtb.unsqueeze(1).to_broadcast([P, M, 8]), ALU.add).then_inc(u_ready, 1)
                if c == 5:
                    dve.wait_ge(u_ln, 1)
                    dve.wait_ge(a_log, 1)
                    link(dve.scalar_tensor_tensor(g8[:], u8[:], 0.0, l8[:], ALU.max, ALU.add))
                    dve.scalar_tensor_tensor(g8[:], g8[:], -1.0, nega[:].unsqueeze(1).to_broadcast([P, M, 8]), ALU.mult, ALU.mult).then_inc(g_ready, 1)
                    dve.wait_ge(b_tanh, 1)
                    link(dve.tensor_scalar(beta[:], beta[:], 0.5, 0.5, ALU.mult, ALU.add))
                    link(dve.tensor_scalar(betah[:], beta[:], 0.5, None, ALU.mult))
                for b in range(6):
                    g = tps.name[("dT", b)]
                    if c == 4 * b + 4:
                        dve.wait_ge(conv0, b + 1)
                        for sh in (1, 2, 3):
                            for k in range(4):
                                w = COL["dn_conv"] + 4 * (4 * b + k) + 3 - sh
                                ins = dve.scalar_tensor_tensor(cv[:, k, sh:], tp[:, g % 2, k, 0:SEQ - sh], col[:, w:w + 1],
                                                               cv[:, k, sh:], ALU.mult, ALU.add)
                            if sh < 3:
                                link(ins)
                        ins.then_inc(tps.sem(g), 1)
                    if c == 4 * b + 5:
                        dve.wait_ge(conv_t, b + 1)
                        dst = cv[:] if b >= 4 else (cqT, ckT)[b // 2][:, 4 * (b % 2):4 * (b % 2) + 4]
                        dve.scalar_tensor_tensor(flat(dst), flat(th[:]), 1.0, flat(cv[:]), ALU.add, ALU.mult).then_inc(conv_out, 1)
                    if c == 4 * b + 7 and b < 4:
                        g = tps.name[("ssq", b)]
                        dst = ssq if b < 2 else ssk
                        dve.wait_ge(tp_done, g + 1)
                        taken(g, dve.tensor_copy(dst[:, :, 4 * (b % 2):4 * (b % 2) + 4], tpf(g)[:, 0:8].rearrange("p (m h) -> p m h", m=M)))
                        if b % 2:
                            dve.tensor_scalar(dst[:], dst[:], 4.0 * EPS, None, ALU.add).then_inc(ss_ready, 1)
                if c == 7:
                    g = tps.name["gc"]
                    dve.wait_ge(tp_done, g + 1)
                    f = tpf(g)
                    dve.tensor_copy(gc[:].rearrange("p m h -> p (m h)"), f[:, 0:16])
                    dve.tensor_copy(gl[:].rearrange("p m h -> p (m h)"), f[:, 16:32])
                    glb_m = glb[:].rearrange("p (m c) h -> p m c h", c=2)
                    dve.tensor_copy(glb_m[:, :, 0], f[:, N:N + 16].rearrange("p (m h) -> p m h", m=M))
                    taken(g, dve.tensor_copy(glb_m[:, :, 1], f[:, 32:48].rearrange("p (m h) -> p m h", m=M)))
                    dve.tensor_tensor(ekd[:], gl[:], gc[:], ALU.subtract).then_inc(ekd_in, 1)
                ident_b = ident.unsqueeze(1).to_broadcast([P, 8, P])

                def diagonal(hf, t, dst):
                    dve.tensor_tensor(dst[:], ident.unsqueeze(1).unsqueeze(1).to_broadcast([P, 4, M, P]), per_mat(t, hf),
                                      ALU.mult).then_inc(dg_ready, 1)

                if c == 9:
                    diagonal(0, gc, diag[0])
                if c in (10, 11):
                    hf = c - 10
                    g = tps.name[("rg", hf)]
                    dve.wait_ge(tp_done, g + 1)
                    if hf == 0:
                        diagonal(1, gc, diag[0])
                    taken(g, dve.tensor_tensor(dec[:, 4 * hf:4 * hf + 4], group4(g), per_mat(gc, hf), ALU.subtract))
                    if hf:
                        dve.tensor_scalar(dec[:], dec[:], 0.0, None, ALU.min).then_inc(diff_ready, 1)
                if c == 13:
                    dve.wait_ge(dec_exp, 1)
                    dve.tensor_tensor(mat4(dec[:]), mat4(dec[:]), tri_c[:].unsqueeze(1).to_broadcast([P, 16, P]), ALU.mult).then_inc(tri_used, 1)
                if c == 20:
                    dve.wait_ge(r_pow, 2)
                    dve.wait_ge(e_gc, 1)
                    dve.tensor_tensor(brk[:], beta[:], rk[:], ALU.mult).then_inc(brk_ready, 1)
                    dve.wait_ge(brk_ready, 1)
                    dve.scalar_tensor_tensor(nber[:], brk[:], -1.0, egc[:], ALU.mult, ALU.mult)
                    dve.tensor_tensor(kds[:], rk[:], ekd[:], ALU.mult)
                    link(dve.tensor_scalar(qsc[:], rq[:], 128 ** -0.5, None, ALU.mult))
                if c == 20:
                    dve.wait_ge(tri_used, 1)
                    link(dve.tensor_tensor(dec[:], dec[:], per_mat(rk), ALU.mult))
                if c == 21:
                    for hf in range(2):
                        g = tps.name[("kk", hf)]
                        dve.wait_ge(tp_done, g + 1)
                        taken(g, dve.tensor_tensor(nT[:, 4 * hf:4 * hf + 4], group4(g), dec[:, 4 * hf:4 * hf + 4], ALU.mult))
                if c == 22:
                    for hf in range(2):
                        g = tps.name[("rb", hf)]
                        dve.wait_ge(tp_done, g + 1)
                        taken(g, dve.tensor_tensor(nT[:, 4 * hf:4 * hf + 4], group4(g), nT[:, 4 * hf:4 * hf + 4], ALU.mult))
                    for hf in range(2):
                        hs = slice(4 * hf, 4 * hf + 4)
                        link(dve.tensor_tensor(mat4(xT[:, hs]), mat4(nT[:, hs]), lvl[:, 0].unsqueeze(1).to_broadcast([P, 8, P]), ALU.mult))
                        dve.tensor_tensor(mat4(xT[:, hs]), ident_b, mat4(xT[:, hs]), ALU.subtract).then_inc(xt0, 1)
                if c == 23 or c == 26:
                    b = 4 if c == 23 else 5
                    g = tps.name[("vN", b)]
                    hs = slice(4 * b - 16, 4 * b - 12)
                    dve.wait_ge(tp_done, g + 1)
                    dve.tensor_tensor(vb[:, :, hs.start * P:hs.stop * P].rearrange("p m (h d) -> p m h d", d=P),
                                      tpf(g).rearrange("p (m h d) -> p m h d", m=M, h=4),
                                      betah[:, :, hs].unsqueeze(3).to_broadcast([P, M, 4, P]), ALU.mult).then_inc(tps.sem(g), 1)
                if c == 23:
                    keys_queries(0)
                for l in range(1, 6):
                    for hf in range(2):
                        hs = slice(4 * hf, 4 * hf + 4)
                        if c == 23 + 2 * l:
                            g = tps.name[("P", l, hf)]
                            dve.wait_ge(tp_done, g + 1)
                            dve.tensor_tensor(mat4(pm[:, hs]), mat4(group4(g)), lvl[:, l].unsqueeze(1).to_broadcast([P, 8, P]),
                                              ALU.mult).then_inc(tps.sem(g), 1)
                        if c == 24 + 2 * l:
                            for name, x_ in ((("D", l, hf), xn), (("DT", l, hf), xT)):
                                if name in tps.name:
                                    g = tps.name[name]
                                    dve.wait_ge(tp_done, g + 1)
                                    dve.tensor_tensor(x_[:, hs], x_[:, hs], group4(g), ALU.subtract).then_inc(tps.sem(g), 1)
                    if c == 23 + 2 * l and l <= 2:
                        hf = l - 1
                        g = tps.name[("kN", hf)]
                        dve.wait_ge(tp_done, g + 1)
                        dve.tensor_tensor(kdec[:, :, hf * N:(hf + 1) * N].rearrange("p m (h d) -> p m h d", d=P),
                                          tpf(g).rearrange("p (m h d) -> p m h d", m=M, h=4),
                                          kds[:, :, 4 * hf:4 * hf + 4].unsqueeze(3).to_broadcast([P, M, 4, P]), ALU.mult).then_inc(tps.sem(g), 1)
                for b in range(2):
                    if c == 27 + 4 * b:
                        blk = accs.name[("z", b)]
                        dve.wait_ge(z_tanh, b + 1)
                        zb_ = zz[:, :, b * N:(b + 1) * N]
                        dve.scalar_tensor_tensor(zb_, nat[:, b], 1.0, acc[:, blk % 2], ALU.add, ALU.mult).then_inc(accs.sem(blk), 1)
                        accs.wait(dve, blk)
                        for m in range(M):
                            zm_ = zz[:, m, b * N:(b + 1) * N].rearrange("p (h d) -> p h d", d=P)
                            ins = dve.scalar_tensor_tensor(zm_, zm_, rhalf[:, 3, m:m + 1], dnorm.unsqueeze(1).to_broadcast([P, 4, P]),
                                                           ALU.mult, ALU.mult)
                        link(ins)

            def copied(name, dst, scale=None):
                g = tps.name[name]
                dve.wait_ge(tp_done, g + 1)
                src = tpf(g)[:, 0:dst.shape[1]]
                ins = dve.tensor_copy(dst, src) if scale is None else dve.tensor_scalar(dst, src, scale, None, ALU.mult)
                ins.then_inc(tps.sem(g), 1)

            def recurrence(c):
                if c == 36:
                    copied("sbqT", flat(sbq[:]))
                if c == 40:
                    copied("sbkT", flat(sbk[:]))
                for cs in range(4):
                    m, part = cs // 2, slice(64 * (cs % 2), 64 * (cs % 2) + 64)
                    vrow = vb[part, m].rearrange("p (h d) -> p h d", d=P)

                    def grp(name, rows_=part):
                        g = tps.name[name]
                        dve.wait_ge(tp_done, g + 1)
                        return g, tpf(g)[rows_].rearrange("p (h d) -> p h d", d=P)

                    if cs and c == 35 + 3 * cs:
                        g, f = grp(("kS", cs))
                        taken(g, dve.tensor_tensor(rv[part], f, nber[part, m].unsqueeze(2).to_broadcast([64, 8, P]), ALU.mult))
                        dve.tensor_tensor(rv[part], rv[part], vrow, ALU.add).then_inc(rv_ready, 1)
                        dve.wait_ge(rv_ready, cs)
                        g, f = grp(("qS", cs))
                        taken(g, dve.tensor_tensor(vrow, f, egc[part, m].unsqueeze(2).to_broadcast([64, 8, P]), ALU.mult))
                    if c == 37 + 3 * cs:
                        g, f = grp(("in", cs))
                        if cs:
                            dve.tensor_tensor(vrow, vrow, f, ALU.add).then_inc(tps.sem(g), 1)
                        else:
                            dve.tensor_copy(vrow, f).then_inc(tps.sem(g), 1)
                        if cs < 3:
                            if cs:
                                link(dve.tensor_tensor(state[:], state[:], glb[:, cs].unsqueeze(2).to_broadcast([P, 8, P]), ALU.mult))
                            g, f = grp(("up", cs), slice(0, P))
                            if cs:
                                dve.tensor_tensor(state[:], state[:], f, ALU.add).then_inc(tps.sem(g), 1)
                            else:
                                dve.tensor_copy(state[:], f).then_inc(tps.sem(g), 1)

            def attention_side(c):
                y16 = vb[:].rearrange("p m (h d) -> p (m h) d", d=P)

                if c == 47:
                    tps.wait(dve, tps.name[("in", 3)])
                    dve.tensor_tensor(y16, y16, qsc[:].rearrange("p m h -> p (m h)").unsqueeze(2).to_broadcast([P, 16, P]), ALU.mult).then_inc(y_scaled, 1)
                    dve.wait_ge(amask_in, 16)
                    for k in range(2):
                        g = tps.name[("sz", k)]
                        dve.wait_ge(tp_done, g + 1)
                        taken(g, dve.scalar_tensor_tensor(zm[:, 2 * k:2 * k + 2], tpf(g).rearrange("p (j n) -> p j n", j=2)[:, :, 0:3 * P],
                                                          128 ** -0.5, amask[:, 0].unsqueeze(1).to_broadcast([P, 2, 3 * P]), ALU.mult, ALU.add))
                    dve.tensor_copy(ms[1][:], mhalf[:, 0:M]).then_inc(zm_ready, 1)
                if c == 48:
                    copied("swqT", flat(swq[:]), 0.125)
                    dve.wait_ge(y_sq, 1)
                    link(dve.tensor_reduce(yss[:].rearrange("p m h -> p (m h)"), ysq[:], AX.X, ALU.add))
                    dve.tensor_scalar(yss[:], yss[:], 1.0 / P, EPS, ALU.mult, ALU.add).then_inc(y_var, 1)
                    dve.wait_ge(sp_ln, 1)
                    dve.scalar_tensor_tensor(sp_[:], zm[:], 0.0, sp_[:], ALU.max, ALU.add).then_inc(sp_ready, 1)
                if c == 49:
                    for k in range(2):
                        g = tps.name[("rev", k)]
                        dve.wait_ge(tp_done, g + 1)
                        dve.tensor_tensor(zm[:, 2 * k:2 * k + 2], zm[:, 2 * k:2 * k + 2],
                                          tpf(g).rearrange("p (j n) -> p j n", j=2)[:, :, 0:3 * P], ALU.subtract).then_inc(tps.sem(g), 1)
                    dve.wait_ge(y_pow, 1)
                    link(dve.tensor_tensor(y16, y16, yrs[:].rearrange("p m h -> p (m h)").unsqueeze(2).to_broadcast([P, 16, P]), ALU.mult))
                    dve.tensor_tensor(vb[:], vb[:], zz[:], ALU.mult).then_inc(y_done, 1)
                if c == 50:
                    copied("swkT", swk[:])
                if c in (51, 52):
                    for k in (2 * (c - 51), 2 * (c - 51) + 1):
                        g = tps.name[("ws", k)]
                        dve.wait_ge(tp_done, g + 1)
                        for j in range(2):
                            hd = 2 * k + j
                            ins = dve.scalar_tensor_tensor(sw[:, hd], amask[:, 1], -(2.0 ** -(hd + 1)), tpf(g)[:, j * N:j * N + 3 * P],
                                                           ALU.mult, ALU.add)
                        taken(g, ins)
                for slot, name, k0, count in ((52, "ysbT", 12, 21), (57, "yswaT", 8, 22), (58, ("ydnT", 0), 0, 23), (59, ("ydnT", 1), 4, 24)):
                    if c == slot:
                        low(tps.name[name], k0 // 4, count)
                if c == 52:
                    dve.tensor_reduce(mx[:, 0], sw[:, :, 0:P], AX.X, ALU.max)
                    link(dve.tensor_reduce(mx[:, 1], sw[:, :, P:3 * P], AX.X, ALU.max))
                    sink_b = sinks.unsqueeze(1).to_broadcast([P, M, 8])
                    link(dve.tensor_tensor(mx[:], mx[:], sink_b, ALU.max))
                    dve.tensor_tensor(es[:], sink_b, mx[:], ALU.subtract)
                    dve.tensor_scalar(nmx[:], mx[:], -1.0, None, ALU.mult).then_inc(sw_max, 1)
                if c == 54:
                    dve.wait_ge(sw_exp, 1)
                    link(dve.tensor_tensor(rs[:], rs[:], es[:], ALU.add))
                    link(dve.reciprocal(rden[:], rs[:]))
                if c == 56:
                    g = tps.name["wo_"]
                    dve.wait_ge(tp_done, g + 1)
                    dve.tensor_tensor(yswa[:].rearrange("p m (h d) -> p (m h) d", d=64), tpf(g).rearrange("p (k d) -> p k d", d=64),
                                      rden[:].rearrange("p m h -> p (m h)").unsqueeze(2).to_broadcast([P, 16, 64]), ALU.mult).then_inc(tps.sem(g), 1)

            for c in range(50):
                dn_side(c)
                recurrence(c)
                attention_side(c)
                split(C_2 + c + AHEAD)

            def merged_low(nb):
                g = tps.name[("mT", nb)]
                dve.wait_ge(m_half, nb + 1)
                dve.scalar_tensor_tensor(flat(m_lo[:, 4 * nb:4 * nb + 4]), tpf(g), 0.5, flat(m_hi[:, 4 * nb:4 * nb + 4]).bitcast(F32),
                                         ALU.mult, ALU.subtract).then_inc(tps.sem(g), 1)

            for nb in range(NB):
                for j in range(16):
                    c = 50 + 16 * nb + j
                    br, first, _ = BRANCH[j]
                    if j in (4, 9, 15):
                        gk = 3 * nb + (4, 9, 15).index(j)
                        gate, blk = accs.name[("gate", nb, br)], accs.name[("br", nb, br)]
                        dve.wait_ge(used, C_2 + c + 1)
                        accs.wait(dve, gate)
                        t = nat[:, gk % 2]
                        dve.scalar_tensor_tensor(t, t, 1.0, acc[:, blk % 2], ALU.add, ALU.mult).then_inc(accs.sem(blk), 1)
                        accs.wait(dve, blk)
                        if br == "swa":
                            if nb >= 2:
                                dve.wait_ge(tp_done, tps.name[("mT", nb - 2)] + 1)
                            dve.tensor_tensor(mg[nb % 2][:], nat[:, 0], nat[:, 1], ALU.add).then_inc(mg_ready, 1)
                        if br == "dn":
                            dve.wait_ge(mg_ready, 2 * nb + 1)
                            dve.tensor_tensor(mg[nb % 2][:], mg[nb % 2][:], t, ALU.add).then_inc(mg_ready, 1)
                    if nb == 0:
                        attention_side(c)
                    elif j == 1:
                        merged_low(nb - 1)
                    split(C_2 + c + AHEAD)
            for c in range(16):
                if c == 1:
                    merged_low(3)
                if c % 4 == 3:
                    add_to_h(("wo", c // 4), c // 4, last=C_WO + c)
                if c in WO_PARTS:
                    j, n = WO_PARTS[c]
                    if j == 4:
                        low_x(4, n, COL["norm_mem"], a_hi, a_lo)
                    else:
                        low_x(5, n, COL["norm_xattn"])
                if c == 12:
                    row_scales(4, 0, 1)
                split(C_WO + c + AHEAD)
            for c in range(12):
                if c == 0:
                    low_x(5, 3, COL["norm_xattn"])
                if c == 1:
                    row_scales(5, 4)
                if c == 4:
                    g = tps.name["xkT"]
                    dve.wait_ge(tp_done, g + 1)
                    dve.tensor_copy(flat(xkT[:]), tpf(g)).then_inc(tps.sem(g), 1)
                if c == 8:
                    g = tps.name["xqT"]
                    dve.wait_ge(tp_done, g + 1)
                    dve.tensor_scalar(flat(xqT[:]), tpf(g), 128 ** -0.5, None, ALU.mult).then_inc(tps.sem(g), 1)
                if c == 9:
                    for m in range(M):
                        g = tps.name[("xs", m)]
                        dve.wait_ge(tp_done, g + 1)
                        link(dve.tensor_reduce(mx[:, m, 0:4], tp[:, g % 2], AX.X, ALU.max))
                        dve.tensor_scalar(nmx[:, m, 0:4], mx[:, m, 0:4], -1.0, None, ALU.mult).then_inc(x_max, 1)
                if c == 10:
                    g = tps.name[("xpT", 0)]
                    dve.wait_ge(tp_done, g + 1)
                    dve.tensor_copy(xpT[:, 0].rearrange("p h b q -> p (h b q)"), tpf(g)).then_inc(tps.sem(g), 1)
                    tps.wait(dve, tps.name[("xs", 1)])
                    link(dve.reciprocal(rden[:, :, 0:4], rs[:, :, 0:4]))
                split(C_X + c + AHEAD)
            g = tps.name["xo_"]
            dve.wait_ge(tp_done, g + 1)
            dve.tensor_tensor(yx[:].rearrange("p m (h d) -> p m h d", d=P), tpf(g).rearrange("p (m h d) -> p m h d", m=M, h=4),
                              rden[:, :, 0:4].unsqueeze(3).to_broadcast([P, M, 4, P]), ALU.mult).then_inc(tps.sem(g), 1)
            low(tps.name["yxT"], 0, 25)
            for c in range(4):
                add_to_h(("xo", c), c, last=C_XO + c)
                if c:
                    low_x(6, c - 1, COL["norm_ffn"])
                split(C_XO + c + AHEAD)
            low_x(6, 3, COL["norm_ffn"])
            row_scales(6, 5)
            dve.memset(ft[:, 0], 0.0).then_inc(f_lo, 1)
            dve.wait_ge(cw_in, 16)
            base = tps.name[("fgT", 0, 0)]
            LINKS = 8
            with dve.Fori(0, 2) as i:
                start = steps[0]
                dve.tensor_copy(cw[:].rearrange("p t s -> p (t s)"), cw_all[:, i]).then_inc(cw_ready, 1)
                for c in range(48):
                    b, q = divmod(c, 4)
                    if q == 0 and 1 <= b <= 8:
                        b -= 1
                        hb, val = divmod(b, 2)
                        g = base + b
                        dst = fv if val else fg
                        if b == 0:
                            dve.wait_ge(cw_ready, at(1, i, 1))
                        dve.wait_ge(conv1, at(b + 1, i, 8))
                        for sh in (1, 2):
                            for k in range(4):
                                t = 16 * val + 4 * hb + k
                                ins = dve.scalar_tensor_tensor(dst[:, k, sh:], tp[:, g % 2, k, 0:SEQ - sh], cw[:, t, 2 - sh:3 - sh],
                                                               dst[:, k, sh:], ALU.mult, ALU.add)
                            if sh == 1:
                                link(ins, i, LINKS)
                        ins.then_inc(tps.sem(g), 1)
                        hcols = slice(4 * hb, 4 * hb + 4)
                        if not val:
                            dve.wait_ge(f_tanh, at(hb + 1, i, 4))
                            dve.scalar_tensor_tensor(flat(fg[:]), flat(ft[:]), 1.0, flat(fg[:]), ALU.add, ALU.mult).then_inc(g_tanh, 1)
                    if q == 1 and b in (2, 4, 6, 8):
                        hb = b // 2 - 1
                        hcols = slice(4 * hb, 4 * hb + 4)
                        dve.wait_ge(g_tanh, at(hb + 1, i, 4))
                        tps.wait(dve, base + b - 1, i, 8)
                        dve.scalar_tensor_tensor(flat(fg[:]), flat(fg[:]), 0.5, flat(fv[:]), ALU.mult, ALU.mult).then_inc(p_ready, 1)
                        dve.wait_ge(f_hi, at(hb + 1, i, 4))
                        dve.tensor_tensor(flat(a_lo[:, hcols]), flat(fg[:]), flat(a_hi[:, hcols]).bitcast(F32), ALU.subtract).then_inc(f_lo, 1)
                    if b >= 8 and q == 3:
                        add_to_h(("fdown", 0, b - 8), b - 8, i, 48, C_FFN + c, 12)
                    split(C_FFN + c + AHEAD, i, 48)
                assert steps[0] - start == LINKS
            steps[0] += LINKS
            dve.wait_ge(row2_in, 16)
            rms(6, passes=2)
            for n in range(NB):
                normed_rows(7, n, frow2, o_fin)


def _stream(parts):
    out = []
    for w, width in parts:
        k, n = w.shape
        kt = k // P
        per = CH // width
        a = w.reshape(kt // per, per, P, n // width, width).transpose(3, 0, 2, 1, 4)
        out.append(a.reshape(-1, P, CH))
    return np.concatenate(out, 0)


def _cols(v):
    return np.asarray(v).reshape(-1, P).T


def _shapes():
    r = np.arange(P)
    same = (r[:, None] // 64 == r[None, :] // 64)
    start = np.broadcast_to(np.arange(SEQ) % 64 != 0, (P, SEQ))
    return np.concatenate([np.eye(P), np.ones((P, P)), start, r[:, None] >= r[None, :], same & (r[:, None] <= r[None, :]),
                           same], 1).astype(np.float32)


def _masks():
    from concourse import mybir
    r = np.arange(P)
    i, j = r[:, None], r[None, :]

    def couples(i, j, s):
        return (i // s == j // s + 1) & (i // (2 * s) == j // (2 * s))

    levels = [couples(j, i, 1)] + [couples(i, j, 2 ** l) for l in range(1, 6)]
    before = np.where(i < j, 0.0, -1e30)
    sb = np.concatenate([before, np.zeros((P, P)), before], 1)
    dist = np.concatenate([np.where(i >= j, i - j, 1e30), np.where(j > i, i + P - j, 1e30), np.where(i >= j, i - j, 1e30)], 1)
    return np.concatenate(levels + [sb, dist], 1).astype(mybir.dt.np(mybir.dt.bfloat16))


def kernel(**inputs):
    import concourse.bacc as bacc
    from concourse import mybir
    from concourse.bass_utils import run_bass_kernel_spmd

    a = {k: np.asarray(v) for k, v in inputs.items()}
    w1 = a["gla_w_in"][0]
    up, down = a["mlp_w_up"][0], a["mlp_w_down"][0]
    parts = [(w1[:, :6144], 512), (a["gla_w_out"][0], 512)]
    for g in range(4):
        parts += [(up[:, 2048 * g:2048 * (g + 1)], 512), (down[2048 * g:2048 * (g + 1)], 512)]
    w2 = a["w_in_2"][0]
    at = np.cumsum([0, 3072, 1024, 8, 8, 512, 256, 1536, 6144])
    qkv, z, aw, bw, swq, swkv, sbqkv, gates = [w2[:, at[k]:at[k + 1]] for k in range(8)]
    swq = swq.reshape(D, 2, 4, 64).transpose(0, 2, 1, 3).reshape(D, 512)
    parts += [(qkv, 512), (z, 512), (sbqkv, 512), (swq, 512), (swkv, 256)]
    brs = {"dn": (0, a["w_br_dn_2"][0]), "swa": (1, a["w_br_swa_2"][0]), "sb": (2, a["w_br_sb_2"][0])}
    for nb in range(4):
        for br in ("sb", "swa", "dn"):
            k, wb = brs[br]
            c = slice(512 * nb, 512 * (nb + 1))
            parts += [(gates[:, D * k:D * (k + 1)][:, c], 512), (wb[:, c], 512)]
    xkv = a["w_xkv_2"][0]
    parts += [(a["w_o_2"][0], 512), (xkv[:, :512], 512), (a["w_xq_2"][0], 512), (xkv[:, 512:], 512), (a["w_xo_2"][0], 512)]
    up2, down2 = a["w_up_2"][0], a["w_down_2"][0]
    for g in range(2):
        for b in range(4):
            c = 2048 * g + 512 * b
            parts += [(up2[:, c:c + 512], 512), (up2[:, 4096 + c:4096 + c + 512], 512)]
        parts += [(down2[2048 * g:2048 * (g + 1)], 512)]
    stream = _stream(parts)
    dn_conv = a["dn_conv_2"][0].reshape(4, 24, P).transpose(2, 1, 0).reshape(P, 96)
    ffn_conv = a["ffn_conv_2"][0].reshape(3, 2, 2, 16, P).transpose(4, 2, 1, 3, 0).reshape(P, 192)
    cols = np.concatenate([_cols(a[k].reshape(-1)) for k in ("gla_norm", "mlp_norm", "gla_b_gate", "norm_mix_2", "norm_xattn_2",
                                                            "norm_mem_2", "norm_ffn_2")]
                          + [dn_conv, _cols(a["final_norm"]), ffn_conv], 1)
    rows = np.concatenate([a[k].reshape(-1) for k in ("gla_o_norm", "final_norm", "norm_final_2", "dn_a_log_2", "dn_dt_bias_2",
                                                      "swa_sinks_2", "dn_norm_2")])
    rows = np.broadcast_to(rows, (P, rows.size))
    wglow = w1[:, 6144:].reshape(16, P, 16).transpose(1, 0, 2)
    wab = np.concatenate([aw, bw], 1).reshape(16, P, 16).transpose(1, 0, 2)
    data = {"x": a["x"][0], "mem": a["mem_2"][0], "stream": stream, "cols": cols, "rows": rows, "wglow": wglow, "wab": wab,
            "wgu": a["gla_w_gate_up"][0], "shapes": _shapes(), "masks": _masks()}
    data = {k: np.ascontiguousarray(v) for k, v in data.items()}
    nc = bacc.Bacc("TRN2", target_bir_lowering=False, num_devices=1)
    arrays, args = {}, []
    for name, v in data.items():
        arrays["in_" + name] = v
        args.append(nc.dram_tensor("in_" + name, v.shape, mybir.dt.from_np(v.dtype), kind="ExternalInput").ap())
    out = nc.dram_tensor("out_y", (SEQ, D), mybir.dt.float32, kind="ExternalOutput").ap()
    build(nc, *args, out)
    r = run_bass_kernel_spmd(nc, [arrays], core_ids=[0])
    return r.results[0]["out_y"].reshape(1, SEQ, D)
```
